# Optimizing a Trainium2 kernel written in Bass

```python
import math
import jax, jax.numpy as jnp
from jax import lax
import numpy as np

D_MODEL = 1024
BATCH = 1
SEQ = 1024
DEPTH = 1
DEC_BATCH = 1
DEC_SEQ = 32
PAST_LEN = 256

CHUNK = 64
EPS = 1e-6
DN_HEADS = 8
DN_DK = 128
DN_DV = 128
DN_QK = DN_HEADS * DN_DK
DN_V = DN_HEADS * DN_DV
DN_CONV_CH = 2 * DN_QK + DN_V
CONV_W = 4
MLA_HEADS = 8
QK_NOPE = 128
QK_ROPE = 64
QK_HEAD = QK_NOPE + QK_ROPE
V_HEAD = 128
KV_RANK = 512
MLA_Q = MLA_HEADS * QK_HEAD
MLA_V = MLA_HEADS * V_HEAD
ROPE_THETA = 10000.0
Q_BLOCK = 128
IN_WIDTHS = (DN_CONV_CH, DN_V, DN_HEADS, DN_HEADS, MLA_Q, KV_RANK, QK_ROPE, MLA_V, D_MODEL, D_MODEL)
IN_WIDTH = DN_CONV_CH + DN_V + 2 * DN_HEADS + MLA_Q + KV_RANK + QK_ROPE + MLA_V + 2 * D_MODEL

kernel_name = 'hybrid_gdn_mla_stream_step'

def _rms(x, gain):
    xf = x.astype(jnp.float32)
    y = xf * lax.rsqrt(jnp.mean(xf * xf, axis=-1, keepdims=True) + EPS)
    return (y * gain.astype(jnp.float32)).astype(x.dtype)

def _l2norm(x):
    return x * lax.rsqrt(jnp.sum(x * x, axis=-1, keepdims=True) + EPS)

def _rope(x, pos):
    half = QK_ROPE // 2
    inv = ROPE_THETA ** (-jnp.arange(half, dtype=jnp.float32) / half)
    ang = pos.astype(jnp.float32)[:, None] * inv
    ang = ang.reshape(ang.shape[0], *([1] * (x.ndim - 3)), half)
    cos, sin = jnp.cos(ang), jnp.sin(ang)
    xf = x.astype(jnp.float32)
    x1, x2 = xf[..., :half], xf[..., half:]
    return jnp.concatenate([x1 * cos - x2 * sin, x2 * cos + x1 * sin], axis=-1).astype(x.dtype)

def _split_in(proj):
    idx, s = [], 0
    for w in IN_WIDTHS[:-1]:
        s += w
        idx.append(s)
    return jnp.split(proj, idx, axis=-1)

def _short_conv(u, buf, w_conv):
    full = jnp.concatenate([buf, u], axis=1)
    T = u.shape[1]
    out = full[:, 0:T] * w_conv[0]
    for i in range(1, CONV_W):
        out = out + full[:, i:i + T] * w_conv[i]
    return jax.nn.silu(out), full[:, -(CONV_W - 1):]

def _gated_delta(q, k, v, g, beta, s0):
    B, T, H, _ = q.shape
    C = min(CHUNK, T)
    N = T // C
    qc, kc, vc = [jnp.moveaxis(a.reshape(B, N, C, H, a.shape[-1]), 3, 2) for a in (q, k, v)]
    gc, bc = [jnp.moveaxis(a.reshape(B, N, C, H), 3, 2) for a in (g, beta)]
    gcum = jnp.cumsum(gc, axis=-1)
    tri_incl = jnp.tril(jnp.ones((C, C), bool))
    tri_strict = jnp.tril(jnp.ones((C, C), bool), -1)
    decay = jnp.exp(jnp.where(tri_incl, gcum[..., :, None] - gcum[..., None, :], -jnp.inf))
    kb = kc * bc[..., None]
    L = jnp.where(tri_strict, jnp.einsum('bnhid,bnhjd->bnhij', kb, kc) * decay, 0.0)
    eye = jnp.eye(C, dtype=q.dtype)
    tinv = lax.linalg.triangular_solve(eye + L, jnp.broadcast_to(eye, L.shape), left_side=True, lower=True)
    eg = jnp.exp(gcum)
    w = tinv @ (kb * eg[..., None])
    u = tinv @ (vc * bc[..., None])
    attn = jnp.einsum('bnhid,bnhjd->bnhij', qc, kc) * decay
    qg = qc * eg[..., None]
    kd = kc * jnp.exp(gcum[..., -1:] - gcum)[..., None]
    glast = jnp.exp(gcum[..., -1])

    def step(S, xs):
        w_, u_, qg_, attn_, kd_, gl_ = xs
        vnew = u_ - w_ @ S
        o = qg_ @ S + attn_ @ vnew
        S = S * gl_[..., None, None] + jnp.swapaxes(kd_, -1, -2) @ vnew
        return S, o

    xs = tuple(jnp.moveaxis(a, 1, 0) for a in (w, u, qg, attn, kd, glast))
    S, o = lax.scan(step, s0, xs)
    o = jnp.moveaxis(jnp.moveaxis(o, 0, 1), 2, 3).reshape(B, T, H, v.shape[-1])
    return o, S

def _deltanet(qkv_raw, beta_raw, alpha_raw, conv_buf, s0, p):
    qkv, conv_new = _short_conv(qkv_raw, conv_buf, p['w_conv'])
    B, T, _ = qkv.shape
    f32 = jnp.float32
    q, k, v = jnp.split(qkv.astype(f32), [DN_QK, 2 * DN_QK], axis=-1)
    q = _l2norm(q.reshape(B, T, DN_HEADS, DN_DK)) * (DN_DK ** -0.5)
    k = _l2norm(k.reshape(B, T, DN_HEADS, DN_DK))
    v = v.reshape(B, T, DN_HEADS, DN_DV)
    beta = jax.nn.sigmoid(beta_raw.astype(f32))
    g = -jnp.exp(p['a_log'].astype(f32)) * jax.nn.softplus(alpha_raw.astype(f32) + p['dt_bias'].astype(f32))
    o, S = _gated_delta(q, k, v, g, beta, s0.astype(f32))
    o = _rms(o, p['dn_out_norm'])
    return o.reshape(B, T, DN_V).astype(qkv_raw.dtype), conv_new, S.astype(qkv_raw.dtype)

def _attend(qn, qr, qpos, kn, kr, v, kpos):
    s = jnp.einsum('bqhd,bkhd->bhqk', qn, kn) + jnp.einsum('bqhd,bkd->bhqk', qr, kr)
    s = s.astype(jnp.float32) * (QK_HEAD ** -0.5)
    mask = (kpos[None, :] // CHUNK) <= (qpos[:, None] // CHUNK)
    s = jnp.where(mask, s, -jnp.inf)
    pr = jax.nn.softmax(s, axis=-1).astype(v.dtype)
    return jnp.einsum('bhqk,bkhd->bqhd', pr, v)

def _mla(q_raw, ckv_raw, kr_raw, pos, past_ckv, past_kr, p):
    B, T, _ = q_raw.shape
    q = q_raw.reshape(B, T, MLA_HEADS, QK_HEAD)
    q_nope = _rms(q[..., :QK_NOPE], p['q_nope_norm'])
    q_rope = _rope(_rms(q[..., QK_NOPE:], p['q_rope_norm']), pos)
    ckv_new = _rms(ckv_raw, p['kv_norm'])
    kr_new = _rope(_rms(kr_raw, p['k_rope_norm']), pos)
    if past_ckv is None:
        ckv_all, kr_all, kpos = ckv_new, kr_new, pos
    else:
        ckv_all = jnp.concatenate([past_ckv, ckv_new], axis=1)
        kr_all = jnp.concatenate([past_kr, kr_new], axis=1)
        kpos = jnp.concatenate([jnp.arange(past_ckv.shape[1]), pos])
    Tk = ckv_all.shape[1]
    k_nope = _rms((ckv_all @ p['w_uk']).reshape(B, Tk, MLA_HEADS, QK_NOPE), p['k_nope_norm'])
    v = (ckv_all @ p['w_uv']).reshape(B, Tk, MLA_HEADS, V_HEAD)
    qb = Q_BLOCK if T % Q_BLOCK == 0 else T
    nb = T // qb
    qn_b = jnp.moveaxis(q_nope.reshape(B, nb, qb, MLA_HEADS, QK_NOPE), 1, 0)
    qr_b = jnp.moveaxis(q_rope.reshape(B, nb, qb, MLA_HEADS, QK_ROPE), 1, 0)
    qp_b = pos.reshape(nb, qb)
    o = lax.map(lambda a: _attend(a[0], a[1], a[2], k_nope, kr_all, v, kpos), (qn_b, qr_b, qp_b))
    o = jnp.moveaxis(o, 0, 1).reshape(B, T, MLA_V)
    return o, ckv_new, kr_new

def _layer(x, c, pos, conv_buf, s0, past_ckv, past_kr, p):
    B = x.shape[0]
    mod = c @ p['w_ada'] + p['b_ada']
    shift, scale, gate = jnp.split(mod, 3, axis=-1)
    h = _rms(x, p['norm_gain']) * (1 + scale[:, None, :]) + shift[:, None, :]
    (qkv_raw, z_a, beta_raw, alpha_raw, q_raw, ckv_raw, kr_raw, z_b, g_a, g_b) = _split_in(h @ p['w_in'])
    if conv_buf is None:
        conv_buf = jnp.zeros((B, CONV_W - 1, DN_CONV_CH), x.dtype)
    if s0 is None:
        s0 = jnp.zeros((B, DN_HEADS, DN_DK, DN_DV), jnp.float32)
    o_a, conv_new, s_new = _deltanet(qkv_raw, beta_raw, alpha_raw, conv_buf, s0, p)
    o_b, ckv_new, kr_new = _mla(q_raw, ckv_raw, kr_raw, pos, past_ckv, past_kr, p)
    u_a = o_a * jax.nn.silu(z_a)
    u_b = o_b * jax.nn.silu(z_b)
    merged = jax.nn.sigmoid(g_a) * (u_a @ p['w_o_dn']) + jax.nn.sigmoid(g_b) * (u_b @ p['w_o_mla'])
    y = x + gate[:, None, :] * (merged @ p['w_out'])
    return y, conv_new, s_new, ckv_new, kr_new

def setup_inputs(seed: int = 0) -> dict:
    key = jax.random.key(seed)
    ks = jax.random.split(key, 32)
    f32 = jnp.float32

    def nrm(k, shape, scale):
        return jax.random.normal(k, shape, f32) * scale

    def gain(k, n):
        return 1.0 + 0.05 * jax.random.normal(k, (DEPTH, n), f32)

    dt = jnp.exp(jax.random.uniform(ks[12], (DEPTH, DN_HEADS), f32, math.log(1e-3), math.log(1e-1)))
    return {
        'x_prompt': nrm(ks[0], (BATCH, SEQ, D_MODEL), 1.0),
        'x_sample': nrm(ks[1], (DEC_BATCH, DEC_SEQ, D_MODEL), 1.0),
        'c_prompt': nrm(ks[2], (BATCH, D_MODEL), 1.0),
        'c_sample': nrm(ks[3], (DEC_BATCH, D_MODEL), 1.0),
        'cache_ckv': nrm(ks[4], (DEPTH, DEC_BATCH, PAST_LEN, KV_RANK), 1.0),
        'cache_krope': nrm(ks[5], (DEPTH, DEC_BATCH, PAST_LEN, QK_ROPE), 1.0),
        'state_delta': nrm(ks[6], (DEPTH, DEC_BATCH, DN_HEADS, DN_DK, DN_DV), 0.1),
        'state_conv': nrm(ks[7], (DEPTH, DEC_BATCH, CONV_W - 1, DN_CONV_CH), 1.0),
        'norm_gain': gain(ks[8], D_MODEL),
        'w_ada': nrm(ks[9], (DEPTH, D_MODEL, 3 * D_MODEL), 0.5 * D_MODEL ** -0.5),
        'b_ada': nrm(ks[10], (DEPTH, 3 * D_MODEL), 0.01),
        'w_in': nrm(ks[11], (DEPTH, D_MODEL, IN_WIDTH), D_MODEL ** -0.5),
        'w_conv': nrm(ks[13], (DEPTH, CONV_W, DN_CONV_CH), CONV_W ** -0.5),
        'a_log': jnp.log(jax.random.uniform(ks[14], (DEPTH, DN_HEADS), f32, 1.0, 16.0)),
        'dt_bias': dt + jnp.log(-jnp.expm1(-dt)),
        'dn_out_norm': gain(ks[15], DN_DV),
        'q_nope_norm': gain(ks[16], QK_NOPE),
        'q_rope_norm': gain(ks[17], QK_ROPE),
        'k_nope_norm': gain(ks[18], QK_NOPE),
        'k_rope_norm': gain(ks[19], QK_ROPE),
        'kv_norm': gain(ks[20], KV_RANK),
        'w_uk': nrm(ks[21], (DEPTH, KV_RANK, MLA_HEADS * QK_NOPE), KV_RANK ** -0.5),
        'w_uv': nrm(ks[22], (DEPTH, KV_RANK, MLA_V), KV_RANK ** -0.5),
        'w_o_dn': nrm(ks[23], (DEPTH, DN_V, D_MODEL), DN_V ** -0.5),
        'w_o_mla': nrm(ks[24], (DEPTH, MLA_V, D_MODEL), MLA_V ** -0.5),
        'w_out': nrm(ks[25], (DEPTH, D_MODEL, D_MODEL), D_MODEL ** -0.5),
    }

def reference(x_prompt, x_sample, c_prompt, c_sample, cache_ckv, cache_krope, state_delta, state_conv,
              norm_gain, w_ada, b_ada, w_in, w_conv, a_log, dt_bias, dn_out_norm,
              q_nope_norm, q_rope_norm, k_nope_norm, k_rope_norm, kv_norm,
              w_uk, w_uv, w_o_dn, w_o_mla, w_out):
    pos_p = jnp.arange(x_prompt.shape[1])
    pos_s = cache_ckv.shape[2] + jnp.arange(x_sample.shape[1])
    yp, ys = x_prompt, x_sample
    ckv_p, kr_p, sd_p, cv_p = [], [], [], []
    ckv_s, kr_s, sd_s, cv_s = [], [], [], []
    for l in range(DEPTH):
        p = dict(norm_gain=norm_gain[l], w_ada=w_ada[l], b_ada=b_ada[l], w_in=w_in[l], w_conv=w_conv[l],
                 a_log=a_log[l], dt_bias=dt_bias[l], dn_out_norm=dn_out_norm[l],
                 q_nope_norm=q_nope_norm[l], q_rope_norm=q_rope_norm[l], k_nope_norm=k_nope_norm[l],
                 k_rope_norm=k_rope_norm[l], kv_norm=kv_norm[l], w_uk=w_uk[l], w_uv=w_uv[l],
                 w_o_dn=w_o_dn[l], w_o_mla=w_o_mla[l], w_out=w_out[l])
        yp, cvp, sdp, kvp, krp = _layer(yp, c_prompt, pos_p, None, None, None, None, p)
        ys, cvs, sds, kvs, krs = _layer(ys, c_sample, pos_s, state_conv[l], state_delta[l],
                                        cache_ckv[l], cache_krope[l], p)
        ckv_p.append(kvp); kr_p.append(krp); sd_p.append(sdp); cv_p.append(cvp)
        ckv_s.append(kvs); kr_s.append(krs); sd_s.append(sds); cv_s.append(cvs)
    new_ckv_p, new_kr_p = jnp.stack(ckv_p), jnp.stack(kr_p)
    new_sd_p, new_cv_p = jnp.stack(sd_p), jnp.stack(cv_p)
    new_ckv_s, new_kr_s = jnp.stack(ckv_s), jnp.stack(kr_s)
    new_sd_s, new_cv_s = jnp.stack(sd_s), jnp.stack(cv_s)
    return (yp, ys, new_ckv_p, new_kr_p, new_sd_p, new_cv_p, new_ckv_s, new_kr_s, new_sd_s, new_cv_s)


_drawn_inputs = setup_inputs


def setup_inputs(seed=0):
    import zlib

    import numpy as np

    out = dict(_drawn_inputs(seed))
    spreads = {}
    factors = {'cache_ckv': 3.063,
     'cache_krope': 5.933,
     'b_ada': 3.091,
     'dn_out_norm': 5.519,
     'q_nope_norm': 8.0,
     'q_rope_norm': 8.0,
     'k_nope_norm': 8.0,
     'w_uk': 3.794}
    for name, (base, spread) in spreads.items():
        noise = np.random.default_rng([zlib.crc32(name.encode()), seed]).standard_normal(out[name].shape)
        drawn = base * np.exp(spread * noise) if base else spread * noise
        out[name] = __import__('jax').numpy.asarray(drawn.astype(out[name].dtype))
    for name, factor in factors.items():
        out[name] = (out[name] * factor).astype(out[name].dtype)
    return out
```

```python
from contextlib import ExitStack

import numpy as np

import concourse.bass as bass
import concourse.mybir as mybir

F32 = mybir.dt.float32
F32R = mybir.dt.float32r
I32 = mybir.dt.int32
ACT = mybir.ActivationFunctionType
ALU = mybir.AluOpType
AX = mybir.AxisListType

P = 128
D = 1024
KD = D // P
SEQ, DEC, PAST = 1024, 32, 256
CHUNK = 64
H = 8
HD = 128
ROPE = 64
KV = 512
KR = KV // P
QH = HD + ROPE
CONV = 4
EPS = 1e-6
NT = SEQ // P
TOK = SEQ + DEC
TPAD = SEQ + P
NB = 3
TB = TOK // NB
CONV_CH = 3 * H * HD
NCV = CONV_CH // P

COL_BA = CONV_CH + H * HD
COL_Q = COL_BA + 2 * H
COL_KR = COL_Q + H * QH + KV
COL_ZB = COL_KR + ROPE
C_QKV, C_ZA, C_Q, C_CKV, C_ZB, C_GA, C_GB, C_MISC = 0, 24, 32, 44, 48, 56, 64, 72
NCHUNK = 73
BA = 2 * H
MISC = BA + ROPE

LEVELS = [1, 2, 4, 8, 16, 32, 64]
K_ID, K_ONE, K_INC, K_STR, K_LEV = 0, P, 2 * P, 3 * P, 4 * P
NCST = K_LEV + len(LEVELS) * P
A_CONV, A_GAIN, A_C = 0, 96, 104
B_STATE, B_ADA, B_DN, B_QN, B_KN = 0, 72, 96, 97, 98


def shape_constants():
    i, j = np.indices((P, P))
    masks = [i == j, np.ones((P, P)), i <= j, i < j]
    masks += [(i // (2 * s) == j // (2 * s)) & (i % (2 * s) >= s) & (j % (2 * s) < s) for s in LEVELS]
    return np.concatenate([m.astype(np.float32) for m in masks], axis=1)


def rotary_tables():
    half = ROPE // 2
    inv = np.float32(10000.0) ** (-np.arange(half, dtype=np.float32) / np.float32(half))
    pos = np.concatenate([np.arange(SEQ), PAST + np.arange(P)]).astype(np.float32)
    ang = pos[:, None] * inv.astype(np.float32)
    return np.concatenate([np.cos(ang), np.sin(ang)], axis=1).astype(np.float32)


def rsqrt(dve, out, tmp, x):
    dve.tensor_scalar(tmp.bitcast(I32), x.bitcast(I32), 1, None, ALU.arith_shift_right)
    dve.drain()
    dve.tensor_scalar(out.bitcast(I32), tmp.bitcast(I32), -1.0, float(0x5F3759DF), ALU.mult, ALU.add)
    dve.drain()
    for _ in range(3):
        dve.tensor_tensor(tmp, out, out, ALU.mult)
        dve.drain()
        dve.scalar_tensor_tensor(tmp, tmp, -0.5, x, ALU.mult, ALU.mult)
        dve.drain()
        dve.scalar_tensor_tensor(out, tmp, 1.5, out, ALU.add, ALU.mult)
        dve.drain()


def build(nc, a, o, scr, ctx):
    def sb(stack, name, shape, dt=F32):
        return stack.enter_context(nc.sbuf_tensor(name, shape, dt))

    def sem(name):
        return ctx.enter_context(nc.semaphore(name))

    PS = ctx.enter_context(nc.psum_tensor("PS", [P, 8, 512], F32))
    cst = sb(ctx, "cst", [P, NCST])
    ident = cst[:, K_ID:K_ID + P]
    ones = cst[:, K_ONE:K_ONE + P]
    colA = sb(ctx, "colA", [P, 120])
    colB = sb(ctx, "colB", [P, 99])
    mod = sb(ctx, "mod", [P, 24, 2])
    ba = sb(ctx, "ba", [P, NT + 1, BA])

    p1 = ExitStack()
    HH = sb(p1, "HH", [P, KD, TOK], F32R)
    HL = sb(p1, "HL", [P, KD, TOK], F32R)
    Wraw = sb(p1, "Wraw", [P, 4, KD, 256])
    WH = sb(p1, "WH", [P, 2, KD, 256], F32R)
    WL = sb(p1, "WL", [P, 2, KD, 256], F32R)
    R = sb(p1, "R", [P, 9, D])
    rows = sb(p1, "rows", [P, 2, P])
    hf = sb(p1, "hf", [P, 2, 512])
    G = sb(p1, "G", [P, KD, 2])
    xst = sb(p1, "xst", [P, 3, 9])
    Rf = R[:, :, :].rearrange("p a b -> p (a b)")
    XW = 3 + SEQ + 3 + DEC
    Xr = Rf[:, 0:2 * XW].rearrange("p (s n) -> p s n", s=2)
    cvo = 2 * XW
    cv = Rf[:, cvo:cvo + XW - 3]
    sto = cvo + XW - 3
    stage = Rf[:, sto:sto + 2 * TPAD].rearrange("p (s n) -> p s n", s=2)
    wco = sto + 2 * TPAD
    wcv = Rf[:, wco:wco + 8].rearrange("p (s n) -> p s n", s=2)
    edo = wco + 8
    edge = Rf[:, edo:edo + 144]
    edT = Rf[:, edo + 144:edo + 144 + 2 * P].rearrange("p (s n) -> p s n", s=2)
    assert edo + 144 + 2 * P <= 9 * D
    p1.close()

    s_cst = sem("constants_loaded")
    s_rows = sem("vector_rows_loaded")
    s_cols = sem("vectors_transposed")
    s_colc = sem("vector_columns_ready")
    s_x = [sem(f"x_loaded_{i}") for i in range(3)]
    s_ada = [sem(f"w_ada_loaded_{i}") for i in range(4)]
    s_adam = sem("w_ada_chunk_used")
    s_mod = sem("modulation_ready")
    s_xst = sem("x_statistics_cleared")
    s_xss = sem("x_squares_summed")
    s_xn = sem("x_normalised")
    s_xT = sem("x_transposed")
    s_hf = sem("h_float_ready")
    s_hh = sem("h_hi_ready")
    s_hl = sem("h_lo_ready")
    s_raw = [sem(f"w_loaded_{i}") for i in range(2)]
    s_misc = sem("w_beta_alpha_loaded")
    s_whi = sem("w_hi_ready")
    s_wlo = sem("w_lo_ready")
    s_chunk = sem("chunk_in_psum")
    s_evac = sem("chunk_evacuated")
    s_pad = sem("conv_edges_ready")
    s_edge = sem("edges_kept")
    s_conv = sem("chunk_convolved")
    s_stage = sem("chunk_staged")
    s_store = [sem(f"chunk_stored_{i}") for i in range(2)]
    s_edT = sem("edges_transposed")
    s_edc = sem("edge_rows_ready")
    s_out = sem("outputs_stored")

    NG = 2 * KD + KD

    def x_group(n):
        g, k = divmod(n, KD)
        return g, k, (512 if g < 2 else DEC)

    SEGMENTS = [(NCV // 4, 0, "conv"), (2, CONV_CH, "silu"), (4, COL_Q, "copy"), (2, COL_ZB, "silu"),
                (4, COL_ZB + D, "sigmoid")]

    NKT = NT + PAST // P + 1
    KEYS = NKT * P
    SCALE = float(QH) ** -0.5
    p2 = ExitStack()
    kT = sb(p2, "kT", [P, H, KEYS])
    V = sb(p2, "V", [P, NKT, H * HD])
    krT = sb(p2, "krT", [P, KEYS])
    rotq = sb(p2, "rotq", [P, NT + 1, 2, ROPE])
    rotk = sb(p2, "rotk", [P, NT + 1, 2, ROPE])
    gq = sb(p2, "gq", [P, 2, ROPE])
    p2a = ExitStack()
    Uraw = sb(p2a, "Uraw", [P, 2, KR, 256])
    UH = sb(p2a, "UH", [P, 2, KR, H * HD], F32R)
    UL = sb(p2a, "UL", [P, 2, KR, H * HD], F32R)
    kvg = sb(p2a, "kvg", [P, KV])
    latT = sb(p2a, "latT", [P, KR + 1, P])
    lat = sb(p2a, "lat", [P, KV])
    kr2 = sb(p2a, "kr2", [P, 2, ROPE])
    LH = sb(p2a, "LH", [P, 2, KR, P], F32R)
    LL = sb(p2a, "LL", [P, 2, KR, P], F32R)
    ksq = sb(p2a, "ksq", [P, H * HD])
    kn = sb(p2a, "kn", [P, H * HD])
    rot = kn[:, 0:(NT + 1) * ROPE].rearrange("p (t n) -> p t n", n=ROPE)
    lst = sb(p2a, "lst", [P, 3, H + 2])
    lrt = sb(p2a, "lrt", [P, 2, ROPE])
    p2a.close()
    p2b = ExitStack()
    qT = sb(p2b, "qT", [P, 2, H, P])
    qrT = sb(p2b, "qrT", [P, 2, H // 2, P])
    qraw = sb(p2b, "qraw", [P, 12, P])
    qtok = sb(p2b, "qtok", [P, H, QH])
    qsq = sb(p2b, "qsq", [P, H, QH])
    qrr = sb(p2b, "qrr", [P, H, ROPE])
    qrx = sb(p2b, "qrx", [P, 2, H, ROPE])
    qst = sb(p2b, "qst", [P, 3, 2, H])
    zb = sb(p2b, "zb", [P, 2, 4, P])
    pr = sb(p2b, "pr", [P, 2, D])
    pT = sb(p2b, "pT", [P, 2, NT, P])
    on = sb(p2b, "on", [P, 4, P])
    ub = sb(p2b, "ub", [P, 2, 4, P])
    amx = sb(p2b, "amx", [P, 2, 2])
    ars = sb(p2b, "ars", [P, 2, 4])
    ari = sb(p2b, "ari", [P, 4])
    p2b.close()
    p2.close()

    s_pass = sem("engines_through_a_pass")
    s_tab = sem("mla_vectors_loaded")
    s_rot = sem("rotary_tables_ready")
    s_u = [sem(f"w_u_loaded_{i}") for i in range(2)]
    s_uh = sem("w_u_hi_ready")
    s_ul = sem("w_u_lo_ready")
    s_lraw = sem("latent_raw_loaded")
    s_lca = sem("cached_latent_loaded")
    s_la = sem("latent_token_major")
    s_lsq = sem("latent_squares_summed")
    s_lat = sem("latent_ready")
    s_lout = sem("latent_stored")
    s_lb = sem("latent_transposed")
    s_lh = sem("latent_hi_ready")
    s_krT = sem("rotary_key_ready")
    s_ll = sem("latent_lo_ready")
    s_kp = sem("keys_in_psum")
    s_vp = sem("values_in_psum")
    s_ksq = sem("key_squares_ready")
    s_kn = sem("keys_normalised")
    s_vv = sem("values_ready")
    s_kt = sem("keys_transposed")
    s_kT = sem("keys_ready")
    s_qraw = sem("q_raw_loaded")
    s_qc = sem("q_tokens_copied")
    s_qsq = sem("q_squared")
    s_qr = sem("q_norms_ready")
    s_qn = sem("q_normalised")
    s_qrr = sem("q_rotated")
    s_qe = sem("q_ready")
    s_sc = sem("scores_in_psum")
    s_mx = sem("score_maximum_ready")
    s_ex = sem("probabilities_ready")
    s_pt = sem("probabilities_transposed")
    s_pa = sem("probabilities_first_bank_copied")
    s_pd = sem("probabilities_second_bank_copied")
    s_pv = sem("attended_in_psum")
    s_on = sem("attended_normalised")
    s_t7 = sem("small_transposes_made")
    s_r7 = sem("small_transposes_read")
    s_zb = [sem(f"zb_loaded_{i}") for i in range(2)]
    s_us = [sem(f"u_b_stored_{i}") for i in range(2)]

    def meet(eng, n):
        eng.drain().then_inc(s_pass, 1)
        eng.wait_ge(s_pass, 5 * n)

    def sp_latents(sp):
        sp_lraw(sp, 0, 0)
        sp.dma_start(rot[:, :, :], a["rotary_tables"].rearrange("(t p) n -> p t n", p=P)).then_inc(s_tab, 16)
        sp.dma_start(kvg[:, :], a["kv_norm"].to_broadcast([P, KV])).then_inc(s_tab, 16)
        sp.dma_start(gq[:, 0], a["q_rope_norm"].to_broadcast([P, ROPE])).then_inc(s_tab, 16)
        sp.dma_start(gq[:, 1], a["k_rope_norm"].to_broadcast([P, ROPE])).then_inc(s_tab, 16)
        for i in range(8):
            w = a["w_uv"] if i < 4 else a["w_uk"]
            if i == 2:
                sp.wait_ge(s_la, 1)
                sp_lraw(sp, 1, 1)
                sp_lout(sp, 0, P, o["new_ckv_prompt"][0, 0, 0:P], o["new_krope_prompt"][0, 0, 0:P])
            if i >= 2:
                sp.wait_ge(s_ul, i - 1)
            sp.dma_start(Uraw[:, i % 2], w[0, :, 256 * (i % 4):256 * (i % 4) + 256].rearrange("(k p) n -> p k n", p=P)).then_inc(s_u[i % 2], 16)
        with sp.Fori(1, NT) as t:
            sp.wait_ge(s_la, t + 1)
            sp_lraw(sp, t + 1, t + 1)
            sp_lout(sp, t, P, o["new_ckv_prompt"][0, 0, bass.ds(t * P, P)], o["new_krope_prompt"][0, 0, bass.ds(t * P, P)])
        for i in range(PAST // P):
            sp.wait_ge(s_lb, NT + i)
            sp.wait_ge(s_lout, 32 * NT)
            sp.dma_start(lat[:, :], a["cache_ckv"][0, 0, i * P:(i + 1) * P]).then_inc(s_lca, 16)
            for d in range(2):
                sp.dma_start(kr2[:, d], a["cache_krope"][0, 0, i * P:(i + 1) * P]).then_inc(s_lca, 16)
        sp_lout(sp, NT, DEC, o["new_ckv_sample"][0, 0], o["new_krope_sample"][0, 0])
        sp.wait_ge(s_lout, 32 * (NT + 1))

    def sp_lraw(sp, t, tile):
        sp.dma_start(latT[:, 0:KR], scr["proj"][C_CKV:C_CKV + KR, :, bass.ds(tile * P, P)].rearrange("c p n -> p c n")).then_inc(s_lraw, 16)
        sp.dma_start(latT[0:MISC, KR], scr["proj"][C_MISC, 0:MISC, bass.ds(tile * P, P)]).then_inc(s_lraw, 16)

    def sp_lout(sp, t, n, ckv, kr):
        sp.wait_ge(s_lat, t + 1)
        sp.dma_start(ckv, lat[0:n, :]).then_inc(s_lout, 16)
        sp.dma_start(kr, kr2[0:n, 0]).then_inc(s_lout, 16)

    def pe_lat_tokens(pe, t):
        pe.wait_ge(s_lraw, 32 * (t + 1))
        for c in range(KR):
            pe.transpose(PS[:, 0, c * P:(c + 1) * P], latT[:, c], ident)
        pe.transpose(PS[:, 1, 0:MISC], latT[0:MISC, KR], ident[0:MISC, 0:MISC]).then_inc(s_la, 1)

    def pe_lat_back(pe):
        for c in range(KR):
            pe.transpose(PS[:, 2, c * P:(c + 1) * P], lat[:, c * P:(c + 1) * P], ident)
        pe.transpose(PS[:, 3, 0:P], kr2[:, :, :].rearrange("p a b -> p (a b)"), ident).then_inc(s_lb, 1)

    def pe_up(pe, slot, j, bank, done, first=False):
        for half in range(2):
            if first:
                pe.wait_ge(s_ul, 4 * (1 - j) + 2 * half + 2)
            for r in range(KR):
                for l, u, begin in ((LL, UH, True), (LH, UL, False), (LH, UH, False)):
                    last = pe.matmul(PS[:, bank + half], l[:, slot, r], u[:, j, r, 512 * half:512 * half + 512],
                                     start=(r == 0 and begin), stop=(r == KR - 1 and l is LH and u is UH))
        last.then_inc(done, 1)

    def pe_keys_back(pe, t):
        pe.wait_ge(s_kn, t + 1)
        for h in range(H):
            last = pe.transpose(PS[:, 4 + h // 4, (h % 4) * P:(h % 4 + 1) * P], kn[:, h * HD:(h + 1) * HD], ident)
        last.then_inc(s_kt, 1)

    def later(t):
        return not isinstance(t, int) or t > 0

    def latent_steps(eng, step):
        step(0, 0)
        with eng.Fori(0, (NT - 4) // 2) as i:
            step(2 * i + 1, 1)
            step(2 * i + 2, 0)
        for t in range(NT - 3, NKT):
            step(t, t % 2)

    def made(t):
        if not isinstance(t, int) or t + 2 < NT:
            return t + 2
        return NT if t == NT else None

    def pe_latents(pe):
        pe_lat_tokens(pe, 0)
        pe.wait_ge(s_lat, 1)
        pe_lat_back(pe)
        pe_lat_tokens(pe, 1)

        def step(t, slot):
            pe.wait_ge(s_ll, t + 1)
            if later(t):
                pe.wait_ge(s_vv, t)
            pe_up(pe, slot, 1, 6, s_vp, first=not later(t))
            if later(t):
                pe_keys_back(pe, t - 1)
            if not isinstance(t, int) or t + 1 < NKT:
                if isinstance(t, int) and NT <= t + 1 < NKT - 1:
                    pe.wait_ge(s_lca, 48 * (t + 2 - NT))
                else:
                    pe.wait_ge(s_lat, t + 2 if not isinstance(t, int) or t + 1 < NT else NT + 1)
                pe_lat_back(pe)
            if made(t) is not None:
                pe_lat_tokens(pe, made(t))
            if later(t):
                pe.wait_ge(s_kT, t)
            pe_up(pe, slot, 0, 4, s_kp, first=not later(t))
        latent_steps(pe, step)
        pe_keys_back(pe, NKT - 1)

    def act_lat_squares(act, t):
        act.wait_ge(s_la, t + 1)
        act.activation(ksq[:, 0:KV], PS[:, 0], ACT.Square, accum_out=lst[:, 0, H:H + 1])
        act.activation(ba[:, bass.ds(t, 1) if not isinstance(t, int) else slice(t, t + 1), :].rearrange("p a b -> p (a b)"), PS[:, 1, 0:BA], ACT.Copy)
        act.drain()
        act.activation(ksq[:, 0:ROPE], PS[:, 1, BA:MISC], ACT.Square, accum_out=lst[:, 0, H + 1:H + 2]).then_inc(s_lsq, 1)

    def act_key_squares(act, t):
        act.drain()
        act.wait_ge(s_kp, t + 1)
        act.activation(ksq[:, :].rearrange("p (a b) -> p a b", a=2), PS[:, 4:6], ACT.Square).then_inc(s_ksq, 1)

    def act_values(act, t):
        act.wait_ge(s_vp, t + 1)
        act.activation(V[:, bass.ds(t, 1)].rearrange("p a (b n) -> p (a b) n", b=2), PS[:, 6:8], ACT.Copy).then_inc(s_vv, 1)

    def act_lat_hi(act, t, slot):
        act.wait_ge(s_lb, t + 1)
        act.activation(LH[:, slot].rearrange("p a b -> p (a b)"), PS[:, 2], ACT.Copy).then_inc(s_lh, 1)
        act.activation(krT[:, bass.ds(t * P, P)], PS[:, 3, 0:P], ACT.Copy).then_inc(s_krT, 1)

    def act_keys(act, t):
        act.wait_ge(s_kt, t + 1)
        for g in range(2):
            last = act.activation(kT[:, 4 * g:4 * g + 4, bass.ds(t * P, P)], PS[:, 4 + g].rearrange("p (h n) -> p h n", h=4),
                                  ACT.Copy, scale=colB[:, B_KN:B_KN + 1])
        last.then_inc(s_kT, 1)

    def act_latents(act):
        def split_hi(i):
            act.wait_ge(s_u[i % 2], 16 * (i // 2 + 1))
            act.activation(UH[:, 1 - i // 4, :, 256 * (i % 4):256 * (i % 4) + 256], Uraw[:, i % 2], ACT.Copy).then_inc(s_uh, 1)
        act.wait_ge(s_rot, 1)
        act_lat_squares(act, 0)
        split_hi(0)
        act_lat_hi(act, 0, 0)
        act_lat_squares(act, 1)
        for i in range(1, 8):
            split_hi(i)

        def step(t, slot):
            if later(t):
                act_keys(act, t - 1)
            if not isinstance(t, int) or t + 1 < NKT:
                act_lat_hi(act, t + 1, 1 - slot)
            if made(t) is not None:
                if later(t):
                    act.wait_ge(s_kn, t)
                act_lat_squares(act, made(t))
            act_values(act, t)
            act_key_squares(act, t)
        latent_steps(act, step)
        act_keys(act, NKT - 1)

    def dve_latent(dve, t, tile):
        dve.wait_ge(s_lsq, t + 1)
        r = lst[:, 1]
        dve.tensor_scalar(lst[:, 0, H:H + 1], lst[:, 0, H:H + 1], 1.0 / KV, EPS, ALU.mult, ALU.add)
        dve.tensor_scalar(lst[:, 0, H + 1:H + 2], lst[:, 0, H + 1:H + 2], 1.0 / ROPE, EPS, ALU.mult, ALU.add)
        dve.drain()
        rsqrt(dve, lst[:, 1, H:H + 2], lst[:, 2, H:H + 2], lst[:, 0, H:H + 2])
        if not isinstance(t, int) or t:
            dve.wait_ge(s_lout, 32 * t)
        dve.scalar_tensor_tensor(lat[:, :], PS[:, 0], r[:, H:H + 1], kvg[:, :], ALU.mult, ALU.mult)
        x, half = PS[:, 1, BA:MISC], ROPE // 2
        cs = rotk[:, bass.ds(tile, 1)].rearrange("p a c n -> p (a c) n")
        dve.scalar_tensor_tensor(lrt[:, 0], x, r[:, H + 1:H + 2], cs[:, 0], ALU.mult, ALU.mult)
        dve.scalar_tensor_tensor(lrt[:, 1, 0:half], x[:, half:ROPE], r[:, H + 1:H + 2], cs[:, 1, 0:half], ALU.mult, ALU.mult)
        dve.scalar_tensor_tensor(lrt[:, 1, half:ROPE], x[:, 0:half], r[:, H + 1:H + 2], cs[:, 1, half:ROPE], ALU.mult, ALU.mult)
        dve.drain()
        dve.tensor_tensor(kr2[:, 0], lrt[:, 0], lrt[:, 1], ALU.add)
        dve.tensor_tensor(kr2[:, 1], lrt[:, 0], lrt[:, 1], ALU.add).then_inc(s_lat, 1)

    def dve_lat_lo(dve, t, slot):
        dve.wait_ge(s_lh, t + 1)
        dve.tensor_tensor(LL[:, slot].rearrange("p a b -> p (a b)"), PS[:, 2], LH[:, slot].rearrange("p a b -> p (a b)").bitcast(F32), ALU.subtract).then_inc(s_ll, 1)

    def dve_keys(dve, t):
        dve.wait_ge(s_ksq, t + 1)
        ss, r, tmp = lst[:, 0, 0:H], lst[:, 1, 0:H], lst[:, 2, 0:H]
        dve.tensor_reduce(ss, ksq[:, :].rearrange("p (h n) -> p h n", h=H), AX.X, ALU.add)
        dve.drain()
        dve.tensor_scalar(ss, ss, 1.0 / HD, EPS, ALU.mult, ALU.add)
        dve.drain()
        rsqrt(dve, r, tmp, ss)
        for g in range(2):
            last = dve.tensor_tensor(kn[:, 512 * g:512 * g + 512].rearrange("p (h n) -> p h n", h=4), PS[:, 4 + g].rearrange("p (h n) -> p h n", h=4),
                                     r[:, 4 * g:4 * g + 4].unsqueeze(2).to_broadcast([P, 4, HD]), ALU.mult)
        last.then_inc(s_kn, 1)

    def dve_latents(dve):
        dve.memset(lst[:, :, :], 1.0)
        dve.wait_ge(s_tab, 64)
        half = ROPE // 2
        for table, g in ((rotq, gq[:, 0]), (rotk, gq[:, 1])):
            cos, sin = rot[:, :, 0:half], rot[:, :, half:ROPE]

            def row(c):
                return g[:, c:c + half].unsqueeze(1).to_broadcast([P, NT + 1, half])
            dve.tensor_tensor(table[:, :, 0, 0:half], cos, row(0), ALU.mult)
            dve.tensor_tensor(table[:, :, 0, half:ROPE], cos, row(half), ALU.mult)
            dve.tensor_tensor(table[:, :, 1, 0:half], sin, row(half), ALU.mult)
            dve.tensor_tensor(table[:, :, 1, half:ROPE], sin, row(0), ALU.mult)
            dve.drain()
            dve.tensor_scalar(table[:, :, 1, 0:half], table[:, :, 1, 0:half], -1.0, None, ALU.mult)
        dve.drain().then_inc(s_rot, 1)

        def split_lo(i):
            dve.wait_ge(s_uh, i + 1)
            c = slice(256 * (i % 4), 256 * (i % 4) + 256)
            dve.tensor_tensor(UL[:, 1 - i // 4, :, c], Uraw[:, i % 2], UH[:, 1 - i // 4, :, c].bitcast(F32), ALU.subtract).then_inc(s_ul, 1)
        dve_latent(dve, 0, 0)
        split_lo(0)
        dve_lat_lo(dve, 0, 0)
        for i in range(1, 8):
            split_lo(i)
            if i == 1:
                dve.wait_ge(s_lb, 1)
                dve_latent(dve, 1, 1)

        def step(t, slot):
            if not isinstance(t, int) or t + 1 < NKT:
                dve_lat_lo(dve, t + 1, 1 - slot)
            n = made(t)
            if n is not None:
                dve.wait_ge(s_lb, t + 2)
                dve_latent(dve, n, n)
            dve_keys(dve, t)
        latent_steps(dve, step)

    NQ = NT + 1
    NX = NQ * H
    jobs = {-1: [("q", 0, 0), ("q", 0, 1), ("q", 0, 2), ("b", 0, 0), ("b", 0, 1), ("b", 0, 2)]}
    for i in range(NQ):
        for step, job in ((0, ("q", 0)), (1, ("q", 1)), (2, ("q", 2)), (5, ("b", 0)), (6, ("b", 1)), (6, ("b", 2))):
            if i + 1 < NQ:
                jobs.setdefault(H * i + step, []).append((job[0], i + 1, job[1]))
        for g in range(2):
            jobs.setdefault(H * i + 4 * g + 5, []).append(("o", 2 * i + g, 0))
    order = [(x, job) for x in sorted(jobs) for job in jobs[x]]
    turn = {job: n for n, (_, job) in enumerate(order)}

    def keys_of(i):
        base, n = (0, P * (i + 1)) if i < NT else (SEQ, PAST + DEC)
        return base, n, [min(P, n - P * k) for k in range(-(-n // P))]

    second = [0]
    for x in range(NX):
        second.append(second[-1] + (len(keys_of(x // H)[2]) > 4))

    def scores_of(x):
        b = 2 * (x % 2)
        return PS[:, b:b + 2].rearrange("p a b -> p (a b)")[:, 0:keys_of(x // H)[1]]

    def sp_attention(sp):
        def load_q(i):
            sp.dma_start(qraw[:, :], scr["proj"][C_Q:C_Q + 12, :, i * P:(i + 1) * P].rearrange("c p n -> p c n")).then_inc(s_qraw, 16)
        load_q(0)
        for i in range(NQ):
            if i + 1 < NQ:
                sp.wait_ge(s_t7, turn[("q", i, 2)] + 1)
                load_q(i + 1)
            for g in range(2):
                if i:
                    sp.wait_ge(s_r7, turn[("o", 2 * i - 2 + g, 0)] + 1)
                    store_ub(sp, 2 * i - 2 + g)
                sp.dma_start(zb[:, g], scr["proj"][C_ZB + 4 * g:C_ZB + 4 * g + 4, :, i * P:(i + 1) * P].rearrange("c p n -> p c n")).then_inc(s_zb[g], 16)
        for g in range(2):
            sp.wait_ge(s_r7, turn[("o", 2 * NT + g, 0)] + 1)
            store_ub(sp, 2 * NT + g)
        for g in range(2):
            sp.wait_ge(s_us[g], 16 * NQ)

    def store_ub(sp, og):
        i, g = divmod(og, 2)
        sp.dma_start(scr["u"][H + 4 * g:H + 4 * g + 4, :, i * P:(i + 1) * P].rearrange("c p n -> p c n"), ub[:, g]).then_inc(s_us[g], 16)

    def pe_job(pe, job):
        kind, i, part = job
        n = turn[job]
        if n:
            pe.wait_ge(s_r7, n)
        if kind == "q":
            pe.wait_ge(s_qraw, 16 * (i + 1))
            srcs = [qraw[:, 4 * part + c] for c in range(4)]
        elif kind == "b" and part < 2:
            pe.wait_ge(s_qn, i + 1)
            srcs = [qsq[:, 4 * part + c, 0:HD] for c in range(4)]
        elif kind == "b":
            pe.wait_ge(s_qrr, i + 1)
            srcs = [qrr[:, 2 * c:2 * c + 2].rearrange("p a b -> p (a b)") for c in range(4)]
        else:
            pe.wait_ge(s_on, i + 1)
            srcs = [on[:, c] for c in range(4)]
        for c, src in enumerate(srcs):
            last = pe.transpose(PS[:, 7, c * P:(c + 1) * P], src, ident)
        last.then_inc(s_t7, 1)

    def pe_scores(pe, x):
        i, h = divmod(x, H)
        base, n, _ = keys_of(i)
        if h == 0:
            pe.wait_ge(s_qe, 3 * (i + 1))
        if x >= 2:
            pe.wait_ge(s_ex, x - 1)
        lo = ROPE * (h % 2)
        for b in range(-(-n // 512)):
            w = min(512, n - 512 * b)
            c = base + 512 * b
            out = PS[:, 2 * (x % 2) + b, 0:w]
            pe.matmul(out, qT[:, i % 2, h], kT[:, h, c:c + w], start=True, stop=False)
            last = pe.matmul(out, qrT[lo:lo + ROPE, i % 2, h // 2], krT[lo:lo + ROPE, c:c + w], start=False, stop=True)
        last.then_inc(s_sc, 1)

    def pe_transposes(pe, x):
        widths = keys_of(x // H)[2]
        pe.wait_ge(s_ex, x + 1)
        if x:
            pe.wait_ge(s_pa, x)
            if second[x]:
                pe.wait_ge(s_pd, second[x])
        for k, w in enumerate(widths):
            last = pe.transpose(PS[0:w, 4 + k // 4, (k % 4) * P:(k % 4 + 1) * P], pr[:, x % 2, k * P:k * P + w], ident)
        last.then_inc(s_pt, 1)

    def pe_values(pe, x):
        i, h = divmod(x, H)
        base, n, widths = keys_of(i)
        pe.wait_ge(s_pa, x + 1)
        if second[x + 1]:
            pe.wait_ge(s_pd, second[x + 1])
        if x % 4 == 0 and x:
            pe.wait_ge(s_on, x // 4)
        for k, w in enumerate(widths):
            last = pe.matmul(PS[:, 6, (h % 4) * P:(h % 4 + 1) * P], pT[0:w, x % 2, k], V[0:w, base // P + k, h * HD:(h + 1) * HD],
                             start=(k == 0), stop=(k == len(widths) - 1))
        last.then_inc(s_pv, 1)

    def pe_attention(pe):
        for job in jobs[-1]:
            pe_job(pe, job)
        pe_scores(pe, 0)
        for x in range(NX + 2):
            if x + 1 < NX:
                pe_scores(pe, x + 1)
            if 1 <= x <= NX:
                pe_values(pe, x - 1)
            if x < NX:
                pe_transposes(pe, x)
            for job in jobs.get(x, []):
                pe_job(pe, job)

    def act_job(act, job):
        kind, i, part = job
        if kind == "o" or (kind == "b" and part == 2):
            return
        act.wait_ge(s_t7, turn[job] + 1)
        if kind == "q":
            if i:
                act.wait_ge(s_qn, i)
                act.wait_ge(s_qrr, i)
            act.activation(qtok[:, :, :].rearrange("p a b -> p (a b)")[:, 512 * part:512 * part + 512], PS[:, 7], ACT.Copy).then_inc(s_r7, 1)
        else:
            act.activation(qT[:, i % 2, 4 * part:4 * part + 4].rearrange("p a b -> p (a b)"), PS[:, 7], ACT.Copy, scale=colB[:, B_QN:B_QN + 1]).then_inc(s_r7, 1)
            act.wait_ge(s_r7, turn[job] + 1)
            act.sem_inc(s_qe, 1)

    def act_exp(act, x):
        n = keys_of(x // H)[1]
        act.wait_ge(s_mx, x + 1)
        if x >= 2:
            act.wait_ge(s_pt, x - 1)
        if x % 4 == 0 and x >= 8:
            act.wait_ge(s_on, x // 4 - 1)
        act.activation(pr[:, x % 2, 0:n], scores_of(x), ACT.Exp, bias=amx[:, x % 2, 1:2], scale=SCALE,
                       accum_out=ars[:, x // 4 % 2, x % 4:x % 4 + 1]).then_inc(s_ex, 1)

    def act_attention(act):
        for job in jobs[-1]:
            act_job(act, job)
        act_exp(act, 0)
        for x in range(NX):
            if x + 1 < NX:
                act_exp(act, x + 1)
            nk = min(4, len(keys_of(x // H)[2]))
            act.wait_ge(s_pt, x + 1)
            if x >= 2:
                act.wait_ge(s_pv, x - 1)
            act.activation(pT[:, x % 2, 0:nk].rearrange("p a b -> p (a b)"), PS[:, 4, 0:nk * P], ACT.Copy).then_inc(s_pa, 1)
            for job in jobs.get(x, []):
                act_job(act, job)

    def pool_attention(pool):
        half = ROPE // 2
        for i in range(NQ):
            pool.wait_ge(s_r7, turn[("q", i, 2)] + 1)
            if i:
                pool.wait_ge(s_t7, turn[("b", i - 1, 2)] + 1)
            pool.tensor_tensor(qsq[:, :, :], qtok[:, :, :], qtok[:, :, :], ALU.mult).then_inc(s_qsq, 1)
            pool.wait_ge(s_qr, i + 1)
            r = qst[:, 1, 1].unsqueeze(2).to_broadcast([P, H, ROPE])
            cos = rotq[:, i:i + 1, 0].to_broadcast([P, H, ROPE])
            sin = rotq[:, i:i + 1, 1].to_broadcast([P, H, ROPE])
            pool.tensor_tensor(qrr[:, :, :], qtok[:, :, HD:QH], r, ALU.mult)
            pool.drain()
            pool.tensor_tensor(qrx[:, 0], qrr[:, :, :], cos, ALU.mult)
            pool.tensor_tensor(qrx[:, 1, :, 0:half], qrr[:, :, half:ROPE], sin[:, :, 0:half], ALU.mult)
            pool.tensor_tensor(qrx[:, 1, :, half:ROPE], qrr[:, :, 0:half], sin[:, :, half:ROPE], ALU.mult)
            pool.drain()
            pool.tensor_tensor(qrr[:, :, :], qrx[:, 0], qrx[:, 1], ALU.add).then_inc(s_qrr, 1)

    def dve_q_norms(dve, i):
        dve.wait_ge(s_qsq, i + 1)
        ss = qst[:, 0]
        dve.tensor_reduce(ss[:, 0], qsq[:, :, 0:HD], AX.X, ALU.add)
        dve.tensor_reduce(ss[:, 1], qsq[:, :, HD:QH], AX.X, ALU.add)
        dve.drain()
        dve.tensor_scalar(ss[:, 0], ss[:, 0], 1.0 / HD, EPS, ALU.mult, ALU.add)
        dve.tensor_scalar(ss[:, 1], ss[:, 1], 1.0 / ROPE, EPS, ALU.mult, ALU.add)
        dve.drain()
        if i:
            dve.wait_ge(s_qrr, i)
        rsqrt(dve, qst[:, 1].rearrange("p a b -> p (a b)"), qst[:, 2].rearrange("p a b -> p (a b)"), ss.rearrange("p a b -> p (a b)"))
        dve.drain().then_inc(s_qr, 1)
        dve.tensor_tensor(qsq[:, :, 0:HD], qtok[:, :, 0:HD], qst[:, 1, 0].unsqueeze(2).to_broadcast([P, H, HD]), ALU.mult).then_inc(s_qn, 1)

    def dve_job(dve, job):
        kind, i, part = job
        if kind == "q" and part == 2:
            dve_q_norms(dve, i)
        if kind == "b" and part == 2:
            dve.wait_ge(s_t7, turn[job] + 1)
            dve.tensor_copy(qrT[:, i % 2].rearrange("p a b -> p (a b)"), PS[:, 7]).then_inc(s_r7, 1)
            dve.wait_ge(s_r7, turn[job] + 1)
            dve.sem_inc(s_qe, 1)
        if kind == "o":
            t, g = divmod(i, 2)
            dve.wait_ge(s_t7, turn[job] + 1)
            dve.wait_ge(s_zb[g], 16 * (t + 1))
            if t:
                dve.wait_ge(s_us[g], 16 * t)
            dve.tensor_tensor(ub[:, g].rearrange("p a b -> p (a b)"), PS[:, 7], zb[:, g].rearrange("p a b -> p (a b)"), ALU.mult).then_inc(s_r7, 1)

    def dve_max(dve, x):
        i, n = x // H, keys_of(x // H)[1]
        s = scores_of(x)
        dve.wait_ge(s_sc, x + 1)
        if i < NT:
            dve.memset(s[0:CHUNK, n - CHUNK:n], -1.0e30)
            dve.drain()
        dve.tensor_reduce(amx[:, x % 2, 0:1], s, AX.X, ALU.max)
        dve.drain()
        dve.tensor_scalar(amx[:, x % 2, 1:2], amx[:, x % 2, 0:1], -SCALE, None, ALU.mult).then_inc(s_mx, 1)

    def dve_attention(dve):
        for job in jobs[-1]:
            dve_job(dve, job)
        dve_max(dve, 0)
        for x in range(NX + 2):
            if x + 1 < NX:
                dve_max(dve, x + 1)
            if 4 <= x <= NX and x % 4 == 0:
                g = x // 4 - 1
                dve.wait_ge(s_pv, x)
                dve.reciprocal(ari[:, :], ars[:, g % 2])
                dve.drain()
                if g:
                    dve.wait_ge(s_t7, turn[("o", g - 1, 0)] + 1)
                dve.tensor_tensor(on[:, :, :], PS[:, 6].rearrange("p (h n) -> p h n", h=4), ari[:, :].unsqueeze(2).to_broadcast([P, 4, HD]), ALU.mult).then_inc(s_on, 1)
            if x < NX:
                nk = len(keys_of(x // H)[2])
                if nk > 4:
                    dve.wait_ge(s_pt, x + 1)
                    if x >= 2:
                        dve.wait_ge(s_pv, x - 1)
                    dve.tensor_copy(pT[:, x % 2, 4:nk].rearrange("p a b -> p (a b)"), PS[:, 5, 0:(nk - 4) * P]).then_inc(s_pd, 1)
            for job in jobs.get(x, []):
                dve_job(dve, job)

    p3 = ExitStack()
    NL7 = len(LEVELS)
    TVN = 6
    tvs = sb(p3, "tvs", [P, NT + 1, TVN, H])
    gat = sb(p3, "gat", [P, NT + 1, H])
    gtm = sb(p3, "gtm", [P, 4, NT + 1, H])
    avec = sb(p3, "avec", [P, 2, H])
    gcT = sb(p3, "gcT", [(NT + 1) * H, P])
    QKV = sb(p3, "QKV", [P, 2, 3 * H, P])
    GB = sb(p3, "GB", [P, 2, H * P])
    za = sb(p3, "za", [P, 2, H, P])
    tv = sb(p3, "tv", [P, 2, TVN, H])
    S = sb(p3, "S", [P, 2, H, HD])
    dst = sb(p3, "dst", [P, 3, 2, 2, 4])
    vec = sb(p3, "vec", [P, 2, 5, 2, 4])
    ost = sb(p3, "ost", [P, 4, 2, 4])

    def per_group(name, slots=None):
        shape = [P, 2] + ([slots] if slots else []) + [4 * P]
        return sb(p3, name, shape)
    Kt = per_group("Kt", 2)
    Vn = per_group("Vn", 2)
    sq = per_group("sq")
    sq2 = per_group("sq2")
    E = per_group("E")
    Em = per_group("Em")
    Es = per_group("Es")
    NL = per_group("NL")
    AT = per_group("AT")
    QL = per_group("QL", NL7)
    X = per_group("X")
    XT = per_group("XT")
    RR = per_group("RR")
    Z = per_group("Z")
    ZD = per_group("ZD")
    O1 = per_group("O1")
    O2 = per_group("O2")
    ON = per_group("ON")
    UA = per_group("UA")
    p3.close()

    s_av = sem("decay_vectors_loaded")
    s_bs = sem("beta_ready")
    s_gd1 = sem("gate_softplus_step")
    s_gg = sem("log_decay_ready")
    s_gp = sem("log_decay_summed")
    s_gx = sem("log_decay_copied")
    s_ge = sem("decay_scalars_ready")
    s_gT = sem("log_decay_rows_ready")
    s_gw = sem("log_decay_rows_stored")
    s_st = sem("sample_state_loaded")
    s_zero = sem("delta_buffers_set")
    s_tv = sem("tile_scalars_ready")
    s_seen = sem("level_product_seen")
    s_in = [sem(f"qkv_tile_loaded_{i}") for i in range(2)]
    s_za = [sem(f"za_tile_loaded_{i}") for i in range(2)]
    s_ua = sem("u_a_stored")
    s_so = sem("states_stored")

    PE_PREP, PE_MAIN, PE_OUT = ("k", "q", "v", "kk", "qk"), ("l", "x0") + tuple(
        f"{a}{l}" for l in range(1, NL7) for a in "px") + ("ks", "qs", "y", "st", "av"), ("on",)
    ACT_PREP, ACT_MAIN, ACT_OUT = ("k", "q", "e"), tuple(f"x{l}" for l in range(NL7)) + ("o1",), ("sq",)
    DVE_PREP, DVE_MAIN, DVE_OUT = ("sub", "vn", "nl", "at"), tuple(f"q{l}" for l in range(NL7)) + (
        "r", "zd", "z", "s", "o2"), ("on", "u")
    s_pe = {n: [sem(f"delta_pe_{n}_{g}") for g in range(2)] for n in ("prep", "main", "out")}
    s_ac = {n: [sem(f"delta_act_{n}_{g}") for g in range(2)] for n in ("prep", "main", "out")}
    s_dv = {n: [sem(f"delta_dve_{n}_{g}") for g in range(2)] for n in ("prep", "main", "out")}
    s_em = [sem(f"masked_decays_ready_{g}") for g in range(2)]

    def after(eng, sems, steps, g, t, step):
        eng.wait_ge(sems[g], len(steps) * t + steps.index(step) + 1)

    def bank(g, b):
        return PS[:, 4 * g + b]

    def hs(x, h):
        return x[:, h * P:(h + 1) * P]

    def heads(x):
        return x.rearrange("p (h n) -> p h n", h=4)

    def wide(v):
        return v.unsqueeze(2).to_broadcast([P, 4, P])

    def run_tiles(eng, body):
        body(0, 0, True)
        with eng.Fori(0, (NT - 2) // 2) as i:
            body(2 * i + 1, 1, False)
            body(2 * i + 2, 0, False)
        body(NT - 1, 1, False)
        body(NT, 0, False)

    p4 = ExitStack()
    M4 = sb(p4, "M4", [P, KD, TOK])
    gate = sb(p4, "gate", [P, 2, D])
    Vraw = sb(p4, "Vraw", [P, 2, KD, 256])
    p4a = ExitStack()
    FH = sb(p4a, "FH", [P, KD, TOK], F32R)
    FL = sb(p4a, "FL", [P, KD, TOK], F32R)
    VH = sb(p4a, "VH", [P, 2, KD, 256], F32R)
    VL = sb(p4a, "VL", [P, 2, KD, 256], F32R)
    NFR = 4
    fr = sb(p4a, "fr", [P, NFR, TOK])
    gr = sb(p4a, "gr", [P, 2, TOK])
    p4a.close()
    p4b = ExitStack()
    OH = sb(p4b, "OH", [P, KD, D], F32R)
    OL = sb(p4b, "OL", [P, KD, D], F32R)
    MH = sb(p4b, "MH", [P, 2, KD, P], F32R)
    ML = sb(p4b, "ML", [P, 2, KD, P], F32R)
    xt = sb(p4b, "xt", [P, 2, D])
    yt = sb(p4b, "yt", [P, 2, D])
    p4b.close()
    p4.close()
    GD = M4[:, 0:2, 0:D]

    s_fr = [sem(f"u_rows_loaded_{i}") for i in range(NFR)]
    s_fh = sem("u_hi_ready")
    s_fl = sem("u_lo_ready")
    s_vr = [sem(f"w_o_loaded_{i}") for i in range(2)]
    s_vh = sem("w_o_hi_ready")
    s_vl = sem("w_o_lo_ready")
    s_o = sem("branch_chunk_in_psum")
    s_ur = sem("u_a_row_used")
    s_gr = [sem(f"gate_rows_loaded_{i}") for i in range(2)]
    s_m = sem("merged_chunk_ready")
    s_gdg = sem("gate_diagonal_ready")
    s_gps = sem("gate_in_psum")
    s_gok = sem("gate_ready")
    s_or = [sem(f"w_out_loaded_{i}") for i in range(2)]
    s_oh = sem("w_out_hi_ready")
    s_ol = sem("w_out_lo_ready")
    s_mh = sem("merged_tile_hi_ready")
    s_ml = sem("merged_tile_lo_ready")
    s_yp = sem("y_in_psum")
    s_xt = [sem(f"x_tile_loaded_{i}") for i in range(2)]
    s_y = sem("y_tile_ready")
    s_ys = [sem(f"y_tile_stored_{i}") for i in range(2)]

    def sp_out(sp):
        for l in range(2):
            sp_w_o(sp, l)
        for n in range(2):
            sp_gate_rows(sp, n)

        def row(r):
            if r >= NFR:
                sp.wait_ge(s_fl, r - NFR + 1)
            sp.dma_start(fr[:, r % NFR], scr["u"][r, :, 0:TOK]).then_inc(s_fr[r % NFR], 16)

        def weights(l):
            sp.wait_ge(s_vl, l - 1)
            sp_w_o(sp, l)

        def gates(n):
            sp.wait_ge(s_m, n - 1)
            sp_gate_rows(sp, n)

        for r in range(KD):
            row(r)
        weights(2)
        for r in range(KD, KD + NFR):
            row(r)
        for l in range(3, 6):
            weights(l)
            gates(2 * l - 4)
            gates(2 * l - 3)
        gates(KD)
        for r in range(KD + NFR, 2 * KD):
            row(r)
        gates(KD + 1)
        weights(6)
        weights(7)
        for n in range(KD + 2, 2 * KD):
            gates(n)
            if n in (2 * KD - 3, 2 * KD - 2):
                i = n - (2 * KD - 3)
                sp.wait_ge(s_vl, KD - 1 + i)
                sp_w_out(sp, i)

    def sp_w_out(sp, i):
        sp.dma_start(Vraw[:, i % 2], a["w_out"][0, :, 256 * i:256 * i + 256].rearrange("(k p) n -> p k n", p=P)).then_inc(s_or[i % 2], 16)

    def sp_w_o(sp, l):
        w = a["w_o_dn"] if l < 4 else a["w_o_mla"]
        sp.dma_start(Vraw[:, l % 2], w[0, :, 256 * (l % 4):256 * (l % 4) + 256].rearrange("(k p) n -> p k n", p=P)).then_inc(s_vr[l % 2], 16)

    def sp_gate_rows(sp, n):
        sp.dma_start(gr[:, n % 2], scr["proj"][C_GA + n, :, 0:TOK]).then_inc(s_gr[n % 2], 16)

    def act_out(act):
        def split_w(l):
            act.wait_ge(s_vr[l % 2], 16 * (l // 2 + 1))
            if l >= 2:
                act.wait_ge(s_o, 2 * l - 2)
            act.activation(VH[:, l % 2], Vraw[:, l % 2], ACT.Copy).then_inc(s_vh, 1)
        split_w(0)
        for r in range(2 * KD):
            if r == KD:
                split_w(1)
                for l in range(2, 5):
                    split_w(l)
            if r >= KD:
                if r < 2 * KD - 1:
                    act.wait_ge(s_ur, r - KD + 1)
                else:
                    act.wait_ge(s_o, KD)
            act.wait_ge(s_fr[r % NFR], 16 * (r // NFR + 1))
            act.activation(FH[:, r % KD], fr[:, r % NFR], ACT.Copy).then_inc(s_fh, 1)
        for l in range(5, KD):
            split_w(l)

    def dve_gate(dve):
        for i in range(4):
            j, s = 16 + 4 * (i % 2), i // 2
            dve.tensor_tensor(GD[:, s, 512 * (i % 2):512 * (i % 2) + 512].rearrange("p (j n) -> p j n", j=4), ident.unsqueeze(1).to_broadcast([P, 4, P]),
                              mod[:, j:j + 4, s:s + 1].to_broadcast([P, 4, P]), ALU.mult).then_inc(s_gdg, 1)
        for i in range(4):
            dve.wait_ge(s_gps, i + 1)
            dve.tensor_copy(gate[:, i // 2, 512 * (i % 2):512 * (i % 2) + 512], PS[:, i]).then_inc(s_gok, 1)

    def dve_branches(dve):
        def split_w(l):
            dve.wait_ge(s_vh, l + 1)
            dve.tensor_tensor(VL[:, l % 2], Vraw[:, l % 2], VH[:, l % 2].bitcast(F32), ALU.subtract).then_inc(s_vl, 1)

        def merge(n):
            d = n % KD
            dve.wait_ge(s_o, n + 1)
            dve.wait_ge(s_gr[n % 2], 16 * (n // 2 + 1))
            b3 = PS[:, 3 * (n % 2):3 * (n % 2) + 3, 0:TB]
            rows3 = gr[:, n % 2].rearrange("p (b n) -> p b n", b=3)
            if n < KD:
                dve.tensor_tensor(M4[:, d].rearrange("p (b n) -> p b n", b=3), b3, rows3, ALU.mult).then_inc(s_m, 1)
            else:
                dve.tensor_tensor(rows3, b3, rows3, ALU.mult)
                dve.drain()
                dve.tensor_tensor(M4[:, d], M4[:, d], gr[:, n % 2], ALU.add).then_inc(s_m, 1)

        dve_gate(dve)
        split_w(0)
        for r in range(2 * KD):
            if r == KD:
                split_w(1)
                for n in range(KD - 1):
                    merge(n)
                    if n % 2:
                        split_w(n // 2 + 2)
            if r == 2 * KD - 1:
                merge(KD - 1)
            dve.wait_ge(s_fh, r + 1)
            dve.tensor_tensor(FL[:, r % KD], fr[:, r % NFR], FH[:, r % KD].bitcast(F32), ALU.subtract).then_inc(s_fl, 1)
        for n in range(KD, 2 * KD):
            if n % 2 == 0 and n // 2 + 1 < KD:
                split_w(n // 2 + 1)
            merge(n)

    def pe_branches(pe):
        for i in range(4):
            pe.wait_ge(s_gdg, i + 1)
            pe.matmul(PS[:, i], ones, GD[:, i // 2, 512 * (i % 2):512 * (i % 2) + 512], start=True, stop=True).then_inc(s_gps, 1)
        pe.wait_ge(s_gok, 4)
        for n in range(2 * KD):
            l = n // 2
            pe.wait_ge(s_vl, l + 1)
            if n >= 2:
                pe.wait_ge(s_m, n - 1)
            for k in range(KD):
                if n % KD == 0:
                    pe.wait_ge(s_fl, n + k + 1)
                for w, u, first in ((VL, FH, True), (VH, FL, False), (VH, FH, False)):
                    for b in range(NB):
                        last = pe.matmul(PS[:, 3 * (n % 2) + b, 0:TB], w[:, l % 2, k, (n % 2) * P:(n % 2) * P + P], u[:, k, b * TB:(b + 1) * TB],
                                         start=(k == 0 and first), stop=(k == KD - 1 and u is FH and not first))
                if n == KD - 1 and k < KD - 1:
                    last.then_inc(s_ur, 1)
            last.then_inc(s_o, 1)

    def sp_y(sp):
        for i in range(2, 4):
            sp.wait_ge(s_ol, i - 1)
            sp_w_out(sp, i)
        sp.wait_ge(s_m, 2 * KD)
        for s in range(2):
            sp.dma_start(xt[:, s], a["x_prompt"][0, P * s:P * s + P]).then_inc(s_xt[s], 16)

        def store(t, s):
            sp.wait_ge(s_y, 2 * (t + 1))
            sp.dma_start(o["y_prompt"][0, bass.ds(t * P, P)], yt[:, s]).then_inc(s_ys[s], 16)
        with sp.Fori(0, NT // 2 - 1) as i:
            for s in range(2):
                store(2 * i + s, s)
                sp.dma_start(xt[:, s], a["x_prompt"][0, bass.ds(P * (2 * i + s + 2), P)]).then_inc(s_xt[s], 16)
        store(NT - 2, 0)
        sp.dma_start(xt[0:DEC, 0], a["x_sample"][0]).then_inc(s_xt[0], 16)
        store(NT - 1, 1)
        sp.wait_ge(s_y, 2 * NT + 2)
        sp.dma_start(o["y_sample"][0], yt[0:DEC, 0]).then_inc(s_ys[0], 16)
        sp.wait_ge(s_ys[0], 16 * 5)
        sp.wait_ge(s_ys[1], 16 * 4)

    def act_y(act):
        act.wait_ge(s_o, 2 * KD)
        act.sem_inc(s_yp, 2)

        def split_w(i):
            act.wait_ge(s_or[i % 2], 16 * (i // 2 + 1))
            act.activation(OH[:, :, 256 * i:256 * i + 256], Vraw[:, i % 2], ACT.Copy).then_inc(s_oh, 1)

        def tile(t, slot, n):
            act.wait_ge(s_yp, t + 1)
            act.activation(MH[:, slot, :, 0:n], M4[:, :, bass.ds(t * P, n)], ACT.Copy).then_inc(s_mh, 1)
        split_w(0)
        act.wait_ge(s_m, 2 * KD)
        tile(0, 0, P)
        for i in range(1, 4):
            split_w(i)
        with act.Fori(0, NT // 2 - 1) as i:
            tile(2 * i + 1, 1, P)
            tile(2 * i + 2, 0, P)
        tile(NT - 1, 1, P)
        tile(NT, 0, DEC)

    def dve_y(dve):
        def low(t, slot, n):
            dve.wait_ge(s_mh, t + 1)
            dve.tensor_tensor(ML[:, slot, :, 0:n], M4[:, :, bass.ds(t * P, n)], MH[:, slot, :, 0:n].bitcast(F32), ALU.subtract).then_inc(s_ml, 1)

        for i in range(4):
            if i == 1:
                low(0, 0, P)
            dve.wait_ge(s_oh, i + 1)
            dve.tensor_tensor(OL[:, :, 256 * i:256 * i + 256], Vraw[:, i % 2], OH[:, :, 256 * i:256 * i + 256].bitcast(F32), ALU.subtract).then_inc(s_ol, 1)

        def body(t, slot, n, first):
            if not (isinstance(t, int) and t == NT):
                low(t + 1, 1 - slot, DEC if isinstance(t, int) and t == NT - 1 else P)
            dve.wait_ge(s_yp, t + 3)
            for h in range(2):
                c = slice(512 * h, 512 * h + 512)
                if h == 0:
                    dve.wait_ge(s_xt[slot], 16 * ((t - slot) // 2 + 1))
                    if not (isinstance(t, int) and t < 2):
                        dve.wait_ge(s_ys[slot], 16 * ((t - slot) // 2))
                g = 1 if isinstance(t, int) and t == NT else 0
                dve.tensor_tensor(yt[0:n, slot, c], PS[0:n, 4 * slot + h], gate[0:n, g, c], ALU.mult)
                dve.drain()
                dve.tensor_tensor(yt[0:n, slot, c], yt[0:n, slot, c], xt[0:n, slot, c], ALU.add).then_inc(s_y, 1)
        body(0, 0, P, True)
        body(1, 1, P, False)
        with dve.Fori(1, NT // 2 - 1) as i:
            body(2 * i, 0, P, False)
            body(2 * i + 1, 1, P, False)
        body(NT - 2, 0, P, False)
        body(NT - 1, 1, P, False)
        body(NT, 0, DEC, False)

    def pe_y(pe):
        def body(t, slot, n, first):
            pe.wait_ge(s_ml, t + 1)
            if not (isinstance(t, int) and t < 2):
                pe.wait_ge(s_y, 2 * t - 2)
            for h in range(2):
                if first:
                    pe.wait_ge(s_ol, 2 * h + 2)
                for k in range(KD):
                    for m, w, fst in ((ML, OH, True), (MH, OL, False), (MH, OH, False)):
                        last = pe.matmul(PS[:, 4 * slot + h], m[:, slot, k], w[:, k, 512 * h:512 * h + 512],
                                         start=(k == 0 and fst), stop=(k == KD - 1 and m is MH and w is OH))
            last.then_inc(s_yp, 1)
        body(0, 0, P, True)
        body(1, 1, P, False)
        with pe.Fori(1, NT // 2) as i:
            body(2 * i, 0, P, False)
            body(2 * i + 1, 1, P, False)
        body(NT, 0, DEC, False)

    def sp_load_tile(sp, t, slot):
        for c in range(3):
            sp.dma_start(QKV[:, slot, H * c:H * c + H], scr["proj"][C_QKV + H * c:C_QKV + H * c + H, :, bass.ds(t * P, P)].rearrange("c p n -> p c n")).then_inc(s_in[slot], 16)
        sp.dma_start(GB[:, slot], scr["gcum"][bass.ds(t, 1)].rearrange("a h n -> a (h n)").to_broadcast([P, H * P])).then_inc(s_in[slot], 16)

    def sp_load_za(sp, t, slot):
        sp.dma_start(za[:, slot], scr["proj"][C_ZA:C_ZA + H, :, bass.ds(t * P, P)].rearrange("c p n -> p c n")).then_inc(s_za[slot], 16)

    def sp_store_u(sp, t):
        for g in range(2):
            after(sp, s_dv["out"], DVE_OUT, g, t, "u")
            sp.dma_start(scr["u"][4 * g:4 * g + 4, :, bass.ds(t * P, P)].rearrange("c p n -> p c n"), heads(UA[:, g])).then_inc(s_ua, 16)

    def sp_delta(sp):
        sp.dma_start(avec[:, 0], a["a_log"].to_broadcast([P, H])).then_inc(s_av, 16)
        sp.dma_start(avec[:, 1], a["dt_bias"].to_broadcast([P, H])).then_inc(s_av, 16)
        sp.dma_start(S[:, 1], a["state_delta"][0, 0].rearrange("h k v -> k h v")).then_inc(s_st, 16)
        sp.wait_ge(s_gT, 1)
        sp.dma_start(scr["gcum"].rearrange("t h n -> (t h) n"), gcT[:, :]).then_inc(s_gw, 16)
        sp.wait_ge(s_gw, 16)
        sp_load_tile(sp, 0, 0)
        sp_load_za(sp, 0, 0)
        sp_load_tile(sp, 1, 1)
        sp_load_za(sp, 1, 1)

        def body(t, slot, first):
            if not first:
                sp_store_u(sp, t - 1)
                if not (isinstance(t, int) and t == NT):
                    sp_load_za(sp, t + 1, 1 - slot)
            if isinstance(t, int) and t >= NT - 1:
                if t == NT - 1:
                    for g in range(2):
                        after(sp, s_dv["main"], DVE_MAIN, g, t, "s")
                    sp.dma_start(o["new_delta_prompt"][0, 0].rearrange("h k v -> k h v"), S[:, 0]).then_inc(s_so, 16)
                return
            for g in range(2):
                after(sp, s_pe["main"], PE_MAIN, g, t, "qs")
                after(sp, s_dv["prep"], DVE_PREP, g, t, "at")
            sp_load_tile(sp, t + 2, slot)
        run_tiles(sp, body)
        sp_store_u(sp, NT)
        sp.dma_start(o["new_delta_sample"][0, 0].rearrange("h k v -> k h v"), S[:, 1]).then_inc(s_so, 16)
        sp.wait_ge(s_so, 32)
        sp.wait_ge(s_ua, 32 * (NT + 1))

    def pe_prep(pe, t, slot, part, prev=True):
        q0 = {"q": 0, "k": H, "v": 2 * H}[part]
        for g in range(2):
            if part == "k":
                pe.wait_ge(s_in[slot], 64 * (t // 2 + 1) if isinstance(t, int) else 64 * fills(t, slot))
                if prev:
                    after(pe, s_dv["main"], DVE_MAIN, g, t - 2, "z")
                    after(pe, s_dv["out"], DVE_OUT, g, t - 2, "u")
            else:
                after(pe, s_ac["prep"], ACT_PREP, g, t, "k" if part == "q" else "q")
            for h in range(4):
                last = pe.transpose(hs(bank(g, 2), h), QKV[:, slot, q0 + 4 * g + h], ident)
            last.then_inc(s_pe["prep"][g], 1)

    def fills(t, slot):
        return (t - slot) // 2 + 1

    def pe_products(pe, t, slot, prev=True):
        for part, b, r0 in (("kk", 3, H), ("qk", 1, 0)):
            for g in range(2):
                if prev:
                    after(pe, s_dv["main"], DVE_MAIN, g, t - 1, "s")
                    after(pe, s_ac["main"], ACT_MAIN, g, t - 1, "o1")
                for h in range(4):
                    last = pe.matmul(hs(bank(g, b), h), QKV[:, slot, H + 4 * g + h], QKV[:, slot, r0 + 4 * g + h], start=True, stop=True)
                last.then_inc(s_pe["prep"][g], 1)

    def pe_out(pe, t):
        for g in range(2):
            after(pe, s_dv["out"], DVE_OUT, g, t, "on")
            for h in range(4):
                last = pe.transpose(hs(bank(g, 2), h), hs(ON[:, g], h), ident)
            last.then_inc(s_pe["out"][g], 1)

    def pe_delta(pe):
        def four(g, b, lhs, rhs, count):
            for h in range(4):
                last = pe.matmul(hs(bank(g, b), h), lhs(h), rhs(h), start=True, stop=True)
            if count:
                last.then_inc(s_pe["main"][g], 1)

        pe.wait_ge(s_gg, 1)
        pe.matmul(PS[:, 0, 0:72], cst[:, K_INC:K_INC + P], gat[:, :, :].rearrange("p t h -> p (t h)"), start=True, stop=True).then_inc(s_gp, 1)
        pe.matmul(PS[:, 1, 0:72], ones, gat[:, :, :].rearrange("p t h -> p (t h)"), start=True, stop=True).then_inc(s_gp, 1)
        pe.wait_ge(s_gx, 1)
        pe.transpose(PS[0:72, 2, 0:P], gtm[:, 0].rearrange("p t h -> p (t h)"), ident).then_inc(s_gp, 1)
        pe.wait_ge(s_gT, 1)
        pe.wait_ge(s_ge, 1)
        for part in "kqv":
            pe_prep(pe, 0, 0, part, prev=False)
        pe_products(pe, 0, 0, prev=False)

        def body(t, slot, first):
            last = isinstance(t, int) and t == NT
            st = 1 if last else 0
            for g in range(2):
                after(pe, s_dv["prep"], DVE_PREP, g, t, "nl")
                for h in range(4):
                    x = pe.transpose(hs(bank(g, 0), h), hs(NL[:, g], h), ident)
                x.then_inc(s_pe["main"][g], 1)
            for g in range(2):
                after(pe, s_dv["main"], DVE_MAIN, g, t, "q0")
                for h in range(4):
                    x = pe.transpose(hs(bank(g, 3), h), hs(QL[:, g, 0], h), ident)
                x.then_inc(s_pe["main"][g], 1)
            for l in range(1, NL7):
                for g in range(2):
                    after(pe, s_ac["main"], ACT_MAIN, g, t, f"x{l - 1}")
                    Xl = QL[:, g, 0] if l == 1 else X[:, g]
                    four(g, 0, lambda h: hs(NL[:, g], h), lambda h: hs(Xl, h), True)
                for g in range(2):
                    after(pe, s_dv["main"], DVE_MAIN, g, t, f"q{l}")
                    if l == 1:
                        after(pe, s_dv["prep"], DVE_PREP, g, t, "at")
                    if l < NL7 - 1:
                        four(g, 1, lambda h: hs(XT[:, g], h), lambda h: hs(QL[:, g, l], h), False)
                    four(g, 3, lambda h: hs(QL[:, g, l], h), lambda h: hs(XT[:, g], h), True)
                if l == 1 and not first:
                    pe_out(pe, t - 1)
                if not last and 2 <= l <= 4:
                    pe_prep(pe, t + 1, 1 - slot, "kqv"[l - 2], prev=not first)
            if last:
                pe.wait_ge(s_st, 16)
            for name, b, r0 in (("ks", 0, H), ("qs", 1, 0)):
                for g in range(2):
                    if not first and not last:
                        after(pe, s_dv["main"], DVE_MAIN, g, t - 1, "s")
                    four(g, b, lambda h: QKV[:, slot, r0 + 4 * g + h], lambda h: S[:, st, 4 * g + h], True)
            for g in range(2):
                after(pe, s_dv["main"], DVE_MAIN, g, t, "r")
                after(pe, s_ac["main"], ACT_MAIN, g, t, f"x{NL7 - 1}")
                if not last:
                    after(pe, s_dv["prep"], DVE_PREP, g, t + 1, "vn")
                else:
                    after(pe, s_dv["out"], DVE_OUT, g, t - 1, "u")
                four(g, 2, lambda h: hs(XT[:, g], h), lambda h: hs(RR[:, g], h), True)
            for g in range(2):
                after(pe, s_dv["main"], DVE_MAIN, g, t, "zd")
                four(g, 3, lambda h: hs(Kt[:, g, slot], h), lambda h: hs(ZD[:, g], h), True)
            for g in range(2):
                after(pe, s_dv["main"], DVE_MAIN, g, t, "z")
                four(g, 0, lambda h: hs(AT[:, g], h), lambda h: hs(Z[:, g], h), True)
            if not last:
                pe_products(pe, t + 1, 1 - slot)
            else:
                pe_out(pe, t)
        run_tiles(pe, body)

    def act_prep(act, t, slot, parts):
        for g in range(2):
            for part in parts:
                if part == "e":
                    after(act, s_dv["prep"], DVE_PREP, g, t, "sub")
                    act.activation(E[:, g], E[:, g], ACT.Exp).then_inc(s_ac["prep"][g], 1)
                    continue
                after(act, s_pe["prep"], PE_PREP, g, t, part)
                if part == "k":
                    act.activation(Kt[:, g, slot], bank(g, 2), ACT.Copy)
                act.activation((sq if part == "k" else sq2)[:, g], bank(g, 2), ACT.Square).then_inc(s_ac["prep"][g], 1)

    def act_delta(act):
        act.wait_ge(s_av, 32)
        act.wait_ge(s_gd1, 1)
        act.activation(tvs[:, :, 5], ba[:, :, 0:H], ACT.Sigmoid)
        act.activation(gtm[:, 1], gtm[:, 0], ACT.Abs)
        act.drain()
        act.activation(gtm[:, 1], gtm[:, 1], ACT.Exp, scale=-1.0)
        act.activation(avec[:, 0], avec[:, 0], ACT.Exp).then_inc(s_bs, 1)
        act.wait_ge(s_gd1, 2)
        act.activation(gtm[:, 3], gtm[:, 2], ACT.Ln).then_inc(s_bs, 1)
        act.wait_ge(s_gp, 2)
        act.activation(tvs[:, :, 0], PS[:, 0, 0:72].rearrange("p (t h) -> p t h", h=H), ACT.Copy)
        act.activation(gtm[:, 0], PS[:, 0, 0:72].rearrange("p (t h) -> p t h", h=H), ACT.Copy)
        act.activation(gtm[:, 1], PS[:, 1, 0:72].rearrange("p (t h) -> p t h", h=H), ACT.Copy)
        act.drain().then_inc(s_gx, 1)
        act.activation(tvs[:, :, 1], gtm[:, 0], ACT.Exp)
        act.activation(tvs[:, :, 4], gtm[:, 1], ACT.Exp)
        act.wait_ge(s_gd1, 3)
        act.activation(tvs[:, :, 3], gtm[:, 2], ACT.Exp)
        act.drain().then_inc(s_bs, 1)
        act.wait_ge(s_gp, 3)
        act.activation(gcT[:, :], PS[0:72, 2, 0:P], ACT.Copy).then_inc(s_gT, 1)
        act_prep(act, 0, 0, "kqe")

        def body(t, slot, first):
            last = isinstance(t, int) and t == NT
            if not first:
                for g in range(2):
                    after(act, s_dv["main"], DVE_MAIN, g, t - 1, "o2")
                    if isinstance(t, int) and t == 1 or not isinstance(t, int) or t > 1:
                        act.activation(sq[:, g], O2[:, g], ACT.Square).then_inc(s_ac["out"][g], 1)
            for l in range(NL7):
                for g in range(2):
                    after(act, s_pe["main"], PE_MAIN, g, t, f"x{l}")
                    if 0 < l < NL7 - 1:
                        act.activation(X[:, g], bank(g, 1), ACT.Copy)
                    act.activation(XT[:, g], bank(g, 3), ACT.Copy).then_inc(s_ac["main"][g], 1)
                if not last and 2 <= l <= 4:
                    act_prep(act, t + 1, 1 - slot, "kqe"[l - 2])
            for g in range(2):
                after(act, s_pe["main"], PE_MAIN, g, t, "qs")
                if not first:
                    after(act, s_dv["main"], DVE_MAIN, g, t - 1, "o2")
                for h in range(4):
                    x = act.activation(hs(O1[:, g], h), hs(bank(g, 1), h), ACT.Copy, scale=tv[:, slot, 1, 4 * g + h:4 * g + h + 1])
                x.then_inc(s_ac["main"][g], 1)
            if last:
                for g in range(2):
                    after(act, s_dv["main"], DVE_MAIN, g, t, "o2")
                    act.activation(sq[:, g], O2[:, g], ACT.Square).then_inc(s_ac["out"][g], 1)
        run_tiles(act, body)

    def pool_delta(pool):
        pool.memset(S[:, 0], 0.0)
        for g in range(2):
            for l in range(NL7):
                for h in range(4):
                    pool.tensor_copy(hs(QL[:, g, l], h), ident)
        pool.drain().then_inc(s_zero, 1)
        pool.wait_ge(s_ge, 1)

        def prep(t, slot, first=False):
            if not first:
                for g in range(2):
                    after(pool, s_dv["prep"], DVE_PREP, g, t - 1, "at")
            pool.tensor_copy(tv[:, slot].rearrange("p (a v) h -> p a v h", a=1), tvs[:, bass.ds(t, 1)]).then_inc(s_tv, 1)
            for g in range(2):
                after(pool, s_ac["prep"], ACT_PREP, g, t, "e")
                for out, m in ((Em, K_INC), (Es, K_STR)):
                    x = pool.tensor_tensor(heads(out[:, g]), heads(E[:, g]), cst[:, m:m + P].unsqueeze(1).to_broadcast([P, 4, P]), ALU.mult)
                x.then_inc(s_em[g], 1)
        prep(0, 0, True)

        def body(t, slot, first):
            if not (isinstance(t, int) and t == NT):
                prep(t + 1, 1 - slot)
        run_tiles(pool, body)

    def dve_sub(dve, t, slot, first=False):
        dve.wait_ge(s_tv, t + 1)
        dve.wait_ge(s_in[slot], 64 * fills(t, slot))
        for g in range(2):
            if not first:
                dve.wait_ge(s_em[g], t)
            for h in range(4):
                x = dve.tensor_scalar(hs(E[:, g], h), GB[:, slot, (4 * g + h) * P:(4 * g + h + 1) * P],
                                      tv[:, slot, 0, 4 * g + h:4 * g + h + 1], 0.0, ALU.subtract, ALU.min)
            x.then_inc(s_dv["prep"][g], 1)

    def dve_norm_a(dve, t):
        for g in range(2):
            after(dve, s_ac["prep"], ACT_PREP, g, t, "q")
            dve.tensor_reduce(dst[:, 0, g, 0], heads(sq[:, g]), AX.X, ALU.add)
            dve.tensor_reduce(dst[:, 0, g, 1], heads(sq2[:, g]), AX.X, ALU.add)
        dve.drain()
        dve.tensor_scalar(dst[:, 0], dst[:, 0], EPS, None, ALU.add)
        dve.drain()

    def dve_norm_b(dve):
        flat = [dst[:, n].rearrange("p a b c -> p (a b c)") for n in range(3)]
        rsqrt(dve, flat[1], flat[2], flat[0])

    def dve_norm_c(dve, t, slot):
        v = vec[:, slot]
        rk, rq, ss = dst[:, 1, :, 0], dst[:, 1, :, 1], dst[:, 0, :, 0]
        beta = tv[:, slot, 5].rearrange("p (g h) -> p g h", g=2)
        edl = tv[:, slot, 3].rearrange("p (g h) -> p g h", g=2)
        dve.tensor_tensor(v[:, 0], ss, rk, ALU.mult)
        dve.tensor_tensor(v[:, 1], rk, rk, ALU.mult)
        dve.tensor_scalar(v[:, 4], rq, 1.0, None, ALU.mult)
        dve.drain()
        dve.tensor_tensor(v[:, 1], v[:, 1], beta, ALU.mult)
        dve.drain()
        dve.tensor_scalar(v[:, 2], v[:, 1], -1.0, None, ALU.mult)
        dve.tensor_tensor(v[:, 3], v[:, 1], edl, ALU.mult)
        dve.drain()
        for g in range(2):
            after(dve, s_pe["prep"], PE_PREP, g, t, "v")
            dve.tensor_tensor(heads(Vn[:, g, slot]), heads(bank(g, 2)), wide(v[:, 0, g]), ALU.mult).then_inc(s_dv["prep"][g], 1)

    def dve_masked(dve, t, slot):
        for g in range(2):
            after(dve, s_pe["prep"], PE_PREP, g, t, "kk")
            dve.wait_ge(s_em[g], t + 1)
            for h in range(4):
                x = dve.scalar_tensor_tensor(hs(NL[:, g], h), hs(bank(g, 3), h), vec[:, slot, 2, g, h:h + 1], hs(Es[:, g], h), ALU.mult, ALU.mult)
            x.then_inc(s_dv["prep"][g], 1)
        for g in range(2):
            after(dve, s_pe["prep"], PE_PREP, g, t, "qk")
            dve.tensor_tensor(AT[:, g], bank(g, 1), Em[:, g], ALU.mult).then_inc(s_dv["prep"][g], 1)

    def dve_out(dve, t, slot, first=False):
        for g in range(2):
            after(dve, s_ac["out"], ACT_OUT, g, t, "sq")
            dve.tensor_reduce(ost[:, 0, g], heads(sq[:, g]), AX.X, ALU.add)
        rq = vec[:, slot, 4]
        dve.tensor_tensor(ost[:, 3], rq, rq, ALU.mult)
        dve.drain()
        dve.tensor_tensor(ost[:, 0], ost[:, 0], ost[:, 3], ALU.mult)
        dve.drain()
        dve.tensor_scalar(ost[:, 0], ost[:, 0], 1.0 / (HD * HD), EPS, ALU.mult, ALU.add)
        dve.drain()
        flat = [ost[:, n].rearrange("p a b -> p (a b)") for n in range(3)]
        rsqrt(dve, flat[1], flat[2], flat[0])
        dve.scalar_tensor_tensor(ost[:, 3], ost[:, 1], float(HD) ** -0.5, rq, ALU.mult, ALU.mult)
        dve.drain()
        for g in range(2):
            if not first:
                after(dve, s_pe["out"], PE_OUT, g, t - 1, "on")
            dve.tensor_tensor(heads(ON[:, g]), heads(O2[:, g]), wide(ost[:, 3, g]), ALU.mult).then_inc(s_dv["out"][g], 1)

    def dve_u(dve, t, slot, first=False):
        dve.wait_ge(s_za[slot], 16 * fills(t, slot))
        if not first:
            dve.wait_ge(s_ua, 32 * t)
        for g in range(2):
            after(dve, s_pe["out"], PE_OUT, g, t, "on")
            dve.scalar_tensor_tensor(UA[:, g], bank(g, 2), colB[:, B_DN:B_DN + 1], za[:, slot, 4 * g:4 * g + 4].rearrange("p h n -> p (h n)"),
                                     ALU.mult, ALU.mult).then_inc(s_dv["out"][g], 1)

    def dve_delta(dve):
        dve.wait_ge(s_av, 32)
        x0, t1, u, ln = (gtm[:, n] for n in range(4))
        dve.tensor_tensor(x0, ba[:, :, H:BA], avec[:, 1:2].to_broadcast([P, NT + 1, H]), ALU.add)
        dve.drain().then_inc(s_gd1, 1)
        dve.wait_ge(s_bs, 1)
        dve.tensor_scalar(u, t1, 1.0, None, ALU.add)
        dve.drain().then_inc(s_gd1, 1)
        dve.tensor_scalar(gat[:, :, :], u, -1.0, None, ALU.add)
        dve.drain()
        dve.tensor_scalar(dst_m(0), gat[:, :, :], 0.0, None, ALU.is_equal)
        dve.drain()
        dve.tensor_tensor(gat[:, :, :], gat[:, :, :], dst_m(0), ALU.add)
        dve.drain()
        dve.reciprocal(dst_m(1), gat[:, :, :])
        dve.wait_ge(s_bs, 2)
        dve.drain()
        dve.tensor_tensor(dst_m(1), dst_m(1), ln, ALU.mult)
        dve.drain()
        dve.tensor_tensor(dst_m(1), dst_m(1), dst_m(0), ALU.add)
        dve.drain()
        dve.tensor_tensor(dst_m(1), dst_m(1), t1, ALU.mult)
        dve.drain()
        dve.scalar_tensor_tensor(gat[:, :, :], x0, 0.0, dst_m(1), ALU.max, ALU.add)
        dve.drain()
        dve.scalar_tensor_tensor(gat[:, :, :], gat[:, :, :], -1.0, avec[:, 0:1].to_broadcast([P, NT + 1, H]), ALU.mult, ALU.mult)
        dve.drain()
        dve.memset(gat[DEC:2 * DEC, NT], 0.0)
        dve.memset(gat[2 * DEC:P, NT], 0.0)
        dve.drain().then_inc(s_gg, 1)
        dve.wait_ge(s_gx, 1)
        dve.tensor_tensor(gtm[:, 2], gtm[:, 1], gtm[:, 0], ALU.subtract)
        dve.drain().then_inc(s_gd1, 1)
        dve.wait_ge(s_bs, 3)
        dve.tensor_scalar(tvs[:, :, 2], tvs[:, :, 1], -1.0, None, ALU.mult)
        dve.drain().then_inc(s_ge, 1)
        dve_sub(dve, 0, 0, True)
        dve_norm_a(dve, 0)
        dve_norm_b(dve)
        dve_norm_c(dve, 0, 0)
        dve_masked(dve, 0, 0)
        dve.wait_ge(s_zero, 1)

        def body(t, slot, first):
            last = isinstance(t, int) and t == NT
            st = 1 if last else 0
            if not first:
                dve_out(dve, t - 1, 1 - slot, first=(isinstance(t, int) and t == 1))
            for l in range(NL7):
                for g in range(2):
                    after(dve, s_pe["main"], PE_MAIN, g, t, "l" if l == 0 else f"p{l}")
                    dve.sem_inc(s_seen, 1)
                    for h in range(4):
                        x = dve.copy_predicated(hs(QL[:, g, l], h), cst[:, K_LEV + l * P:K_LEV + (l + 1) * P].bitcast(I32), hs(bank(g, 0), h))
                    x.then_inc(s_dv["main"][g], 1)
                if l == 1 and not first:
                    dve_u(dve, t - 1, 1 - slot, first=(isinstance(t, int) and t == 1))
                if last:
                    continue
                if l == 0:
                    dve_sub(dve, t + 1, 1 - slot)
                if l == 4:
                    dve_norm_a(dve, t + 1)
                    dve_norm_b(dve)
                    dve_norm_c(dve, t + 1, 1 - slot)
            v = tv[:, slot]
            for g in range(2):
                after(dve, s_pe["main"], PE_MAIN, g, t, "ks")
                for h in range(4):
                    x = dve.scalar_tensor_tensor(hs(RR[:, g], h), hs(bank(g, 0), h), v[:, 2, 4 * g + h:4 * g + h + 1], hs(Vn[:, g, slot], h), ALU.mult, ALU.add)
                x.then_inc(s_dv["main"][g], 1)
            for g in range(2):
                after(dve, s_pe["main"], PE_MAIN, g, t, "y")
                dve.tensor_tensor(heads(ZD[:, g]), heads(bank(g, 2)), wide(vec[:, slot, 3, g]), ALU.mult).then_inc(s_dv["main"][g], 1)
                dve.tensor_tensor(heads(Z[:, g]), heads(bank(g, 2)), wide(vec[:, slot, 1, g]), ALU.mult).then_inc(s_dv["main"][g], 1)
            for g in range(2):
                after(dve, s_pe["main"], PE_MAIN, g, t, "st")
                for h in range(4):
                    x = dve.scalar_tensor_tensor(S[:, st, 4 * g + h], S[:, st, 4 * g + h], v[:, 4, 4 * g + h:4 * g + h + 1], hs(bank(g, 3), h), ALU.mult, ALU.add)
                x.then_inc(s_dv["main"][g], 1)
            for g in range(2):
                after(dve, s_pe["main"], PE_MAIN, g, t, "av")
                after(dve, s_ac["main"], ACT_MAIN, g, t, "o1")
                dve.tensor_tensor(O2[:, g], bank(g, 0), O1[:, g], ALU.add).then_inc(s_dv["main"][g], 1)
            if not last:
                dve_masked(dve, t + 1, 1 - slot)
            else:
                dve_out(dve, t, slot)
                dve_u(dve, t, slot)
        run_tiles(dve, body)

    def dst_m(n):
        return UA[:, n, 0:72].rearrange("p (t h) -> p t h", h=H)

    block = ctx.enter_context(nc.Block())

    def sp_pass01(sp):
        for l3 in range(3):
            for s in range(4):
                l = 4 * l3 + s
                if l3:
                    sp.wait_ge(s_adam, l - 3)
                sp.dma_start(Wraw[:, s], a["w_ada"][0, :, l * 256:(l + 1) * 256].rearrange("(k p) n -> p k n", p=P)).then_inc(s_ada[s], 16)
        sp.sem_inc(s_store[0], 16)
        sp.sem_inc(s_store[1], 16)
        with sp.Fori(0, (NCHUNK - 1) // 2) as it:
            for c in range(2):
                sp.wait_ge(s_stage, 2 * it + c + 2)
                sp.dma_start(scr["proj"][bass.ds(2 * it + c, 1)].rearrange("a p n -> (a p) n"), stage[:, c]).then_inc(s_store[c], 16)
        sp.wait_ge(s_stage, NCHUNK + 1)
        sp.dma_start(scr["proj"][C_MISC, 0:MISC], stage[0:MISC, 0]).then_inc(s_store[0], 16)
        sp.wait_ge(s_edc, 2)
        for i, name in enumerate(("new_conv_prompt", "new_conv_sample")):
            sp.dma_start(o[name][0, 0].rearrange("i (c p) -> (i c) p", p=P), edT[0:72, i]).then_inc(s_out, 16)
        sp.wait_ge(s_store[0], 16 * 38)
        sp.wait_ge(s_store[1], 16 * 37)

    @block.sync
    def _(sp):
        sp_pass01(sp)
        meet(sp, 1)
        sp_latents(sp)
        meet(sp, 2)
        sp_attention(sp)
        meet(sp, 3)
        sp_delta(sp)
        meet(sp, 4)
        sp_out(sp)
        sp_y(sp)
        sp.wait_ge(s_out, 16 * 2)

    def pool_pass01(pool):
        def load(l, s, col):
            pool.wait_ge(s_wlo, l + 1)
            pool.dma_start(Wraw[:, s], a["w_in"][0, :, bass.ds(col + 256 * s, 256)].rearrange("(k p) n -> p k n", p=P)).then_inc(s_raw[s], 16)

        pool.sem_inc(s_edge, 2)
        pool.wait_ge(s_colc, 2)
        pool.wait_ge(s_adam, 12)
        load(0, 0, 0)
        load(1, 1, 0)
        pool.wait_ge(s_hl, NG)
        pool.memset(stage[:, 0, TOK:TPAD], 0.0)
        pool.memset(stage[:, 1, TOK:TPAD], 0.0)
        pool.memset(Xr[:, 0, 0:3], 0.0)
        pool.memset(Xr[:, 1, 0:3], 0.0)
        pool.drain().then_inc(s_pad, 1)
        taps = colA[:, A_CONV:A_CONV + 96].rearrange("p (i c) -> p i c", c=NCV)
        state = colB[:, B_STATE:B_STATE + 72].rearrange("p (i c) -> p i c", c=NCV)
        kept = edge.rearrange("p (s i c) -> p s i c", s=2, c=NCV)
        with pool.Fori(0, NCV // 4) as it:
            for c in range(4):
                n = 4 * it + c
                if c % 2 == 0:
                    load(2 * it + c // 2 + 2, c // 2, 512 * it + 512)
                pool.wait_ge(s_conv, n + 1)
                pool.tensor_copy(wcv[:, c % 2].rearrange("p (i a) -> p i a", a=1), taps[:, :, bass.ds(n, 1)])
                pool.tensor_copy(Xr[:, c % 2, 3 + SEQ:6 + SEQ].rearrange("p (i a) -> p i a", a=1), state[:, :, bass.ds(n, 1)])
                pool.drain().then_inc(s_pad, 1)
                pool.wait_ge(s_evac, n + 3)
                pool.tensor_copy(kept[:, 0, :, bass.ds(n, 1)], Xr[:, c % 2, SEQ:SEQ + 3].rearrange("p (i a) -> p i a", a=1))
                pool.tensor_copy(kept[:, 1, :, bass.ds(n, 1)], Xr[:, c % 2, XW - 3:XW].rearrange("p (i a) -> p i a", a=1))
                pool.drain().then_inc(s_edge, 1)
        done = NCV // 4 + 1
        for iters, col in ((1, CONV_CH + 512), (4, COL_Q), (6, COL_ZB)):
            with pool.Fori(0, iters) as it:
                for s in range(2):
                    load(2 * it + 2 * done + s, s, 512 * it + col)
            done += iters
        pool.wait_ge(s_wlo, 2 * done + 1)
        for c, lo, n, landed in ((0, COL_BA, BA, s_misc), (BA, COL_KR, ROPE, s_raw[0])):
            pool.dma_start(Wraw[:, 0, :, c:c + n], a["w_in"][0, :, lo:lo + n].rearrange("(k p) n -> p k n", p=P)).then_inc(landed, 16)
            pool.wait_ge(s_misc, 16)

    @block.gpsimd
    def _(pool):
        pool_pass01(pool)
        meet(pool, 1)
        meet(pool, 2)
        pool_attention(pool)
        meet(pool, 3)
        pool_delta(pool)
        meet(pool, 4)

    def act_pass01(act):
        act.dma_start(cst[:, :], a["shape_constants"]).then_inc(s_cst, 16)
        act.dma_start(rows[0:96, 0], a["w_conv"][0].rearrange("i (c p) -> (i c) p", p=P)).then_inc(s_rows, 16)
        act.dma_start(rows[96:104, 0], a["norm_gain"][0].rearrange("(c p) -> c p", p=P)).then_inc(s_rows, 16)
        act.dma_start(rows[104:112, 0], a["c_prompt"][0].rearrange("(c p) -> c p", p=P)).then_inc(s_rows, 16)
        act.dma_start(rows[112:120, 0], a["c_sample"][0].rearrange("(c p) -> c p", p=P)).then_inc(s_rows, 16)
        act.dma_start(rows[0:72, 1], a["state_conv"][0, 0].rearrange("i (c p) -> (i c) p", p=P)).then_inc(s_rows, 16)
        act.dma_start(rows[72:96, 1], a["b_ada"][0].rearrange("(c p) -> c p", p=P)).then_inc(s_rows, 16)
        for i, name in enumerate(("dn_out_norm", "q_nope_norm", "k_nope_norm")):
            act.dma_start(rows[96 + i:97 + i, 1], a[name]).then_inc(s_rows, 16)
        for i in range(2):
            act.dma_start(R[:, 4 * i:4 * i + 4], a["x_prompt"][0, 512 * i:512 * i + 512].rearrange("(t p) n -> p t n", p=P)).then_inc(s_x[i], 16)
        act.dma_start(R[0:DEC, 8], a["x_sample"][0]).then_inc(s_x[2], 16)
        act.sem_inc(s_evac, 2)
        act.sem_inc(s_stage, 1)
        act.wait_ge(s_cols, 2)
        act.activation(colA[:, :], PS[:, 0, 0:120], ACT.Copy).then_inc(s_colc, 1)
        act.activation(colB[:, :], PS[:, 1, 0:99], ACT.Copy).then_inc(s_colc, 1)
        act.wait_ge(s_xst, 1)
        for t in range(9):
            rows_t = P if t < 8 else DEC
            act.wait_ge(s_x[t // 4], 16)
            act.activation(hf[0:rows_t].rearrange("p a b -> p (a b)"), R[0:rows_t, t], ACT.Square, accum_out=xst[0:rows_t, 0, t:t + 1]).then_inc(s_xss, 1)
            act.drain()
        for n in range(NG):
            g, k, w = x_group(n)
            act.wait_ge(s_hf, n + 1)
            act.activation(HH[:, k, 512 * g:512 * g + w], hf[:, n % 2, 0:w], ACT.Copy).then_inc(s_hh, 1)
        def split_hi(s, l, fill):
            act.wait_ge(s_raw[s], fill)
            act.wait_ge(s_chunk, 2 * l + 2)
            act.activation(WH[:, s], Wraw[:, s], ACT.Copy).then_inc(s_whi, 1)

        split_hi(0, 0, 16)
        base = 0
        for iters, _, kind in SEGMENTS:
            with act.Fori(0, iters) as it:
                for c in range(4):
                    n = 4 * it + 4 * base + c
                    if c % 2 == 0:
                        split_hi(1 - c // 2, 2 * (it + base) + c // 2 + 1, 16 * (it + base + c // 2 + 1))
                    act.wait_ge(s_chunk, n + 1 + 4)
                    b3 = PS[:, 3 * (c % 2):3 * (c % 2) + 3, 0:TB]
                    st = stage[:, c % 2, 0:TOK]
                    if kind == "conv":
                        act.wait_ge(s_pad, n + 2)
                        act.wait_ge(s_edge, n + 1)
                        act.activation(Xr[:, c % 2, 3:3 + 2 * TB].rearrange("p (b n) -> p b n", b=2), b3[:, 0:2], ACT.Copy)
                        act.activation(Xr[:, c % 2, 3 + 2 * TB:3 + SEQ], PS[:, 3 * (c % 2) + 2, 0:SEQ - 2 * TB], ACT.Copy)
                        act.activation(Xr[:, c % 2, 6 + SEQ:XW], PS[:, 3 * (c % 2) + 2, SEQ - 2 * TB:TB], ACT.Copy).then_inc(s_evac, 1)
                        act.wait_ge(s_conv, n + 3)
                        act.wait_ge(s_store[c % 2], 16 * (2 * (it + base) + c // 2 + 1))
                        act.activation(stage[:, c % 2, 0:SEQ], cv[:, 0:SEQ], ACT.Silu)
                        act.activation(stage[:, c % 2, SEQ:TOK], cv[:, SEQ + 3:SEQ + 3 + DEC], ACT.Silu).then_inc(s_stage, 1)
                    else:
                        act.wait_ge(s_store[c % 2], 16 * (2 * (it + base) + c // 2 + 1))
                        f = {"silu": ACT.Silu, "copy": ACT.Copy, "sigmoid": ACT.Sigmoid}[kind]
                        act.activation(st.rearrange("p (b n) -> p b n", b=3), b3, f).then_inc(s_stage, 1)
                        act.drain().then_inc(s_evac, 1)
            base += iters
        act.wait_ge(s_chunk, 4 * base + 5)
        act.wait_ge(s_store[0], 16 * (2 * base + 1))
        act.activation(stage[0:MISC, 0, 0:TOK].rearrange("p (b n) -> p b n", b=3), PS[0:MISC, 0:3, 0:TB], ACT.Copy).then_inc(s_stage, 1)
        for i in range(2):
            act.wait_ge(s_edT, i + 1)
            act.activation(edT[0:72, i], PS[0:72, 6 + i, 0:P], ACT.Copy).then_inc(s_edc, 1)

    @block.scalar
    def _(act):
        act_pass01(act)
        meet(act, 1)
        act_latents(act)
        meet(act, 2)
        act_attention(act)
        meet(act, 3)
        act_delta(act)
        meet(act, 4)
        act_out(act)
        act_y(act)

    def pe_chunk(pe, s, c, psum, lo=0, m=P):
        for k in range(KD):
            for w, h, first in ((WL, HH, True), (WH, HL, False), (WH, HH, False)):
                for b in range(NB):
                    last = pe.matmul(PS[0:m, psum + b, 0:TB], w[:, s, k, c * P:c * P + m], h[:, k, b * TB:(b + 1) * TB],
                                     start=(k == 0 and first), stop=(k == KD - 1 and h is HH and not first))
        last.then_inc(s_chunk, 1)

    def pe_pass01(pe):
        pe.wait_ge(s_cst, 16)
        pe.wait_ge(s_rows, 16 * 9)
        pe.transpose(PS[:, 0, 0:120], rows[0:120, 0], ident[0:120, 0:120]).then_inc(s_cols, 1)
        pe.transpose(PS[:, 1, 0:99], rows[0:99, 1], ident[0:99, 0:99]).then_inc(s_cols, 1)
        pe.wait_ge(s_colc, 2)
        for l in range(12):
            pe.wait_ge(s_ada[l % 4], 16 * (l // 4 + 1))
            for j in range(2):
                for k in range(KD):
                    last = pe.matmul(PS[:, 2, 4 * l + 2 * j:4 * l + 2 * j + 2], Wraw[:, l % 4, k, j * P:(j + 1) * P],
                                     colA[:, A_C + k:A_C + 16:8], start=(k == 0), stop=(k == KD - 1))
            last.then_inc(s_adam, 1)
        for n in range(NG):
            g, k, w = x_group(n)
            if k == 0:
                pe.wait_ge(s_xn, min(4 * g + 4, 9))
            if n >= 2:
                pe.wait_ge(s_hf, n - 1)
            for t in range(4 if g < 2 else 1):
                r = P if g < 2 else DEC
                last = pe.transpose(PS[:, 3 + n % 2, t * P:t * P + r], R[0:r, 4 * g + t, k * P:(k + 1) * P], ident[0:r, 0:r])
            last.then_inc(s_xT, 1)
        pe.wait_ge(s_hl, NG)
        pe.wait_ge(s_hh, NG)
        pe.sem_inc(s_chunk, 4)
        with pe.Fori(0, 18) as it:
            for c in range(4):
                if c % 2 == 0:
                    pe.wait_ge(s_wlo, 2 * it + c // 2 + 3)
                pe.wait_ge(s_evac, 4 * it + c + 1)
                pe_chunk(pe, c // 2, c % 2, 3 * (c % 2))
        pe.wait_ge(s_wlo, 39)
        pe.wait_ge(s_evac, 73)
        pe_chunk(pe, 0, 0, 0, m=MISC)
        pe.wait_ge(s_edge, NCV + 2)
        for i in range(2):
            pe.transpose(PS[0:72, 6 + i, 0:P], edge[:, 72 * i:72 * i + 72], ident).then_inc(s_edT, 1)

    @block.tensor
    def _(pe):
        pe_pass01(pe)
        meet(pe, 1)
        pe_latents(pe)
        meet(pe, 2)
        pe_attention(pe)
        meet(pe, 3)
        pe_delta(pe)
        meet(pe, 4)
        pe_branches(pe)
        pe_y(pe)

    def dve_pass01(dve):
        dve.memset(xst[:, :, :], 1.0).then_inc(s_xst, 1)
        dve.wait_ge(s_colc, 2)
        dve.wait_ge(s_xss, 9)
        ss, r, tmp = xst[:, 0], xst[:, 1], xst[:, 2]
        dve.tensor_scalar(ss, ss, 1.0 / D, EPS, ALU.mult, ALU.add)
        dve.drain()
        rsqrt(dve, r, tmp, ss)
        for t in range(9):
            n = P if t < 8 else DEC
            dve.tensor_scalar(R[0:n, t], R[0:n, t], r[0:n, t:t + 1], None, ALU.mult).then_inc(s_xn, 1)
        dve.wait_ge(s_adam, 12)
        dve.tensor_tensor(mod[:, :, :], PS[:, 2, 0:48].rearrange("p (j s) -> p j s", s=2),
                          colB[:, B_ADA:B_ADA + 24].unsqueeze(2).to_broadcast([P, 24, 2]), ALU.add)
        dve.drain()
        dve.scalar_tensor_tensor(G[:, :, :], mod[:, 8:16, :], 1.0,
                                 colA[:, A_GAIN:A_GAIN + 8].unsqueeze(2).to_broadcast([P, 8, 2]), ALU.add, ALU.mult)
        dve.drain()
        for n in range(NG):
            g, k, w = x_group(n)
            s = g // 2
            dve.wait_ge(s_xT, n + 1)
            if n >= 2:
                dve.wait_ge(s_hh, n - 1)
            dve.tensor_scalar(hf[:, n % 2, 0:w], PS[:, 3 + n % 2, 0:w], G[:, k, s:s + 1], mod[:, k, s:s + 1],
                              ALU.mult, ALU.add).then_inc(s_hf, 1)
            dve.wait_ge(s_hh, n + 1)
            dve.tensor_tensor(HL[:, k, 512 * g:512 * g + w], hf[:, n % 2, 0:w], HH[:, k, 512 * g:512 * g + w].bitcast(F32), ALU.subtract).then_inc(s_hl, 1)
        dve.sem_inc(s_wlo, 2)
        dve.sem_inc(s_conv, 2)

        def split_lo(s, l):
            dve.wait_ge(s_whi, l + 1)
            dve.tensor_tensor(WL[:, s], Wraw[:, s], WH[:, s].bitcast(F32), ALU.subtract).then_inc(s_wlo, 1)

        split_lo(0, 0)

        base = 0
        for iters, _, kind in SEGMENTS:
            with dve.Fori(0, iters) as it:
                for c in range(4):
                    n = 4 * it + 4 * base + c
                    if c % 2 == 0:
                        split_lo(1 - c // 2, 2 * (it + base) + c // 2 + 1)
                    if kind == "conv":
                        x = Xr[:, c % 2]
                        wt = wcv[:, c % 2]
                        dve.wait_ge(s_evac, n + 3)
                        dve.wait_ge(s_stage, n + 1)
                        dve.tensor_scalar(cv, x[:, 0:XW - 3], wt[:, 0:1], None, ALU.mult)
                        dve.drain()
                        for i in range(1, CONV):
                            last = dve.scalar_tensor_tensor(cv, x[:, i:i + XW - 3], wt[:, i:i + 1], cv, ALU.mult, ALU.add)
                            if i < CONV - 1:
                                dve.drain()
                        last.then_inc(s_conv, 1)
            base += iters

    @block.vector
    def _(dve):
        dve_pass01(dve)
        meet(dve, 1)
        dve_latents(dve)
        meet(dve, 2)
        dve_attention(dve)
        meet(dve, 3)
        dve_delta(dve)
        meet(dve, 4)
        dve_branches(dve)
        dve_y(dve)


INPUTS = ["x_prompt", "x_sample", "c_prompt", "c_sample", "cache_ckv", "cache_krope", "state_delta", "state_conv",
          "norm_gain", "w_ada", "b_ada", "w_in", "w_conv", "a_log", "dt_bias", "dn_out_norm", "q_nope_norm",
          "q_rope_norm", "k_nope_norm", "k_rope_norm", "kv_norm", "w_uk", "w_uv", "w_o_dn", "w_o_mla", "w_out"]
OUTPUTS = [("y_prompt", (1, SEQ, D)), ("y_sample", (1, DEC, D)),
           ("new_ckv_prompt", (1, 1, SEQ, KV)), ("new_krope_prompt", (1, 1, SEQ, ROPE)),
           ("new_delta_prompt", (1, 1, H, HD, HD)), ("new_conv_prompt", (1, 1, CONV - 1, CONV_CH)),
           ("new_ckv_sample", (1, 1, DEC, KV)), ("new_krope_sample", (1, 1, DEC, ROPE)),
           ("new_delta_sample", (1, 1, H, HD, HD)), ("new_conv_sample", (1, 1, CONV - 1, CONV_CH))]


def kernel(**inputs):
    from concourse import bacc
    from concourse.bass_utils import run_bass_kernel_spmd

    nc = bacc.Bacc("TRN2", target_bir_lowering=False, num_devices=1)
    arrays = {name: np.ascontiguousarray(inputs[name]) for name in INPUTS}
    arrays["shape_constants"] = shape_constants()
    arrays["rotary_tables"] = rotary_tables()
    a = {n: nc.dram_tensor(f"in_{n}", v.shape, F32, kind="ExternalInput").ap() for n, v in arrays.items()}
    o = {n: nc.dram_tensor(f"out_{n}", shape, F32, kind="ExternalOutput").ap() for n, shape in OUTPUTS}
    kind = "Internal"
    scr = {n: nc.dram_tensor(f"scratch_{n}", shape, F32, kind=kind).ap()
           for n, shape in (("proj", (NCHUNK, P, TPAD)), ("u", (2 * H, P, TPAD)), ("gcum", (NT + 1, H, P)))}
    with ExitStack() as ctx:
        build(nc, a, o, scr, ctx)
    r = run_bass_kernel_spmd(nc, [{f"in_{n}": v for n, v in arrays.items()}], core_ids=[0])
    return tuple(r.results[0][f"out_{n}"] for n, _ in OUTPUTS)
```

```python
from contextlib import ExitStack

import numpy as np

import concourse.bass as bass
import concourse.mybir as mybir

F32 = mybir.dt.float32
F32R = mybir.dt.float32r
I32 = mybir.dt.int32
ACT = mybir.ActivationFunctionType
ALU = mybir.AluOpType
AX = mybir.AxisListType

P = 128
D = 1024
KD = D // P
SEQ, DEC, PAST = 1024, 32, 256
CHUNK = 64
H = 8
HD = 128
ROPE = 64
KV = 512
KR = KV // P
QH = HD + ROPE
CONV = 4
EPS = 1e-6
NT = SEQ // P
TOK = SEQ + DEC
TPAD = SEQ + P
NB = 3
TB = TOK // NB
CONV_CH = 3 * H * HD
NCV = CONV_CH // P

COL_BA = CONV_CH + H * HD
COL_Q = COL_BA + 2 * H
COL_KR = COL_Q + H * QH + KV
COL_ZB = COL_KR + ROPE
C_QKV, C_ZA, C_Q, C_CKV, C_ZB, C_GA, C_GB, C_MISC = 0, 24, 32, 44, 48, 56, 64, 72
NCHUNK = 73
BA = 2 * H
MISC = BA + ROPE

LEVELS = [1, 2, 4, 8, 16, 32, 64]
K_ID, K_ONE, K_INC, K_STR, K_LEV = 0, P, 2 * P, 3 * P, 4 * P
NCST = K_LEV + len(LEVELS) * P
A_CONV, A_GAIN, A_C = 0, 96, 104
B_STATE, B_ADA, B_DN, B_QN, B_KN = 0, 72, 96, 97, 98


def shape_constants():
    i, j = np.indices((P, P))
    masks = [i == j, np.ones((P, P)), i <= j, i < j]
    masks += [(i // (2 * s) == j // (2 * s)) & (i % (2 * s) >= s) & (j % (2 * s) < s) for s in LEVELS]
    return np.concatenate([m.astype(np.float32) for m in masks], axis=1)


def rotary_tables():
    half = ROPE // 2
    inv = np.float32(10000.0) ** (-np.arange(half, dtype=np.float32) / np.float32(half))
    pos = np.concatenate([np.arange(SEQ), PAST + np.arange(P)]).astype(np.float32)
    ang = pos[:, None] * inv.astype(np.float32)
    return np.concatenate([np.cos(ang), np.sin(ang)], axis=1).astype(np.float32)


def rsqrt(dve, out, tmp, x):
    dve.tensor_scalar(tmp.bitcast(I32), x.bitcast(I32), 1, None, ALU.arith_shift_right)
    dve.drain()
    dve.tensor_scalar(out.bitcast(I32), tmp.bitcast(I32), -1.0, float(0x5F3759DF), ALU.mult, ALU.add)
    dve.drain()
    for _ in range(3):
        dve.tensor_tensor(tmp, out, out, ALU.mult)
        dve.drain()
        dve.scalar_tensor_tensor(tmp, tmp, -0.5, x, ALU.mult, ALU.mult)
        dve.drain()
        dve.scalar_tensor_tensor(out, tmp, 1.5, out, ALU.add, ALU.mult)
        dve.drain()


def build(nc, a, o, scr, ctx):
    def sb(stack, name, shape, dt=F32):
        return stack.enter_context(nc.sbuf_tensor(name, shape, dt))

    def sem(name):
        return ctx.enter_context(nc.semaphore(name))

    PS = ctx.enter_context(nc.psum_tensor("PS", [P, 8, 512], F32))
    cst = sb(ctx, "cst", [P, NCST])
    ident = cst[:, K_ID:K_ID + P]
    ones = cst[:, K_ONE:K_ONE + P]
    colA = sb(ctx, "colA", [P, 120])
    colB = sb(ctx, "colB", [P, 99])
    mod = sb(ctx, "mod", [P, 24, 2])
    ba = sb(ctx, "ba", [P, NT + 1, BA])

    p1 = ExitStack()
    HH = sb(p1, "HH", [P, KD, TOK], F32R)
    HL = sb(p1, "HL", [P, KD, TOK], F32R)
    Wraw = sb(p1, "Wraw", [P, 4, KD, 256])
    WH = sb(p1, "WH", [P, 2, KD, 256], F32R)
    WL = sb(p1, "WL", [P, 2, KD, 256], F32R)
    R = sb(p1, "R", [P, 9, D])
    rows = sb(p1, "rows", [P, 2, P])
    NHF = 4
    hf = sb(p1, "hf", [P, NHF, 512])
    modr = sb(p1, "modr", [2, 2, 512])
    G = sb(p1, "G", [P, KD, 2])
    xst = sb(p1, "xst", [P, 3, 9])
    Rf = R[:, :, :].rearrange("p a b -> p (a b)")
    XW = 3 + SEQ + 3 + DEC
    Xr = Rf[:, 0:2 * XW].rearrange("p (s n) -> p s n", s=2)
    cvo = 2 * XW
    cv = Rf[:, cvo:cvo + XW - 3]
    sto = cvo + XW - 3
    stage = Rf[:, sto:sto + 2 * TPAD].rearrange("p (s n) -> p s n", s=2)
    wco = sto + 2 * TPAD
    wcv = Rf[:, wco:wco + 8].rearrange("p (s n) -> p s n", s=2)
    edo = wco + 8
    edge = Rf[:, edo:edo + 144]
    edT = Rf[:, edo + 144:edo + 144 + 2 * P].rearrange("p (s n) -> p s n", s=2)
    assert edo + 144 + 2 * P <= 9 * D
    p1.close()

    s_cst = sem("constants_loaded")
    s_rows = sem("vector_rows_loaded")
    s_cols = sem("vectors_transposed")
    s_colc = sem("vector_columns_ready")
    s_x = [sem(f"x_loaded_{i}") for i in range(3)]
    s_ada = [sem(f"w_ada_loaded_{i}") for i in range(4)]
    s_adam = sem("w_ada_chunk_used")
    s_modr = sem("modulation_rows_ready")
    s_modT = sem("modulation_rows_transposed")
    s_vecs = sem("vector_rows_of_pool_loaded")
    s_mod = sem("modulation_ready")
    s_xst = sem("x_statistics_cleared")
    s_xss = sem("x_squares_summed")
    s_xn = sem("x_normalised")
    s_xT = sem("x_transposed")
    s_hf = sem("h_float_ready")
    s_hl = sem("h_lo_ready")
    s_raw = [sem(f"w_loaded_{i}") for i in range(2)]
    s_misc = sem("w_beta_alpha_loaded")
    s_whi = sem("w_hi_ready")
    s_wlo = sem("w_lo_ready")
    s_chunk = sem("chunk_in_psum")
    s_evac = sem("chunk_evacuated")
    s_pad = sem("conv_edges_ready")
    s_edge = sem("edges_kept")
    s_conv = sem("chunk_convolved")
    s_stage = sem("chunk_staged")
    s_store = [sem(f"chunk_stored_{i}") for i in range(2)]
    s_edT = sem("edges_transposed")
    s_edc = sem("edge_rows_ready")
    s_out = sem("outputs_stored")

    def ada_slot(l):
        return l % 4 if l < 8 else 2 + l % 2

    def ada_before(l):
        return max(m for m in range(l) if ada_slot(m) == ada_slot(l))

    def ada_fill(l):
        return sum(ada_slot(m) == ada_slot(l) for m in range(l + 1))

    NG = 2 * KD + KD

    def x_group(n):
        g, k = divmod(n, KD)
        return g, k, (512 if g < 2 else DEC)

    SEGMENTS = [(NCV // 4, 0, "conv"), (2, CONV_CH, "silu"), (4, COL_Q, "copy"), (2, COL_ZB, "silu"),
                (4, COL_ZB + D, "sigmoid")]

    NKT = NT + PAST // P + 1
    KEYS = NKT * P
    SCALE = float(QH) ** -0.5
    p2 = ExitStack()
    rotk = sb(p2, "rotk", [P, NT + 1, 2, ROPE])
    kT = sb(p2, "kT", [P, H, KEYS])
    V = sb(p2, "V", [P, NKT, H * HD])
    krH = sb(p2, "krH", [P, KEYS], F32R)
    krL = sb(p2, "krL", [P, KEYS], F32R)
    rotq = sb(p2, "rotq", [P, NT + 1, 2, ROPE])
    p2a = ExitStack()
    UH = sb(p2a, "UH", [P, 2, KR, H * HD], F32R)
    UL = sb(p2a, "UL", [P, 2, KR, H * HD], F32R)
    LH = sb(p2a, "LH", [P, 2, KR, P], F32R)
    LL = sb(p2a, "LL", [P, 2, KR, P], F32R)
    lat = sb(p2a, "lat", [P, KV])
    kr2 = sb(p2a, "kr2", [P, 2, ROPE])
    kvg = sb(p2a, "kvg", [P, KV])
    latT = sb(p2a, "latT", [P, KR + 1, P])
    gq = sb(p2a, "gq", [P, 2, ROPE])
    lst = sb(p2a, "lst", [P, 3, H + 2])
    lrt = sb(p2a, "lrt", [P, 2, ROPE])
    kn = sb(p2a, "kn", [P, H * HD])
    rot = kn[:, 0:(NT + 1) * ROPE].rearrange("p (t n) -> p t n", n=ROPE)
    Uraw = sb(p2a, "Uraw", [P, 2, KR, 256])
    ksq = Uraw[:, 0].rearrange("p a b -> p (a b)")
    p2a.close()
    p2b = ExitStack()
    qT = sb(p2b, "qT", [P, 2, H, P])
    qrT = sb(p2b, "qrT", [P, 2, H, P], F32R)
    pr = sb(p2b, "pr", [P, 2, D])
    pT = sb(p2b, "pT", [P, 2, NT, P])
    zb = sb(p2b, "zb", [P, 2, 4, P])
    qtok = sb(p2b, "qtok", [P, H, QH])
    qsq = sb(p2b, "qsq", [P, H, QH])
    qrr = sb(p2b, "qrr", [P, H, ROPE])
    qrs = sb(p2b, "qrs", [P, H, 2, ROPE], F32R)
    qrx = sb(p2b, "qrx", [P, 2, H, ROPE])
    on = sb(p2b, "on", [P, 4, P])
    ub = sb(p2b, "ub", [P, 2, 4, P])
    sb(p2b, "attention_spacer", [P, 2048])
    qraw = sb(p2b, "qraw", [P, 12, P])
    qst = sb(p2b, "qst", [P, 3, 2, H])
    amx = sb(p2b, "amx", [P, 2, 2])
    ars = sb(p2b, "ars", [P, 2, 4])
    ari = sb(p2b, "ari", [P, 4])
    p2b.close()
    p2.close()

    s_pass = sem("engines_through_a_pass")
    s_tab = sem("mla_vectors_loaded")
    s_rot = sem("rotary_tables_ready")
    s_u = [sem(f"w_u_loaded_{i}") for i in range(2)]
    s_uh = sem("w_u_hi_ready")
    s_ul = sem("w_u_lo_ready")
    s_lraw = sem("latent_raw_loaded")
    s_lca = sem("cached_latent_loaded")
    s_la = sem("latent_token_major")
    s_lsq = sem("latent_squares_summed")
    s_lat = sem("latent_ready")
    s_lout = sem("latent_stored")
    s_lb = sem("latent_transposed")
    s_lh = sem("latent_hi_ready")
    s_krT = sem("rotary_key_ready")
    s_ll = sem("latent_lo_ready")
    s_kp = sem("keys_in_psum")
    s_vp = sem("values_in_psum")
    s_ksq = sem("key_squares_ready")
    s_kn = sem("keys_normalised")
    s_vv = sem("values_ready")
    s_kt = sem("keys_transposed")
    s_kT = sem("keys_ready")
    s_qraw = sem("q_raw_loaded")
    s_qr = sem("q_norms_ready")
    s_qn = sem("q_normalised")
    s_qrr = sem("q_rotated")
    s_qe = sem("q_ready")
    s_sc = sem("scores_in_psum")
    s_mx = sem("score_maximum_ready")
    s_ex = sem("probabilities_ready")
    s_pt = sem("probabilities_transposed")
    s_pa = sem("probabilities_first_bank_copied")
    s_pd = sem("probabilities_second_bank_copied")
    s_pv = sem("attended_in_psum")
    s_on = sem("attended_normalised")
    s_t7 = sem("small_transposes_made")
    s_r7 = sem("small_transposes_read")
    s_zb = [sem(f"zb_loaded_{i}") for i in range(2)]
    s_us = [sem(f"u_b_stored_{i}") for i in range(2)]

    def meet(eng, n):
        eng.drain().then_inc(s_pass, 1)
        eng.wait_ge(s_pass, 5 * n)

    def sp_latents(sp):
        sp_lraw(sp, 0, 0)
        for i in range(2, 8):
            if i == 2:
                sp.wait_ge(s_la, 1)
                sp_lraw(sp, 1, 1)
                sp_lout(sp, 0, P, o["new_ckv_prompt"][0, 0, 0:P], o["new_krope_prompt"][0, 0, 0:P])
            if i == 4:
                sp.wait_ge(s_la, 2)
                sp_lraw(sp, 2, 2)
                sp_lout(sp, 1, P, o["new_ckv_prompt"][0, 0, P:2 * P], o["new_krope_prompt"][0, 0, P:2 * P])
            sp.wait_ge(s_ul, i - 1)
            sp_w_u(sp, i)
        with sp.Fori(2, NT) as t:
            sp.wait_ge(s_la, t + 1)
            sp_lraw(sp, t + 1, t + 1)
            sp_lout(sp, t, P, o["new_ckv_prompt"][0, 0, bass.ds(t * P, P)], o["new_krope_prompt"][0, 0, bass.ds(t * P, P)])
        for i in range(PAST // P):
            sp.wait_ge(s_lb, NT + i)
            sp.wait_ge(s_lout, 32 * NT)
            sp.dma_start(lat[:, :], a["cache_ckv"][0, 0, i * P:(i + 1) * P]).then_inc(s_lca, 16)
            for d in range(2):
                sp.dma_start(kr2[:, d], a["cache_krope"][0, 0, i * P:(i + 1) * P]).then_inc(s_lca, 16)
        sp_lout(sp, NT, DEC, o["new_ckv_sample"][0, 0], o["new_krope_sample"][0, 0])
        sp.wait_ge(s_lb, NKT)
        sp.wait_ge(s_lout, 32 * (NT + 1))
        load_q(sp, 0)
        sp.wait_ge(s_lout, 32 * (NT + 1))

    def sp_w_u(sp, i):
        w = a["w_uv"] if i < 4 else a["w_uk"]
        sp.dma_start(Uraw[:, i % 2], w[0, :, 256 * (i % 4):256 * (i % 4) + 256].rearrange("(k p) n -> p k n", p=P)).then_inc(s_u[i % 2], 16)

    def sp_latents_early(sp):
        sp.dma_start(rot[:, :, :], a["rotary_tables"].rearrange("(t p) n -> p t n", p=P)).then_inc(s_tab, 16)
        sp.dma_start(kvg[:, :], a["kv_norm"].to_broadcast([P, KV])).then_inc(s_tab, 16)
        sp.dma_start(gq[:, 0], a["q_rope_norm"].to_broadcast([P, ROPE])).then_inc(s_tab, 16)
        sp.dma_start(gq[:, 1], a["k_rope_norm"].to_broadcast([P, ROPE])).then_inc(s_tab, 16)
        for i in range(2):
            sp_w_u(sp, i)

    def sp_lraw(sp, t, tile):
        sp.dma_start(latT[:, 0:KR], scr["proj"][C_CKV:C_CKV + KR, :, bass.ds(tile * P, P)].rearrange("c p n -> p c n")).then_inc(s_lraw, 16)
        sp.dma_start(latT[0:MISC, KR], scr["proj"][C_MISC, 0:MISC, bass.ds(tile * P, P)]).then_inc(s_lraw, 16)

    def sp_lout(sp, t, n, ckv, kr):
        sp.wait_ge(s_lat, t + 1)
        sp.dma_start(ckv, lat[0:n, :]).then_inc(s_lout, 16)
        sp.dma_start(kr, kr2[0:n, 0]).then_inc(s_lout, 16)

    def pe_lat_tokens(pe, t):
        pe.wait_ge(s_lraw, 32 * (t + 1))
        for c in range(KR):
            pe.transpose(PS[:, 0, c * P:(c + 1) * P], latT[:, c], ident)
        pe.transpose(PS[:, 1, 0:MISC], latT[0:MISC, KR], ident[0:MISC, 0:MISC]).then_inc(s_la, 1)

    def pe_lat_back(pe):
        for c in range(KR):
            pe.transpose(PS[:, 2, c * P:(c + 1) * P], lat[:, c * P:(c + 1) * P], ident)
        pe.transpose(PS[:, 3, 0:P], kr2[:, :, :].rearrange("p a b -> p (a b)"), ident).then_inc(s_lb, 1)

    def pe_up(pe, slot, j, bank, done, first=False):
        for half in range(2):
            if first:
                pe.wait_ge(s_ul, 4 * (1 - j) + 2 * half + 2)
            for r in range(KR):
                for l, u, begin in ((LL, UH, True), (LH, UL, False), (LH, UH, False)):
                    last = pe.matmul(PS[:, bank + half], l[:, slot, r], u[:, j, r, 512 * half:512 * half + 512],
                                     start=(r == 0 and begin), stop=(r == KR - 1 and l is LH and u is UH))
        last.then_inc(done, 1)

    def pe_keys_back(pe, t):
        pe.wait_ge(s_kn, t + 1)
        for h in range(H):
            last = pe.transpose(PS[:, 4 + h // 4, (h % 4) * P:(h % 4 + 1) * P], kn[:, h * HD:(h + 1) * HD], ident)
        last.then_inc(s_kt, 1)

    def later(t):
        return not isinstance(t, int) or t > 0

    def latent_steps(eng, step):
        step(0, 0)
        with eng.Fori(0, (NT - 4) // 2) as i:
            step(2 * i + 1, 1)
            step(2 * i + 2, 0)
        for t in range(NT - 3, NKT):
            step(t, t % 2)

    def made(t):
        if not isinstance(t, int) or t + 2 < NT:
            return t + 2
        return NT if t == NT else None

    def pe_latents(pe):
        pe_lat_tokens(pe, 0)
        pe.wait_ge(s_lat, 1)
        pe_lat_back(pe)
        pe_lat_tokens(pe, 1)

        def step(t, slot):
            pe.wait_ge(s_ll, t + 1)
            if later(t):
                pe.wait_ge(s_vv, t)
            pe_up(pe, slot, 1, 6, s_vp, first=not later(t))
            if later(t):
                pe_keys_back(pe, t - 1)
            if not isinstance(t, int) or t + 1 < NKT:
                if isinstance(t, int) and NT <= t + 1 < NKT - 1:
                    pe.wait_ge(s_lca, 48 * (t + 2 - NT))
                else:
                    pe.wait_ge(s_lat, t + 2 if not isinstance(t, int) or t + 1 < NT else NT + 1)
                pe_lat_back(pe)
            if made(t) is not None:
                pe_lat_tokens(pe, made(t))
            if later(t):
                pe.wait_ge(s_kT, t)
            pe_up(pe, slot, 0, 4, s_kp, first=not later(t))
        latent_steps(pe, step)
        pe_keys_back(pe, NKT - 1)

    def act_lat_squares(act, t, junk=None):
        junk = ksq if junk is None else junk
        act.wait_ge(s_la, t + 1)
        act.activation(junk[:, 0:KV], PS[:, 0], ACT.Square, accum_out=lst[:, 0, H:H + 1])
        act.activation(ba[:, bass.ds(t, 1) if not isinstance(t, int) else slice(t, t + 1), :].rearrange("p a b -> p (a b)"), PS[:, 1, 0:BA], ACT.Copy)
        act.drain()
        act.activation(junk[:, 0:ROPE], PS[:, 1, BA:MISC], ACT.Square, accum_out=lst[:, 0, H + 1:H + 2]).then_inc(s_lsq, 1)

    def act_key_squares(act, t):
        act.drain()
        act.wait_ge(s_kp, t + 1)
        act.activation(ksq[:, :].rearrange("p (a b) -> p a b", a=2), PS[:, 4:6], ACT.Square).then_inc(s_ksq, 1)

    def act_values(act, t):
        act.wait_ge(s_vp, t + 1)
        act.activation(V[:, bass.ds(t, 1)].rearrange("p a (b n) -> p (a b) n", b=2), PS[:, 6:8], ACT.Copy).then_inc(s_vv, 1)

    def act_lat_hi(act, t, slot):
        act.wait_ge(s_lb, t + 1)
        act.activation(LH[:, slot].rearrange("p a b -> p (a b)"), PS[:, 2], ACT.Copy).then_inc(s_lh, 1)
        act.activation(krH[:, bass.ds(t * P, P)], PS[:, 3, 0:P], ACT.Copy).then_inc(s_krT, 1)

    def act_keys(act, t):
        act.wait_ge(s_kt, t + 1)
        for g in range(2):
            last = act.activation(kT[:, 4 * g:4 * g + 4, bass.ds(t * P, P)], PS[:, 4 + g].rearrange("p (h n) -> p h n", h=4),
                                  ACT.Copy, scale=colB[:, B_KN:B_KN + 1])
        last.then_inc(s_kT, 1)

    def act_latents(act):
        def split_hi(i):
            act.wait_ge(s_u[i % 2], 16 * (i // 2 + 1))
            act.activation(UH[:, 1 - i // 4, :, 256 * (i % 4):256 * (i % 4) + 256], Uraw[:, i % 2], ACT.Copy).then_inc(s_uh, 1)
        act.wait_ge(s_rot, 1)
        act_lat_squares(act, 0, kn)
        split_hi(0)
        act_lat_hi(act, 0, 0)
        act_lat_squares(act, 1, kn)
        for i in range(1, 8):
            split_hi(i)

        def step(t, slot):
            if later(t):
                act_keys(act, t - 1)
            if not isinstance(t, int) or t + 1 < NKT:
                act_lat_hi(act, t + 1, 1 - slot)
            if made(t) is not None:
                if later(t):
                    act.wait_ge(s_kn, t)
                else:
                    act.wait_ge(s_ul, 8)
                act_lat_squares(act, made(t))
            act_values(act, t)
            act_key_squares(act, t)
        latent_steps(act, step)
        act_keys(act, NKT - 1)

    def dve_latent(dve, t, tile):
        dve.wait_ge(s_lsq, t + 1)
        r = lst[:, 1]
        dve.tensor_scalar(lst[:, 0, H:H + 1], lst[:, 0, H:H + 1], 1.0 / KV, EPS, ALU.mult, ALU.add)
        dve.tensor_scalar(lst[:, 0, H + 1:H + 2], lst[:, 0, H + 1:H + 2], 1.0 / ROPE, EPS, ALU.mult, ALU.add)
        dve.drain()
        rsqrt(dve, lst[:, 1, H:H + 2], lst[:, 2, H:H + 2], lst[:, 0, H:H + 2])
        if not isinstance(t, int) or t:
            dve.wait_ge(s_lout, 32 * t)
        dve.scalar_tensor_tensor(lat[:, :], PS[:, 0], r[:, H:H + 1], kvg[:, :], ALU.mult, ALU.mult)
        x, half = PS[:, 1, BA:MISC], ROPE // 2
        cs = rotk[:, bass.ds(tile, 1)].rearrange("p a c n -> p (a c) n")
        dve.scalar_tensor_tensor(lrt[:, 0], x, r[:, H + 1:H + 2], cs[:, 0], ALU.mult, ALU.mult)
        dve.scalar_tensor_tensor(lrt[:, 1, 0:half], x[:, half:ROPE], r[:, H + 1:H + 2], cs[:, 1, 0:half], ALU.mult, ALU.mult)
        dve.scalar_tensor_tensor(lrt[:, 1, half:ROPE], x[:, 0:half], r[:, H + 1:H + 2], cs[:, 1, half:ROPE], ALU.mult, ALU.mult)
        dve.drain()
        dve.tensor_tensor(kr2[:, 0], lrt[:, 0], lrt[:, 1], ALU.add)
        dve.tensor_tensor(kr2[:, 1], lrt[:, 0], lrt[:, 1], ALU.add).then_inc(s_lat, 1)

    def dve_lat_lo(dve, t, slot):
        dve.wait_ge(s_krT, t + 1)
        dve.tensor_tensor(krL[0:ROPE, bass.ds(t * P, P)], PS[0:ROPE, 3, 0:P], krH[0:ROPE, bass.ds(t * P, P)].bitcast(F32), ALU.subtract)
        dve.wait_ge(s_lh, t + 1)
        dve.tensor_tensor(LL[:, slot].rearrange("p a b -> p (a b)"), PS[:, 2], LH[:, slot].rearrange("p a b -> p (a b)").bitcast(F32), ALU.subtract).then_inc(s_ll, 1)

    def dve_keys(dve, t):
        dve.wait_ge(s_ksq, t + 1)
        ss, r, tmp = lst[:, 0, 0:H], lst[:, 1, 0:H], lst[:, 2, 0:H]
        dve.tensor_reduce(ss, ksq[:, :].rearrange("p (h n) -> p h n", h=H), AX.X, ALU.add)
        dve.drain()
        dve.tensor_scalar(ss, ss, 1.0 / HD, EPS, ALU.mult, ALU.add)
        dve.drain()
        rsqrt(dve, r, tmp, ss)
        for g in range(2):
            last = dve.tensor_tensor(kn[:, 512 * g:512 * g + 512].rearrange("p (h n) -> p h n", h=4), PS[:, 4 + g].rearrange("p (h n) -> p h n", h=4),
                                     r[:, 4 * g:4 * g + 4].unsqueeze(2).to_broadcast([P, 4, HD]), ALU.mult)
        last.then_inc(s_kn, 1)

    def dve_latents(dve):
        dve.memset(lst[:, :, :], 1.0)
        dve.wait_ge(s_tab, 64)
        half = ROPE // 2
        for table, g in ((rotq, gq[:, 0]), (rotk, gq[:, 1])):
            cos, sin = rot[:, :, 0:half], rot[:, :, half:ROPE]

            def row(c):
                return g[:, c:c + half].unsqueeze(1).to_broadcast([P, NT + 1, half])
            dve.tensor_tensor(table[:, :, 0, 0:half], cos, row(0), ALU.mult)
            dve.tensor_tensor(table[:, :, 0, half:ROPE], cos, row(half), ALU.mult)
            dve.tensor_tensor(table[:, :, 1, 0:half], sin, row(half), ALU.mult)
            dve.tensor_tensor(table[:, :, 1, half:ROPE], sin, row(0), ALU.mult)
            dve.drain()
            dve.tensor_scalar(table[:, :, 1, 0:half], table[:, :, 1, 0:half], -1.0, None, ALU.mult)
        dve.drain().then_inc(s_rot, 1)

        def split_lo(i):
            dve.wait_ge(s_uh, i + 1)
            c = slice(256 * (i % 4), 256 * (i % 4) + 256)
            dve.tensor_tensor(UL[:, 1 - i // 4, :, c], Uraw[:, i % 2], UH[:, 1 - i // 4, :, c].bitcast(F32), ALU.subtract).then_inc(s_ul, 1)
        dve_latent(dve, 0, 0)
        split_lo(0)
        dve_lat_lo(dve, 0, 0)
        for i in range(1, 8):
            split_lo(i)
            if i == 1:
                dve.wait_ge(s_lb, 1)
                dve_latent(dve, 1, 1)

        def step(t, slot):
            if not isinstance(t, int) or t + 1 < NKT:
                dve_lat_lo(dve, t + 1, 1 - slot)
            n = made(t)
            if n is not None:
                dve.wait_ge(s_lb, t + 2)
                dve_latent(dve, n, n)
            dve_keys(dve, t)
        latent_steps(dve, step)

    NQ = NT + 1
    NX = NQ * H
    EARLY, LATE = 0, 1
    jobs = {(-1, LATE): [("q", 0, 0), ("q", 0, 1), ("q", 0, 2), ("b", 0, 0), ("b", 0, 1), ("b", 0, 2), ("b", 0, 3)]}
    for i in range(NQ):
        for g in range(2):
            jobs.setdefault((H * i + 4 * g + 5, EARLY), []).append(("o", 2 * i + g, 0))
        for step, phase, kind, part in ((-2, LATE, "q", 0), (-1, LATE, "q", 1), (0, LATE, "q", 2), (4, LATE, "b", 0),
                                        (5, LATE, "b", 1), (6, EARLY, "b", 2), (6, LATE, "b", 3)):
            if i + 1 < NQ:
                jobs.setdefault((max(H * i + step, -1), phase), []).append((kind, i + 1, part))
    XD = H * (NT // 2)
    dve_decays = {XD + 2 * n: n for n in range(5)}
    act_decays = {XD + 1: 0, XD + 3: 1, XD + 7: 2}
    jobs.setdefault((XD + 5, LATE), []).append(("d", 0, 0))
    jobs.setdefault((XD + 9, LATE), []).append(("d", 0, 1))
    order = [job for when in sorted(jobs) for job in jobs[when]]
    turn = {job: n for n, job in enumerate(order)}

    def keys_of(i):
        base, n = (0, P * (i + 1)) if i < NT else (SEQ, PAST + DEC)
        return base, n, [min(P, n - P * k) for k in range(-(-n // P))]

    second = [0]
    for x in range(NX):
        second.append(second[-1] + (len(keys_of(x // H)[2]) > 4))

    def scores_of(x):
        b = 2 * (x % 2)
        return PS[:, b:b + 2].rearrange("p a b -> p (a b)")[:, 0:keys_of(x // H)[1]]

    def load_q(sp, i):
        sp.dma_start(qraw[:, :], scr["proj"][C_Q:C_Q + 12, :, i * P:(i + 1) * P].rearrange("c p n -> p c n")).then_inc(s_qraw, 16)

    def sp_attention(sp):
        sp.dma_start(avec[:, 0], a["a_log"].to_broadcast([P, H])).then_inc(s_av, 16)
        sp.dma_start(avec[:, 1], a["dt_bias"].to_broadcast([P, H])).then_inc(s_av, 16)
        for i in range(NQ):
            if i == NT - 1:
                sp.wait_ge(s_gT, 1)
                sp.dma_start(scr["gcum"].rearrange("t h n -> (t h) n"), gcT).then_inc(s_gw, 16)
            if i + 1 < NQ:
                sp.wait_ge(s_t7, turn[("q", i, 2)] + 1)
                load_q(sp, i + 1)
            for g in range(2):
                if i:
                    sp.wait_ge(s_r7, turn[("o", 2 * i - 2 + g, 0)] + 1)
                    store_ub(sp, 2 * i - 2 + g)
                sp.dma_start(zb[:, g], scr["proj"][C_ZB + 4 * g:C_ZB + 4 * g + 4, :, i * P:(i + 1) * P].rearrange("c p n -> p c n")).then_inc(s_zb[g], 16)
        sp.wait_ge(s_pv, NT * H)
        sp.wait_ge(s_gw, 16)
        for t in range(2):
            sp_load_qkv(sp, t, t)
            sp_load_gcum(sp, t, t)
        for g in range(2):
            sp.wait_ge(s_r7, turn[("o", 2 * NT + g, 0)] + 1)
            store_ub(sp, 2 * NT + g)
        for g in range(2):
            sp.wait_ge(s_us[g], 16 * NQ)

    def store_ub(sp, og):
        i, g = divmod(og, 2)
        sp.dma_start(scr["u"][H + 4 * g:H + 4 * g + 4, :, i * P:(i + 1) * P].rearrange("c p n -> p c n"), ub[:, g]).then_inc(s_us[g], 16)

    def pe_job(pe, job):
        kind, i, part = job
        n = turn[job]
        if n:
            pe.wait_ge(s_r7, n)
        if kind == "d":
            if part == 0:
                pe.wait_ge(s_gg, 1)
                g = gat.rearrange("p t h -> p (t h)")
                pe.matmul(PS[:, 7, 0:TH], cst[:, K_INC:K_INC + P], g, start=True, stop=True)
                pe.matmul(PS[:, 7, P:P + TH], ones, g, start=True, stop=True).then_inc(s_t7, 1)
            else:
                pe.wait_ge(s_gx, 1)
                pe.transpose(PS[0:TH, 7, 0:P], gtm[:, 0].rearrange("p t h -> p (t h)"), ident).then_inc(s_t7, 1)
            return
        if kind == "q":
            pe.wait_ge(s_qraw, 16 * (i + 1))
            srcs = [qraw[:, 4 * part + c] for c in range(4)]
        elif kind == "b" and part < 2:
            pe.wait_ge(s_qn, i + 1)
            srcs = [qsq[:, 4 * part + c, 0:HD] for c in range(4)]
        elif kind == "b":
            pe.wait_ge(s_qrr, i + 1)
            srcs = [qrs[:, 4 * (part - 2) + c].rearrange("p a b -> p (a b)").bitcast(F32) for c in range(4)]
        else:
            pe.wait_ge(s_on, i + 1)
            srcs = [on[:, c] for c in range(4)]
        for c, src in enumerate(srcs):
            last = pe.transpose(PS[:, 7, c * P:(c + 1) * P], src, ident)
        last.then_inc(s_t7, 1)

    def pe_scores(pe, x):
        i, h = divmod(x, H)
        base, n, _ = keys_of(i)
        if h == 0:
            pe.wait_ge(s_qe, 4 * (i + 1))
        if x >= 2:
            pe.wait_ge(s_ex, x - 1)
        for b in range(-(-n // 512)):
            w = min(512, n - 512 * b)
            c = base + 512 * b
            out = PS[:, 2 * (x % 2) + b, 0:w]
            pe.matmul(out, qT[:, i % 2, h], kT[:, h, c:c + w], start=True, stop=False)
            pe.matmul(out, qrT[0:ROPE, i % 2, h], krL[0:ROPE, c:c + w], start=False, stop=False)
            last = pe.matmul(out, qrT[:, i % 2, h], krH[:, c:c + w], start=False, stop=True)
        last.then_inc(s_sc, 1)

    def pe_transposes(pe, x):
        widths = keys_of(x // H)[2]
        pe.wait_ge(s_ex, x + 1)
        if x:
            pe.wait_ge(s_pa, x)
            if second[x]:
                pe.wait_ge(s_pd, second[x])
        for k, w in enumerate(widths):
            last = pe.transpose(PS[0:w, 4 + k // 4, (k % 4) * P:(k % 4 + 1) * P], pr[:, x % 2, k * P:k * P + w], ident)
        last.then_inc(s_pt, 1)

    def pe_values(pe, x):
        i, h = divmod(x, H)
        base, n, widths = keys_of(i)
        pe.wait_ge(s_pa, x + 1)
        if second[x + 1]:
            pe.wait_ge(s_pd, second[x + 1])
        if x % 4 == 0 and x:
            pe.wait_ge(s_on, x // 4)
        for k, w in enumerate(widths):
            last = pe.matmul(PS[:, 6, (h % 4) * P:(h % 4 + 1) * P], pT[0:w, x % 2, k], V[0:w, base // P + k, h * HD:(h + 1) * HD],
                             start=(k == 0), stop=(k == len(widths) - 1))
        last.then_inc(s_pv, 1)

    def pe_attention(pe):
        for job in jobs[-1, LATE]:
            pe_job(pe, job)
        pe_scores(pe, 0)
        for x in range(NX + 2):
            if x + 1 < NX:
                pe_scores(pe, x + 1)
            for job in jobs.get((x, EARLY), []):
                pe_job(pe, job)
            if 1 <= x <= NX:
                pe_values(pe, x - 1)
            if x < NX:
                pe_transposes(pe, x)
            for job in jobs.get((x, LATE), []):
                pe_job(pe, job)

    def act_decay(act, step):
        if step == 0:
            act.wait_ge(s_av, 32)
            act.wait_ge(s_gd1, 1)
            act.activation(tvs[:, :, 5], ba[:, :, 0:H], ACT.Sigmoid)
            act.activation(gtm[:, 1], gtm[:, 0], ACT.Abs)
            act.drain()
            act.activation(gtm[:, 1], gtm[:, 1], ACT.Exp, scale=-1.0)
            act.activation(avec[:, 0], avec[:, 0], ACT.Exp).then_inc(s_bs, 1)
        elif step == 1:
            act.wait_ge(s_gd1, 2)
            act.activation(gtm[:, 3], gtm[:, 2], ACT.Ln).then_inc(s_bs, 1)
        else:
            act.activation(tvs[:, :, 1], gtm[:, 0], ACT.Exp)
            act.activation(tvs[:, :, 4], gtm[:, 1], ACT.Exp)
            act.wait_ge(s_gd1, 3)
            act.activation(tvs[:, :, 3], gtm[:, 2], ACT.Exp)
            act.drain().then_inc(s_bs, 1)

    def act_job(act, job):
        kind, i, part = job
        if kind == "o" or (kind == "b" and part >= 2):
            return
        act.wait_ge(s_t7, turn[job] + 1)
        if kind == "d":
            if part == 0:
                sums, totals = (PS[:, 7, c:c + TH].rearrange("p (t h) -> p t h", h=H) for c in (0, P))
                act.activation(tvs[:, :, 0], sums, ACT.Copy)
                act.activation(gtm[:, 0], sums, ACT.Copy)
                act.activation(gtm[:, 1], totals, ACT.Copy)
                act.drain().then_inc(s_r7, 1)
            else:
                act.activation(gcT, PS[0:TH, 7, 0:P], ACT.Copy).then_inc(s_r7, 1)
            act.wait_ge(s_r7, turn[job] + 1)
            act.sem_inc((s_gx, s_gT)[part], 1)
        elif kind == "q":
            if i:
                act.wait_ge(s_qn, i)
                act.wait_ge(s_qrr, i)
                act.wait_ge(s_t7, turn[("b", i - 1, 1)] + 1)
            cols = slice(512 * part, 512 * part + 512)
            act.activation(qtok[:, :, :].rearrange("p a b -> p (a b)")[:, cols], PS[:, 7], ACT.Copy)
            act.activation(qsq[:, :, :].rearrange("p a b -> p (a b)")[:, cols], PS[:, 7], ACT.Square).then_inc(s_r7, 1)
        else:
            act.activation(qT[:, i % 2, 4 * part:4 * part + 4].rearrange("p a b -> p (a b)"), PS[:, 7], ACT.Copy, scale=colB[:, B_QN:B_QN + 1]).then_inc(s_r7, 1)
            act.wait_ge(s_r7, turn[job] + 1)
            act.sem_inc(s_qe, 1)

    def act_exp(act, x):
        n = keys_of(x // H)[1]
        act.wait_ge(s_mx, x + 1)
        if x >= 2:
            act.wait_ge(s_pt, x - 1)
        if x % 4 == 0 and x >= 8:
            act.wait_ge(s_on, x // 4 - 1)
        act.activation(pr[:, x % 2, 0:n], scores_of(x), ACT.Exp, bias=amx[:, x % 2, 1:2], scale=SCALE,
                       accum_out=ars[:, x // 4 % 2, x % 4:x % 4 + 1]).then_inc(s_ex, 1)

    def act_attention(act):
        for job in jobs[-1, LATE]:
            act_job(act, job)
        act_exp(act, 0)
        for x in range(NX):
            if x + 1 < NX:
                act_exp(act, x + 1)
            for job in jobs.get((x, EARLY), []):
                act_job(act, job)
            nk = min(4, len(keys_of(x // H)[2]))
            act.wait_ge(s_pt, x + 1)
            if x >= 2:
                act.wait_ge(s_pv, x - 1)
            act.activation(pT[:, x % 2, 0:nk].rearrange("p a b -> p (a b)"), PS[:, 4, 0:nk * P], ACT.Copy).then_inc(s_pa, 1)
            for job in jobs.get((x, LATE), []):
                act_job(act, job)
            if x in act_decays:
                act_decay(act, act_decays[x])

    def pool_attention(pool):
        half = ROPE // 2
        for i in range(NQ):
            if i:
                pool.wait_ge(s_t7, turn[("b", i - 1, 3)] + 1)
            pool.wait_ge(s_qr, i + 1)
            r = qst[:, 1, 1].unsqueeze(2).to_broadcast([P, H, ROPE])
            cos = rotq[:, i:i + 1, 0].to_broadcast([P, H, ROPE])
            sin = rotq[:, i:i + 1, 1].to_broadcast([P, H, ROPE])
            pool.tensor_tensor(qrr[:, :, :], qtok[:, :, HD:QH], r, ALU.mult)
            pool.drain()
            pool.tensor_tensor(qrx[:, 0], qrr[:, :, :], cos, ALU.mult)
            pool.tensor_tensor(qrx[:, 1, :, 0:half], qrr[:, :, half:ROPE], sin[:, :, 0:half], ALU.mult)
            pool.tensor_tensor(qrx[:, 1, :, half:ROPE], qrr[:, :, 0:half], sin[:, :, half:ROPE], ALU.mult)
            pool.drain()
            pool.tensor_tensor(qrr[:, :, :], qrx[:, 0], qrx[:, 1], ALU.add)
            pool.drain()
            pool.tensor_copy(qrs[:, :, 0], qrr[:, :, :])
            pool.drain()
            pool.tensor_tensor(qrs[:, :, 1], qrr[:, :, :], qrs[:, :, 0].bitcast(F32), ALU.subtract).then_inc(s_qrr, 1)

    def dve_q_norms(dve, i, part):
        ss = qst[:, 0]
        if part == 0:
            dve.wait_ge(s_r7, turn[("q", i, 2)] + 1)
            dve.tensor_reduce(ss[:, 0], qsq[:, :, 0:HD], AX.X, ALU.add)
            dve.tensor_reduce(ss[:, 1], qsq[:, :, HD:QH], AX.X, ALU.add)
            dve.drain()
            dve.tensor_scalar(ss[:, 0], ss[:, 0], 1.0 / HD, EPS, ALU.mult, ALU.add)
            dve.tensor_scalar(ss[:, 1], ss[:, 1], 1.0 / ROPE, EPS, ALU.mult, ALU.add)
            dve.drain()
        elif part == 1:
            if i:
                dve.wait_ge(s_qrr, i)
            rsqrt(dve, qst[:, 1].rearrange("p a b -> p (a b)"), qst[:, 2].rearrange("p a b -> p (a b)"), ss.rearrange("p a b -> p (a b)"))
            dve.drain().then_inc(s_qr, 1)
        else:
            dve.tensor_tensor(qsq[:, :, 0:HD], qtok[:, :, 0:HD], qst[:, 1, 0].unsqueeze(2).to_broadcast([P, H, HD]), ALU.mult).then_inc(s_qn, 1)

    def dve_decay(dve, step):
        x0, t1, u, ln = (gtm[:, n] for n in range(4))
        same, log1p = gsm[:, 0], gsm[:, 1]
        if step == 0:
            dve.wait_ge(s_av, 32)
            dve.tensor_tensor(x0, ba[:, :, H:BA], avec[:, 1:2].to_broadcast([P, NT + 1, H]), ALU.add)
            dve.drain().then_inc(s_gd1, 1)
        elif step == 1:
            dve.wait_ge(s_bs, 1)
            dve.tensor_scalar(u, t1, 1.0, None, ALU.add)
            dve.drain().then_inc(s_gd1, 1)
        elif step == 2:
            dve.tensor_scalar(gat, u, -1.0, None, ALU.add)
            dve.drain()
            dve.tensor_scalar(same, gat, 0.0, None, ALU.is_equal)
            dve.drain()
            dve.tensor_tensor(gat, gat, same, ALU.add)
            dve.drain()
            dve.reciprocal(log1p, gat)
            dve.wait_ge(s_bs, 2)
            dve.drain()
            dve.tensor_tensor(log1p, log1p, ln, ALU.mult)
            dve.drain()
            dve.tensor_tensor(log1p, log1p, same, ALU.add)
            dve.drain()
            dve.tensor_tensor(log1p, log1p, t1, ALU.mult)
            dve.drain()
            dve.scalar_tensor_tensor(gat, x0, 0.0, log1p, ALU.max, ALU.add)
            dve.drain()
            dve.scalar_tensor_tensor(gat, gat, -1.0, avec[:, 0:1].to_broadcast([P, NT + 1, H]), ALU.mult, ALU.mult)
            dve.drain()
            dve.memset(gat[DEC:2 * DEC, NT], 0.0)
            dve.memset(gat[2 * DEC:P, NT], 0.0)
            dve.drain().then_inc(s_gg, 1)
        elif step == 3:
            dve.wait_ge(s_gx, 1)
            dve.tensor_tensor(gtm[:, 2], gtm[:, 1], gtm[:, 0], ALU.subtract)
            dve.drain().then_inc(s_gd1, 1)
        else:
            dve.wait_ge(s_bs, 3)
            dve.tensor_scalar(tvs[:, :, 2], tvs[:, :, 1], -1.0, None, ALU.mult)
            dve.drain().then_inc(s_ge, 1)

    def dve_job(dve, job):
        kind, i, part = job
        if kind == "q" and part == 2:
            if i == 0:
                for n in range(3):
                    dve_q_norms(dve, 0, n)
        if kind == "b" and part >= 2:
            dve.wait_ge(s_t7, turn[job] + 1)
            dve.tensor_copy(qrT[:, i % 2, 4 * (part - 2):4 * (part - 2) + 4].rearrange("p a b -> p (a b)"), PS[:, 7]).then_inc(s_r7, 1)
            dve.wait_ge(s_r7, turn[job] + 1)
            dve.sem_inc(s_qe, 1)
        if kind == "o":
            t, g = divmod(i, 2)
            dve.wait_ge(s_t7, turn[job] + 1)
            dve.wait_ge(s_zb[g], 16 * (t + 1))
            if t:
                dve.wait_ge(s_us[g], 16 * t)
            dve.tensor_tensor(ub[:, g].rearrange("p a b -> p (a b)"), PS[:, 7], zb[:, g].rearrange("p a b -> p (a b)"), ALU.mult).then_inc(s_r7, 1)

    def dve_max(dve, x):
        i, n = x // H, keys_of(x // H)[1]
        s = scores_of(x)
        dve.wait_ge(s_sc, x + 1)
        if i < NT:
            dve.memset(s[0:CHUNK, n - CHUNK:n], -1.0e30)
            dve.drain()
        dve.tensor_reduce(amx[:, x % 2, 0:1], s, AX.X, ALU.max)
        dve.drain()
        dve.tensor_scalar(amx[:, x % 2, 1:2], amx[:, x % 2, 0:1], -SCALE, None, ALU.mult).then_inc(s_mx, 1)

    def dve_attention(dve):
        for job in jobs[-1, LATE]:
            dve_job(dve, job)
        dve_max(dve, 0)
        for x in range(NX + 2):
            if x + 1 < NX:
                dve_max(dve, x + 1)
            if 4 <= x <= NX and x % 4 == 0:
                g = x // 4 - 1
                dve.wait_ge(s_pv, x)
                dve.reciprocal(ari[:, :], ars[:, g % 2])
                dve.drain()
                if g:
                    dve.wait_ge(s_t7, turn[("o", g - 1, 0)] + 1)
                dve.tensor_tensor(on[:, :, :], PS[:, 6].rearrange("p (h n) -> p h n", h=4), ari[:, :].unsqueeze(2).to_broadcast([P, 4, HD]), ALU.mult).then_inc(s_on, 1)
            for job in jobs.get((x, EARLY), []):
                dve_job(dve, job)
            if x < NX:
                nk = len(keys_of(x // H)[2])
                if nk > 4:
                    dve.wait_ge(s_pt, x + 1)
                    if x >= 2:
                        dve.wait_ge(s_pv, x - 1)
                    dve.tensor_copy(pT[:, x % 2, 4:nk].rearrange("p a b -> p (a b)"), PS[:, 5, 0:(nk - 4) * P]).then_inc(s_pd, 1)
            for job in jobs.get((x, LATE), []):
                dve_job(dve, job)
            if x in dve_decays:
                dve_decay(dve, dve_decays[x])
            if 1 <= x % H <= 3 and x // H + 1 < NQ:
                dve_q_norms(dve, x // H + 1, x % H - 1)

    p3 = ExitStack()
    NL7 = len(LEVELS)
    TVN = 6
    decay = sb(p3, "decay", [P, (NT + 1) * 2 * ROPE])
    TH = (NT + 1) * H

    def decay_part(first, blocks):
        return decay[:, first * TH:(first + blocks) * TH]
    tvs = decay_part(0, TVN).rearrange("p (t v h) -> p t v h", v=TVN, h=H)
    gat = decay_part(TVN, 1).rearrange("p (t h) -> p t h", h=H)
    gtm = decay_part(TVN + 1, 4).rearrange("p (n t h) -> p n t h", n=4, h=H)
    gsm = decay_part(TVN + 5, 2).rearrange("p (n t h) -> p n t h", n=2, h=H)
    avec = decay[:, 13 * TH:13 * TH + 2 * H].rearrange("p (n h) -> p n h", n=2)
    gcT = decay[0:TH, 13 * TH + 2 * H:13 * TH + 2 * H + P]
    def per_group(name, slots=None):
        shape = [P, 2] + ([slots] if slots else []) + [4 * P]
        return sb(p3, name, shape)
    za = sb(p3, "za", [P, 2, H, P])
    S = sb(p3, "S", [P, 2, H, HD])
    Kt = per_group("Kt", 2)
    Vn = per_group("Vn", 2)
    sq = per_group("sq")
    sq2 = per_group("sq2")
    sqo = per_group("sqo")
    QKV = sb(p3, "QKV", [P, 2, 3 * H, P])
    GB = sb(p3, "GB", [P, 2, H * P])
    tv = sb(p3, "tv", [P, 2, TVN, H])
    RS = sb(p3, "RS", [P, 3, 24])
    dst = RS[:, :, 0:16].rearrange("p n (g x h) -> p n g x h", g=2, x=2)
    osum = RS[:, :, 16:24].rearrange("p n (g h) -> p n g h", g=2)
    vec = sb(p3, "vec", [P, 2, 5, 2, 4])
    ost = sb(p3, "ost", [P, 2, 4])

    E = per_group("E")
    Em = per_group("Em")
    Es = per_group("Es")
    NL = per_group("NL")
    AT = per_group("AT")
    QL = per_group("QL", NL7)
    X = per_group("X")
    XT = per_group("XT")
    RR = per_group("RR")
    Z = per_group("Z")
    ZD = per_group("ZD")
    O1 = per_group("O1")
    O2 = per_group("O2")
    ON = per_group("ON")
    UA = per_group("UA")
    p3.close()

    s_av = sem("decay_vectors_loaded")
    s_bs = sem("beta_ready")
    s_gd1 = sem("gate_softplus_step")
    s_gg = sem("log_decay_ready")
    s_gx = sem("log_decay_copied")
    s_ge = sem("decay_scalars_ready")
    s_gT = sem("log_decay_rows_ready")
    s_gw = sem("log_decay_rows_stored")
    s_st = sem("sample_state_loaded")
    s_tv = sem("tile_scalars_ready")
    s_seen = sem("level_product_seen")
    s_in = [sem(f"qkv_tile_loaded_{i}") for i in range(2)]
    s_gb = [sem(f"decay_rows_loaded_{i}") for i in range(2)]
    s_za = [sem(f"za_tile_loaded_{i}") for i in range(2)]
    s_ua = sem("u_a_stored")
    s_so = sem("states_stored")

    PE_PREP, PE_MAIN, PE_OUT = ("k", "q", "v", "kk", "qk"), ("l", "x0") + tuple(
        f"{a}{l}" for l in range(1, NL7) for a in "px") + ("ks", "qs", "y", "st", "av"), ("on",)
    ACT_PREP, ACT_MAIN, ACT_OUT = ("k", "q", "e"), tuple(f"x{l}" for l in range(NL7)) + ("o1",), ("sq",)
    DVE_PREP, DVE_MAIN, DVE_OUT = ("sub", "vn", "nl", "at"), tuple(f"q{l}" for l in range(NL7)) + (
        "r", "zd", "z", "s", "o2"), ("on", "u")
    s_pe = {n: [sem(f"delta_pe_{n}_{g}") for g in range(2)] for n in ("prep", "main", "out")}
    s_ac = {n: [sem(f"delta_act_{n}_{g}") for g in range(2)] for n in ("prep", "main", "out")}
    s_dv = {n: [sem(f"delta_dve_{n}_{g}") for g in range(2)] for n in ("prep", "main", "out")}
    s_em = [sem(f"masked_decays_ready_{g}") for g in range(2)]

    def after(eng, sems, steps, g, t, step):
        eng.wait_ge(sems[g], len(steps) * t + steps.index(step) + 1)

    def bank(g, b):
        return PS[:, 4 * g + b]

    def hs(x, h):
        return x[:, h * P:(h + 1) * P]

    def heads(x):
        return x.rearrange("p (h n) -> p h n", h=4)

    def wide(v):
        return v.unsqueeze(2).to_broadcast([P, 4, P])

    def run_tiles(eng, body):
        body(0, 0, True)
        with eng.Fori(0, (NT - 2) // 2) as i:
            body(2 * i + 1, 1, False)
            body(2 * i + 2, 0, False)
        body(NT - 1, 1, False)
        body(NT, 0, False)

    p4 = ExitStack()
    M4 = sb(p4, "M4", [P, KD, TOK])
    gate = sb(p4, "gate", [P, 2, D])
    p4a = ExitStack()
    FH = sb(p4a, "FH", [P, KD, TOK], F32R)
    FL = sb(p4a, "FL", [P, KD, TOK], F32R)
    VH = sb(p4a, "VH", [P, 2, KD, 256], F32R)
    VL = sb(p4a, "VL", [P, 2, KD, 256], F32R)
    NFR = 4
    fr = sb(p4a, "fr", [P, NFR, TOK])
    gr = sb(p4a, "gr", [P, 2, TOK])
    sb(p4a, "branches_spacer", [P, 1024])
    Vraw = sb(p4a, "Vraw", [P, 2, KD, 256])
    p4a.close()
    p4b = ExitStack()
    OH = sb(p4b, "OH", [P, KD, D], F32R)
    OL = sb(p4b, "OL", [P, KD, D], F32R)
    MH = sb(p4b, "MH", [P, 2, KD, P], F32R)
    ML = sb(p4b, "ML", [P, 2, KD, P], F32R)
    xt = sb(p4b, "xt", [P, 2, D])
    yt = sb(p4b, "yt", [P, 2, D])
    p4b.close()
    p4.close()
    GD = M4[:, 0:2, 0:D]

    s_fr = [sem(f"u_rows_loaded_{i}") for i in range(NFR)]
    s_fh = sem("u_hi_ready")
    s_fl = sem("u_lo_ready")
    s_vr = [sem(f"w_o_loaded_{i}") for i in range(2)]
    s_vh = sem("w_o_hi_ready")
    s_vl = sem("w_o_lo_ready")
    s_o = sem("branch_chunk_in_psum")
    s_ur = sem("u_a_row_used")
    s_gr = [sem(f"gate_rows_loaded_{i}") for i in range(2)]
    s_m = sem("merged_chunk_ready")
    s_gdg = sem("gate_diagonal_ready")
    s_gps = sem("gate_in_psum")
    s_gok = sem("gate_ready")
    s_or = [sem(f"w_out_loaded_{i}") for i in range(2)]
    s_oh = sem("w_out_hi_ready")
    s_ol = sem("w_out_lo_ready")
    s_mh = sem("merged_tile_hi_ready")
    s_ml = sem("merged_tile_lo_ready")
    s_yp = sem("y_in_psum")
    s_xt = [sem(f"x_tile_loaded_{i}") for i in range(2)]
    s_y = sem("y_tile_ready")
    s_ys = [sem(f"y_tile_stored_{i}") for i in range(2)]

    def sp_out(sp):
        def row(r):
            if r >= NFR:
                sp.wait_ge(s_fl, r - NFR + 1)
            sp.dma_start(fr[:, r % NFR], scr["u"][r, :, 0:TOK]).then_inc(s_fr[r % NFR], 16)

        def weights(l):
            sp.wait_ge(s_vl, l - 1)
            sp_w_o(sp, l)

        def gates(n):
            sp.wait_ge(s_m, n - 1)
            sp_gate_rows(sp, n)

        for r in range(KD):
            row(r)
            if r == 3:
                for n in range(2):
                    sp_gate_rows(sp, n)
        weights(2)
        for r in range(KD, KD + NFR):
            row(r)
        for l in range(3, 6):
            weights(l)
            gates(2 * l - 4)
            gates(2 * l - 3)
        gates(KD)
        for r in range(KD + NFR, 2 * KD):
            row(r)
        gates(KD + 1)
        weights(6)
        weights(7)
        for n in range(KD + 2, 2 * KD):
            gates(n)
            if n in (2 * KD - 3, 2 * KD - 2):
                i = n - (2 * KD - 3)
                sp.wait_ge(s_vl, KD - 1 + i)
                sp_w_out(sp, i)

    def sp_w_out(sp, i):
        sp.dma_start(Vraw[:, i % 2], a["w_out"][0, :, 256 * i:256 * i + 256].rearrange("(k p) n -> p k n", p=P)).then_inc(s_or[i % 2], 16)

    def sp_w_o(sp, l):
        w = a["w_o_dn"] if l < 4 else a["w_o_mla"]
        sp.dma_start(Vraw[:, l % 2], w[0, :, 256 * (l % 4):256 * (l % 4) + 256].rearrange("(k p) n -> p k n", p=P)).then_inc(s_vr[l % 2], 16)

    def sp_gate_rows(sp, n):
        sp.dma_start(gr[:, n % 2], scr["proj"][C_GA + n, :, 0:TOK]).then_inc(s_gr[n % 2], 16)

    def act_out(act):
        def split_w(l):
            act.wait_ge(s_vr[l % 2], 16 * (l // 2 + 1))
            if l >= 2:
                act.wait_ge(s_o, 2 * l - 2)
            act.activation(VH[:, l % 2], Vraw[:, l % 2], ACT.Copy).then_inc(s_vh, 1)
        split_w(0)
        for r in range(2 * KD):
            if r == KD:
                split_w(1)
                for l in range(2, 5):
                    split_w(l)
            if r >= KD:
                if r < 2 * KD - 1:
                    act.wait_ge(s_ur, r - KD + 1)
                else:
                    act.wait_ge(s_o, KD)
            act.wait_ge(s_fr[r % NFR], 16 * (r // NFR + 1))
            act.activation(FH[:, r % KD], fr[:, r % NFR], ACT.Copy).then_inc(s_fh, 1)
        for l in range(5, KD):
            split_w(l)

    def dve_gate(dve):
        for i in range(4):
            j, s = 16 + 4 * (i % 2), i // 2
            dve.tensor_tensor(GD[:, s, 512 * (i % 2):512 * (i % 2) + 512].rearrange("p (j n) -> p j n", j=4), ident.unsqueeze(1).to_broadcast([P, 4, P]),
                              mod[:, j:j + 4, s:s + 1].to_broadcast([P, 4, P]), ALU.mult).then_inc(s_gdg, 1)
        for i in range(4):
            dve.wait_ge(s_gps, i + 1)
            dve.tensor_copy(gate[:, i // 2, 512 * (i % 2):512 * (i % 2) + 512], PS[:, i]).then_inc(s_gok, 1)

    def dve_branches(dve):
        def split_w(l):
            dve.wait_ge(s_vh, l + 1)
            dve.tensor_tensor(VL[:, l % 2], Vraw[:, l % 2], VH[:, l % 2].bitcast(F32), ALU.subtract).then_inc(s_vl, 1)

        def merge(n):
            d = n % KD
            dve.wait_ge(s_o, n + 1)
            dve.wait_ge(s_gr[n % 2], 16 * (n // 2 + 1))
            b3 = PS[:, 3 * (n % 2):3 * (n % 2) + 3, 0:TB]
            rows3 = gr[:, n % 2].rearrange("p (b n) -> p b n", b=3)
            if n < KD:
                dve.tensor_tensor(M4[:, d].rearrange("p (b n) -> p b n", b=3), b3, rows3, ALU.mult).then_inc(s_m, 1)
            else:
                dve.tensor_tensor(rows3, b3, rows3, ALU.mult)
                dve.drain()
                dve.tensor_tensor(M4[:, d], M4[:, d], gr[:, n % 2], ALU.add).then_inc(s_m, 1)

        dve_gate(dve)
        split_w(0)
        for r in range(2 * KD):
            if r == KD:
                split_w(1)
                for n in range(KD - 1):
                    merge(n)
                    if n % 2:
                        split_w(n // 2 + 2)
            if r == 2 * KD - 1:
                merge(KD - 1)
            dve.wait_ge(s_fh, r + 1)
            dve.tensor_tensor(FL[:, r % KD], fr[:, r % NFR], FH[:, r % KD].bitcast(F32), ALU.subtract).then_inc(s_fl, 1)
        for n in range(KD, 2 * KD):
            if n % 2 == 0 and n // 2 + 1 < KD:
                split_w(n // 2 + 1)
            merge(n)

    def pe_branches(pe):
        for i in range(4):
            pe.wait_ge(s_gdg, i + 1)
            pe.matmul(PS[:, i], ones, GD[:, i // 2, 512 * (i % 2):512 * (i % 2) + 512], start=True, stop=True).then_inc(s_gps, 1)
        pe.wait_ge(s_gok, 4)
        for n in range(2 * KD):
            l = n // 2
            pe.wait_ge(s_vl, l + 1)
            if n >= 2:
                pe.wait_ge(s_m, n - 1)
            for k in range(KD):
                if n % KD == 0:
                    pe.wait_ge(s_fl, n + k + 1)
                for w, u, first in ((VL, FH, True), (VH, FL, False), (VH, FH, False)):
                    for b in range(NB):
                        last = pe.matmul(PS[:, 3 * (n % 2) + b, 0:TB], w[:, l % 2, k, (n % 2) * P:(n % 2) * P + P], u[:, k, b * TB:(b + 1) * TB],
                                         start=(k == 0 and first), stop=(k == KD - 1 and u is FH and not first))
                if n == KD - 1 and k < KD - 1:
                    last.then_inc(s_ur, 1)
            last.then_inc(s_o, 1)

    def sp_y(sp):
        for i in range(2, 4):
            sp.wait_ge(s_ol, i - 1)
            sp_w_out(sp, i)
        sp.wait_ge(s_m, 2 * KD)
        for s in range(2):
            sp.dma_start(xt[:, s], a["x_prompt"][0, P * s:P * s + P]).then_inc(s_xt[s], 16)

        def store(t, s):
            sp.wait_ge(s_y, 2 * (t + 1))
            sp.dma_start(o["y_prompt"][0, bass.ds(t * P, P)], yt[:, s]).then_inc(s_ys[s], 16)
        with sp.Fori(0, NT // 2 - 1) as i:
            for s in range(2):
                store(2 * i + s, s)
                sp.dma_start(xt[:, s], a["x_prompt"][0, bass.ds(P * (2 * i + s + 2), P)]).then_inc(s_xt[s], 16)
        store(NT - 2, 0)
        sp.dma_start(xt[0:DEC, 0], a["x_sample"][0]).then_inc(s_xt[0], 16)
        store(NT - 1, 1)
        sp.wait_ge(s_y, 2 * NT + 2)
        sp.dma_start(o["y_sample"][0], yt[0:DEC, 0]).then_inc(s_ys[0], 16)
        sp.wait_ge(s_ys[0], 16 * 5)
        sp.wait_ge(s_ys[1], 16 * 4)

    def act_y(act):
        act.wait_ge(s_o, 2 * KD)
        act.sem_inc(s_yp, 2)

        def split_w(i):
            act.wait_ge(s_or[i % 2], 16 * (i // 2 + 1))
            act.activation(OH[:, :, 256 * i:256 * i + 256], Vraw[:, i % 2], ACT.Copy).then_inc(s_oh, 1)

        def tile(t, slot, n):
            act.wait_ge(s_yp, t + 1)
            act.activation(MH[:, slot, :, 0:n], M4[:, :, bass.ds(t * P, n)], ACT.Copy).then_inc(s_mh, 1)
        split_w(0)
        act.wait_ge(s_m, 2 * KD)
        tile(0, 0, P)
        for i in range(1, 4):
            split_w(i)
        with act.Fori(0, NT // 2 - 1) as i:
            tile(2 * i + 1, 1, P)
            tile(2 * i + 2, 0, P)
        tile(NT - 1, 1, P)
        tile(NT, 0, DEC)

    def dve_y(dve):
        def low(t, slot, n):
            dve.wait_ge(s_mh, t + 1)
            dve.tensor_tensor(ML[:, slot, :, 0:n], M4[:, :, bass.ds(t * P, n)], MH[:, slot, :, 0:n].bitcast(F32), ALU.subtract).then_inc(s_ml, 1)

        for i in range(4):
            if i == 1:
                low(0, 0, P)
            dve.wait_ge(s_oh, i + 1)
            dve.tensor_tensor(OL[:, :, 256 * i:256 * i + 256], Vraw[:, i % 2], OH[:, :, 256 * i:256 * i + 256].bitcast(F32), ALU.subtract).then_inc(s_ol, 1)

        def body(t, slot, n, first):
            if not (isinstance(t, int) and t == NT):
                low(t + 1, 1 - slot, DEC if isinstance(t, int) and t == NT - 1 else P)
            dve.wait_ge(s_yp, t + 3)
            for h in range(2):
                c = slice(512 * h, 512 * h + 512)
                if h == 0:
                    dve.wait_ge(s_xt[slot], 16 * ((t - slot) // 2 + 1))
                    if not (isinstance(t, int) and t < 2):
                        dve.wait_ge(s_ys[slot], 16 * ((t - slot) // 2))
                g = 1 if isinstance(t, int) and t == NT else 0
                dve.tensor_tensor(yt[0:n, slot, c], PS[0:n, 4 * slot + h], gate[0:n, g, c], ALU.mult)
                dve.drain()
                dve.tensor_tensor(yt[0:n, slot, c], yt[0:n, slot, c], xt[0:n, slot, c], ALU.add).then_inc(s_y, 1)
        body(0, 0, P, True)
        body(1, 1, P, False)
        with dve.Fori(1, NT // 2 - 1) as i:
            body(2 * i, 0, P, False)
            body(2 * i + 1, 1, P, False)
        body(NT - 2, 0, P, False)
        body(NT - 1, 1, P, False)
        body(NT, 0, DEC, False)

    def pe_y(pe):
        def body(t, slot, n, first):
            pe.wait_ge(s_ml, t + 1)
            if not (isinstance(t, int) and t < 2):
                pe.wait_ge(s_y, 2 * t - 2)
            for h in range(2):
                if first:
                    pe.wait_ge(s_ol, 2 * h + 2)
                for k in range(KD):
                    for m, w, fst in ((ML, OH, True), (MH, OL, False), (MH, OH, False)):
                        last = pe.matmul(PS[:, 4 * slot + h], m[:, slot, k], w[:, k, 512 * h:512 * h + 512],
                                         start=(k == 0 and fst), stop=(k == KD - 1 and m is MH and w is OH))
            last.then_inc(s_yp, 1)
        body(0, 0, P, True)
        body(1, 1, P, False)
        with pe.Fori(1, NT // 2) as i:
            body(2 * i, 0, P, False)
            body(2 * i + 1, 1, P, False)
        body(NT, 0, DEC, False)

    def sp_load_qkv(sp, t, slot):
        for c in range(3):
            sp.dma_start(QKV[:, slot, H * c:H * c + H], scr["proj"][C_QKV + H * c:C_QKV + H * c + H, :, bass.ds(t * P, P)].rearrange("c p n -> p c n")).then_inc(s_in[slot], 16)

    def sp_load_gcum(sp, t, slot):
        sp.dma_start(GB[:, slot], scr["gcum"][bass.ds(t, 1)].rearrange("a h n -> a (h n)").to_broadcast([P, H * P])).then_inc(s_gb[slot], 16)

    def sp_load_za(sp, t, slot):
        sp.dma_start(za[:, slot], scr["proj"][C_ZA:C_ZA + H, :, bass.ds(t * P, P)].rearrange("c p n -> p c n")).then_inc(s_za[slot], 16)

    def sp_store_u(sp, t):
        for g in range(2):
            after(sp, s_dv["out"], DVE_OUT, g, t, "u")
            sp.dma_start(scr["u"][4 * g:4 * g + 4, :, bass.ds(t * P, P)].rearrange("c p n -> p c n"), heads(UA[:, g])).then_inc(s_ua, 16)

    def sp_delta(sp):
        sp_load_za(sp, 0, 0)
        sp_load_za(sp, 1, 1)
        sp.dma_start(S[:, 1], a["state_delta"][0, 0].rearrange("h k v -> k h v")).then_inc(s_st, 16)

        def body(t, slot, first):
            if not first:
                sp_store_u(sp, t - 1)
                if not (isinstance(t, int) and t == NT):
                    sp_load_za(sp, t + 1, 1 - slot)
            if isinstance(t, int) and t >= NT - 1:
                if t == NT - 1:
                    for g in range(2):
                        after(sp, s_dv["main"], DVE_MAIN, g, t, "s")
                    sp.dma_start(o["new_delta_prompt"][0, 0].rearrange("h k v -> k h v"), S[:, 0]).then_inc(s_so, 16)
                return
            for g in range(2):
                after(sp, s_pe["main"], PE_MAIN, g, t, "qs")
                after(sp, s_dv["prep"], DVE_PREP, g, t, "at")
            sp_load_qkv(sp, t + 2, slot)
            sp_load_gcum(sp, t + 2, slot)
        run_tiles(sp, body)
        for l in range(2):
            sp_w_o(sp, l)
        sp_store_u(sp, NT)
        sp.dma_start(o["new_delta_sample"][0, 0].rearrange("h k v -> k h v"), S[:, 1]).then_inc(s_so, 16)
        sp.wait_ge(s_so, 32)
        sp.wait_ge(s_ua, 32 * (NT + 1))

    def pe_prep(pe, t, slot, part, prev=True):
        q0 = {"q": 0, "k": H, "v": 2 * H}[part]
        for g in range(2):
            if part == "k":
                pe.wait_ge(s_in[slot], 48 * fills(t, slot))
                if prev:
                    after(pe, s_dv["main"], DVE_MAIN, g, t - 2, "z")
            else:
                after(pe, s_ac["prep"], ACT_PREP, g, t, "k" if part == "q" else "q")
            for h in range(4):
                last = pe.transpose(hs(bank(g, 2), h), QKV[:, slot, q0 + 4 * g + h], ident)
            last.then_inc(s_pe["prep"][g], 1)

    def fills(t, slot):
        return (t - slot) // 2 + 1

    def pe_products(pe, t, slot, prev=True):
        for part, b, r0 in (("kk", 3, H), ("qk", 1, 0)):
            for g in range(2):
                if prev:
                    after(pe, s_dv["main"], DVE_MAIN, g, t - 1, "s")
                    after(pe, s_ac["main"], ACT_MAIN, g, t - 1, "o1")
                for h in range(4):
                    last = pe.matmul(hs(bank(g, b), h), QKV[:, slot, H + 4 * g + h], QKV[:, slot, r0 + 4 * g + h], start=True, stop=True)
                last.then_inc(s_pe["prep"][g], 1)

    def pe_out(pe, t):
        for g in range(2):
            after(pe, s_dv["out"], DVE_OUT, g, t, "on")
            for h in range(4):
                last = pe.transpose(hs(bank(g, 2), h), hs(ON[:, g], h), ident)
            last.then_inc(s_pe["out"][g], 1)

    def pe_delta(pe):
        def four(g, b, lhs, rhs, count):
            for h in range(4):
                last = pe.matmul(hs(bank(g, b), h), lhs(h), rhs(h), start=True, stop=True)
            if count:
                last.then_inc(s_pe["main"][g], 1)

        for part in "kqv":
            pe_prep(pe, 0, 0, part, prev=False)
        pe_products(pe, 0, 0, prev=False)

        def body(t, slot, first):
            last = isinstance(t, int) and t == NT
            st = 1 if last else 0
            for g in range(2):
                after(pe, s_dv["prep"], DVE_PREP, g, t, "nl")
                for h in range(4):
                    x = pe.transpose(hs(bank(g, 0), h), hs(NL[:, g], h), ident)
                x.then_inc(s_pe["main"][g], 1)
            for g in range(2):
                after(pe, s_dv["main"], DVE_MAIN, g, t, "q0")
                for h in range(4):
                    x = pe.transpose(hs(bank(g, 3), h), hs(QL[:, g, 0], h), ident)
                x.then_inc(s_pe["main"][g], 1)
            if not last:
                pe_prep(pe, t + 1, 1 - slot, "k", prev=not first)
            for l in range(1, NL7):
                for g in range(2):
                    after(pe, s_ac["main"], ACT_MAIN, g, t, f"x{l - 1}")
                    Xl = QL[:, g, 0] if l == 1 else X[:, g]
                    four(g, 0, lambda h: hs(NL[:, g], h), lambda h: hs(Xl, h), True)
                for g in range(2):
                    after(pe, s_dv["main"], DVE_MAIN, g, t, f"q{l}")
                    if l == 1:
                        after(pe, s_dv["prep"], DVE_PREP, g, t, "at")
                    if l < NL7 - 1:
                        four(g, 1, lambda h: hs(XT[:, g], h), lambda h: hs(QL[:, g, l], h), False)
                    four(g, 3, lambda h: hs(QL[:, g, l], h), lambda h: hs(XT[:, g], h), True)
                if not last and 1 <= l <= 2:
                    pe_prep(pe, t + 1, 1 - slot, "qv"[l - 1], prev=not first)
            if not first:
                if not last:
                    for g in range(2):
                        after(pe, s_dv["prep"], DVE_PREP, g, t + 1, "vn")
                pe_out(pe, t - 1)
            if last:
                pe.wait_ge(s_st, 16)
            for name, b, r0 in (("ks", 0, H), ("qs", 1, 0)):
                for g in range(2):
                    if not first and not last:
                        after(pe, s_dv["main"], DVE_MAIN, g, t - 1, "s")
                    four(g, b, lambda h: QKV[:, slot, r0 + 4 * g + h], lambda h: S[:, st, 4 * g + h], True)
            for g in range(2):
                after(pe, s_dv["main"], DVE_MAIN, g, t, "r")
                after(pe, s_ac["main"], ACT_MAIN, g, t, f"x{NL7 - 1}")
                if not first:
                    after(pe, s_dv["out"], DVE_OUT, g, t - 1, "u")
                else:
                    after(pe, s_dv["prep"], DVE_PREP, g, t + 1, "vn")
                four(g, 2, lambda h: hs(XT[:, g], h), lambda h: hs(RR[:, g], h), True)
            for g in range(2):
                after(pe, s_dv["main"], DVE_MAIN, g, t, "zd")
                four(g, 3, lambda h: hs(Kt[:, g, slot], h), lambda h: hs(ZD[:, g], h), True)
            for g in range(2):
                after(pe, s_dv["main"], DVE_MAIN, g, t, "z")
                four(g, 0, lambda h: hs(AT[:, g], h), lambda h: hs(Z[:, g], h), True)
            if not last:
                pe_products(pe, t + 1, 1 - slot)
            else:
                pe_out(pe, t)
        run_tiles(pe, body)

    def act_prep(act, t, slot, parts):
        for g in range(2):
            for part in parts:
                if part == "e":
                    after(act, s_dv["prep"], DVE_PREP, g, t, "sub")
                    act.activation(E[:, g], E[:, g], ACT.Exp).then_inc(s_ac["prep"][g], 1)
                    continue
                after(act, s_pe["prep"], PE_PREP, g, t, part)
                if part == "k":
                    act.activation(Kt[:, g, slot], bank(g, 2), ACT.Copy)
                act.activation((sq if part == "k" else sq2)[:, g], bank(g, 2), ACT.Square).then_inc(s_ac["prep"][g], 1)

    def act_delta(act):
        act_prep(act, 0, 0, "kq")
        act_prep(act, 0, 0, "e")

        def body(t, slot, first):
            last = isinstance(t, int) and t == NT
            if not first:
                for g in range(2):
                    after(act, s_dv["main"], DVE_MAIN, g, t - 1, "o2")
                    if isinstance(t, int) and t == 1 or not isinstance(t, int) or t > 1:
                        act.activation(sqo[:, g], O2[:, g], ACT.Square).then_inc(s_ac["out"][g], 1)
            for l in range(NL7):
                for g in range(2):
                    after(act, s_pe["main"], PE_MAIN, g, t, f"x{l}")
                    if 0 < l < NL7 - 1:
                        act.activation(X[:, g], bank(g, 1), ACT.Copy)
                    act.activation(XT[:, g], bank(g, 3), ACT.Copy).then_inc(s_ac["main"][g], 1)
                if not last and l <= 2:
                    act_prep(act, t + 1, 1 - slot, "kqe"[l])
            for g in range(2):
                after(act, s_pe["main"], PE_MAIN, g, t, "qs")
                if not first:
                    after(act, s_dv["main"], DVE_MAIN, g, t - 1, "o2")
                for h in range(4):
                    x = act.activation(hs(O1[:, g], h), hs(bank(g, 1), h), ACT.Copy, scale=tv[:, slot, 1, 4 * g + h:4 * g + h + 1])
                x.then_inc(s_ac["main"][g], 1)
            if last:
                for g in range(2):
                    after(act, s_dv["main"], DVE_MAIN, g, t, "o2")
                    act.activation(sqo[:, g], O2[:, g], ACT.Square).then_inc(s_ac["out"][g], 1)
        run_tiles(act, body)

    def pool_delta(pool):
        pool.wait_ge(s_ge, 1)

        def prep(t, slot, first=False):
            if not first:
                for g in range(2):
                    after(pool, s_dv["prep"], DVE_PREP, g, t - 1, "at")
            pool.tensor_copy(tv[:, slot].rearrange("p (a v) h -> p a v h", a=1), tvs[:, bass.ds(t, 1)]).then_inc(s_tv, 1)
            for g in range(2):
                after(pool, s_ac["prep"], ACT_PREP, g, t, "e")
                for out, m in ((Em, K_INC), (Es, K_STR)):
                    x = pool.tensor_tensor(heads(out[:, g]), heads(E[:, g]), cst[:, m:m + P].unsqueeze(1).to_broadcast([P, 4, P]), ALU.mult)
                x.then_inc(s_em[g], 1)
        prep(0, 0, True)

        def body(t, slot, first):
            if not (isinstance(t, int) and t == NT):
                prep(t + 1, 1 - slot)
        run_tiles(pool, body)

    def dve_sub(dve, t, slot, first=False):
        dve.wait_ge(s_tv, t + 1)
        dve.wait_ge(s_gb[slot], 16 * fills(t, slot))
        for g in range(2):
            if not first:
                dve.wait_ge(s_em[g], t)
            for h in range(4):
                x = dve.tensor_scalar(hs(E[:, g], h), GB[:, slot, (4 * g + h) * P:(4 * g + h + 1) * P],
                                      tv[:, slot, 0, 4 * g + h:4 * g + h + 1], 0.0, ALU.subtract, ALU.min)
            x.then_inc(s_dv["prep"][g], 1)

    def dve_norm_a(dve, t):
        for g in range(2):
            after(dve, s_ac["prep"], ACT_PREP, g, t, "q")
            dve.tensor_reduce(dst[:, 0, g, 0], heads(sq[:, g]), AX.X, ALU.add)
            dve.tensor_reduce(dst[:, 0, g, 1], heads(sq2[:, g]), AX.X, ALU.add)
        dve.drain()
        dve.tensor_scalar(dst[:, 0], dst[:, 0], EPS, None, ALU.add)
        dve.drain()

    def dve_roots(dve):
        rsqrt(dve, RS[:, 1], RS[:, 2], RS[:, 0])

    def dve_norm_c(dve, t, slot):
        v = vec[:, slot]
        rk, rq, ss = dst[:, 1, :, 0], dst[:, 1, :, 1], dst[:, 0, :, 0]
        beta = tv[:, slot, 5].rearrange("p (g h) -> p g h", g=2)
        edl = tv[:, slot, 3].rearrange("p (g h) -> p g h", g=2)
        dve.tensor_tensor(v[:, 0], ss, rk, ALU.mult)
        dve.tensor_tensor(v[:, 1], rk, rk, ALU.mult)
        dve.tensor_scalar(v[:, 4], rq, 1.0, None, ALU.mult)
        dve.drain()
        dve.tensor_tensor(v[:, 1], v[:, 1], beta, ALU.mult)
        dve.drain()
        dve.tensor_scalar(v[:, 2], v[:, 1], -1.0, None, ALU.mult)
        dve.tensor_tensor(v[:, 3], v[:, 1], edl, ALU.mult)
        dve.drain()
        for g in range(2):
            after(dve, s_pe["prep"], PE_PREP, g, t, "v")
            dve.tensor_tensor(heads(Vn[:, g, slot]), heads(bank(g, 2)), wide(v[:, 0, g]), ALU.mult).then_inc(s_dv["prep"][g], 1)

    def dve_masked(dve, t, slot):
        for g in range(2):
            after(dve, s_pe["prep"], PE_PREP, g, t, "kk")
            dve.wait_ge(s_em[g], t + 1)
            for h in range(4):
                x = dve.scalar_tensor_tensor(hs(NL[:, g], h), hs(bank(g, 3), h), vec[:, slot, 2, g, h:h + 1], hs(Es[:, g], h), ALU.mult, ALU.mult)
            x.then_inc(s_dv["prep"][g], 1)
        for g in range(2):
            after(dve, s_pe["prep"], PE_PREP, g, t, "qk")
            dve.tensor_tensor(AT[:, g], bank(g, 1), Em[:, g], ALU.mult).then_inc(s_dv["prep"][g], 1)

    def dve_out_squares(dve, t, slot):
        for g in range(2):
            after(dve, s_ac["out"], ACT_OUT, g, t, "sq")
            dve.tensor_reduce(osum[:, 0, g], heads(sqo[:, g]), AX.X, ALU.add)
        rq = vec[:, slot, 4]
        dve.tensor_tensor(ost[:, :, :], rq, rq, ALU.mult)
        dve.drain()
        dve.tensor_tensor(osum[:, 0], osum[:, 0], ost[:, :, :], ALU.mult)
        dve.drain()
        dve.tensor_scalar(osum[:, 0], osum[:, 0], 1.0 / (HD * HD), EPS, ALU.mult, ALU.add)
        dve.drain()

    def dve_out(dve, t, slot, first=False):
        dve.scalar_tensor_tensor(ost[:, :, :], osum[:, 1], float(HD) ** -0.5, vec[:, slot, 4], ALU.mult, ALU.mult)
        dve.drain()
        for g in range(2):
            if not first:
                after(dve, s_pe["out"], PE_OUT, g, t - 1, "on")
            dve.tensor_tensor(heads(ON[:, g]), heads(O2[:, g]), wide(ost[:, g]), ALU.mult).then_inc(s_dv["out"][g], 1)

    def dve_u(dve, t, slot, first=False):
        dve.wait_ge(s_za[slot], 16 * fills(t, slot))
        if not first:
            dve.wait_ge(s_ua, 32 * t)
        for g in range(2):
            after(dve, s_pe["out"], PE_OUT, g, t, "on")
            dve.scalar_tensor_tensor(UA[:, g], bank(g, 2), colB[:, B_DN:B_DN + 1], za[:, slot, 4 * g:4 * g + 4].rearrange("p h n -> p (h n)"),
                                     ALU.mult, ALU.mult).then_inc(s_dv["out"][g], 1)

    def dve_delta(dve):
        dve.memset(S[:, 0], 0.0)
        for g in range(2):
            for l in range(NL7):
                dve.tensor_copy(heads(QL[:, g, l]), ident.unsqueeze(1).to_broadcast([P, 4, P]))
        dve_sub(dve, 0, 0, True)
        dve.memset(osum[:, 0], 1.0)
        dve_norm_a(dve, 0)
        dve_roots(dve)
        dve_norm_c(dve, 0, 0)
        dve_masked(dve, 0, 0)

        def body(t, slot, first):
            last = isinstance(t, int) and t == NT
            st = 1 if last else 0
            for l in range(NL7):
                for g in range(2):
                    after(dve, s_pe["main"], PE_MAIN, g, t, "l" if l == 0 else f"p{l}")
                    dve.sem_inc(s_seen, 1)
                    for h in range(4):
                        x = dve.copy_predicated(hs(QL[:, g, l], h), cst[:, K_LEV + l * P:K_LEV + (l + 1) * P].bitcast(I32), hs(bank(g, 0), h))
                    x.then_inc(s_dv["main"][g], 1)
                if l == 0 and not last:
                    dve_sub(dve, t + 1, 1 - slot)
                if l == 1 and not first:
                    dve_out_squares(dve, t - 1, 1 - slot)
                if l == 2 and not last:
                    dve_norm_a(dve, t + 1)
                if l == 3:
                    dve_roots(dve)
                if l == 4 and not first:
                    dve_out(dve, t - 1, 1 - slot, first=(isinstance(t, int) and t == 1))
                if l == 5 and not last:
                    dve_norm_c(dve, t + 1, 1 - slot)
            if not first:
                dve_u(dve, t - 1, 1 - slot, first=(isinstance(t, int) and t == 1))
            v = tv[:, slot]
            for g in range(2):
                after(dve, s_pe["main"], PE_MAIN, g, t, "ks")
                for h in range(4):
                    x = dve.scalar_tensor_tensor(hs(RR[:, g], h), hs(bank(g, 0), h), v[:, 2, 4 * g + h:4 * g + h + 1], hs(Vn[:, g, slot], h), ALU.mult, ALU.add)
                x.then_inc(s_dv["main"][g], 1)
            for g in range(2):
                after(dve, s_pe["main"], PE_MAIN, g, t, "y")
                dve.tensor_tensor(heads(ZD[:, g]), heads(bank(g, 2)), wide(vec[:, slot, 3, g]), ALU.mult).then_inc(s_dv["main"][g], 1)
                dve.tensor_tensor(heads(Z[:, g]), heads(bank(g, 2)), wide(vec[:, slot, 1, g]), ALU.mult).then_inc(s_dv["main"][g], 1)
            for g in range(2):
                after(dve, s_pe["main"], PE_MAIN, g, t, "st")
                for h in range(4):
                    x = dve.scalar_tensor_tensor(S[:, st, 4 * g + h], S[:, st, 4 * g + h], v[:, 4, 4 * g + h:4 * g + h + 1], hs(bank(g, 3), h), ALU.mult, ALU.add)
                x.then_inc(s_dv["main"][g], 1)
            for g in range(2):
                after(dve, s_pe["main"], PE_MAIN, g, t, "av")
                after(dve, s_ac["main"], ACT_MAIN, g, t, "o1")
                dve.tensor_tensor(O2[:, g], bank(g, 0), O1[:, g], ALU.add).then_inc(s_dv["main"][g], 1)
            if not last:
                dve_masked(dve, t + 1, 1 - slot)
            else:
                dve_out_squares(dve, t, slot)
                dve_roots(dve)
                dve_out(dve, t, slot)
                dve_u(dve, t, slot)
        run_tiles(dve, body)

    block = ctx.enter_context(nc.Block())

    def sp_pass01(sp):
        sp.dma_start(cst[:, :], a["shape_constants"]).then_inc(s_cst, 16)
        for l in range(12):
            slot = ada_slot(l)
            if l >= 4:
                sp.wait_ge(s_adam, ada_before(l) + 1)
            sp.dma_start(Wraw[:, slot], a["w_ada"][0, :, l * 256:(l + 1) * 256].rearrange("(k p) n -> p k n", p=P)).then_inc(s_ada[slot], 16)
        sp.sem_inc(s_store[0], 16)
        sp.sem_inc(s_store[1], 16)
        with sp.Fori(0, (NCHUNK - 1) // 2) as it:
            for c in range(2):
                sp.wait_ge(s_stage, 2 * it + c + 2)
                sp.dma_start(scr["proj"][bass.ds(2 * it + c, 1)].rearrange("a p n -> (a p) n"), stage[:, c]).then_inc(s_store[c], 16)
        sp_latents_early(sp)
        sp.wait_ge(s_stage, NCHUNK + 1)
        sp.dma_start(scr["proj"][C_MISC, 0:MISC], stage[0:MISC, 0]).then_inc(s_store[0], 16)
        sp.wait_ge(s_edc, 2)
        for i, name in enumerate(("new_conv_prompt", "new_conv_sample")):
            sp.dma_start(o[name][0, 0].rearrange("i (c p) -> (i c) p", p=P), edT[0:72, i]).then_inc(s_out, 16)
        sp.wait_ge(s_store[0], 16 * 38)
        sp.wait_ge(s_store[1], 16 * 37)

    @block.sync
    def _(sp):
        sp_pass01(sp)
        meet(sp, 1)
        sp_latents(sp)
        meet(sp, 2)
        sp_attention(sp)
        meet(sp, 3)
        sp_delta(sp)
        meet(sp, 4)
        sp_out(sp)
        sp_y(sp)
        sp.wait_ge(s_out, 16 * 2)

    def pool_pass01(pool):
        def load(l, s, col):
            pool.wait_ge(s_wlo, l + 1)
            pool.dma_start(Wraw[:, s], a["w_in"][0, :, bass.ds(col + 256 * s, 256)].rearrange("(k p) n -> p k n", p=P)).then_inc(s_raw[s], 16)

        pool.dma_start(rows[0:72, 1], a["state_conv"][0, 0].rearrange("i (c p) -> (i c) p", p=P)).then_inc(s_vecs, 16)
        pool.dma_start(rows[72:96, 1], a["b_ada"][0].rearrange("(c p) -> c p", p=P)).then_inc(s_vecs, 16)
        for i, name in enumerate(("dn_out_norm", "q_nope_norm", "k_nope_norm")):
            pool.dma_start(rows[96 + i:97 + i, 1], a[name]).then_inc(s_vecs, 16)
        pool.sem_inc(s_edge, 2)
        pool.wait_ge(s_colc, 2)
        pool.wait_ge(s_adam, 5)
        load(0, 0, 0)
        pool.wait_ge(s_adam, 6)
        load(1, 1, 0)
        pool.wait_ge(s_hl, NG)
        pool.memset(stage[:, 0, TOK:TPAD], 0.0)
        pool.memset(stage[:, 1, TOK:TPAD], 0.0)
        pool.memset(Xr[:, 0, 0:3], 0.0)
        pool.memset(Xr[:, 1, 0:3], 0.0)
        pool.drain().then_inc(s_pad, 1)
        taps = colA[:, A_CONV:A_CONV + 96].rearrange("p (i c) -> p i c", c=NCV)
        state = colB[:, B_STATE:B_STATE + 72].rearrange("p (i c) -> p i c", c=NCV)
        kept = edge.rearrange("p (s i c) -> p s i c", s=2, c=NCV)
        with pool.Fori(0, NCV // 4) as it:
            for c in range(4):
                n = 4 * it + c
                if c % 2 == 0:
                    load(2 * it + c // 2 + 2, c // 2, 512 * it + 512)
                pool.wait_ge(s_conv, n + 1)
                pool.tensor_copy(wcv[:, c % 2].rearrange("p (i a) -> p i a", a=1), taps[:, :, bass.ds(n, 1)])
                pool.tensor_copy(Xr[:, c % 2, 3 + SEQ:6 + SEQ].rearrange("p (i a) -> p i a", a=1), state[:, :, bass.ds(n, 1)])
                pool.drain().then_inc(s_pad, 1)
                pool.wait_ge(s_evac, n + 3)
                pool.tensor_copy(kept[:, 0, :, bass.ds(n, 1)], Xr[:, c % 2, SEQ:SEQ + 3].rearrange("p (i a) -> p i a", a=1))
                pool.tensor_copy(kept[:, 1, :, bass.ds(n, 1)], Xr[:, c % 2, XW - 3:XW].rearrange("p (i a) -> p i a", a=1))
                pool.drain().then_inc(s_edge, 1)
        done = NCV // 4 + 1
        for iters, col in ((1, CONV_CH + 512), (4, COL_Q), (6, COL_ZB)):
            with pool.Fori(0, iters) as it:
                for s in range(2):
                    load(2 * it + 2 * done + s, s, 512 * it + col)
            done += iters
        pool.wait_ge(s_wlo, 2 * done + 1)
        for c, lo, n, landed in ((0, COL_BA, BA, s_misc), (BA, COL_KR, ROPE, s_raw[0])):
            pool.dma_start(Wraw[:, 0, :, c:c + n], a["w_in"][0, :, lo:lo + n].rearrange("(k p) n -> p k n", p=P)).then_inc(landed, 16)
            pool.wait_ge(s_misc, 16)

    @block.gpsimd
    def _(pool):
        pool_pass01(pool)
        meet(pool, 1)
        meet(pool, 2)
        pool_attention(pool)
        meet(pool, 3)
        pool_delta(pool)
        meet(pool, 4)

    def act_pass01(act):
        act.dma_start(rows[104:112, 0], a["c_prompt"][0].rearrange("(c p) -> c p", p=P)).then_inc(s_rows, 16)
        act.dma_start(rows[112:120, 0], a["c_sample"][0].rearrange("(c p) -> c p", p=P)).then_inc(s_rows, 16)
        act.dma_start(rows[96:104, 0], a["norm_gain"][0].rearrange("(c p) -> c p", p=P)).then_inc(s_rows, 16)
        act.dma_start(rows[0:96, 0], a["w_conv"][0].rearrange("i (c p) -> (i c) p", p=P)).then_inc(s_rows, 16)
        act.wait_ge(s_cst, 16)
        for i in range(2):
            act.dma_start(R[:, 4 * i:4 * i + 4], a["x_prompt"][0, 512 * i:512 * i + 512].rearrange("(t p) n -> p t n", p=P)).then_inc(s_x[i], 16)
        act.dma_start(R[0:DEC, 8], a["x_sample"][0]).then_inc(s_x[2], 16)
        act.sem_inc(s_evac, 2)
        act.sem_inc(s_stage, 1)
        act.wait_ge(s_cols, 1)
        act.activation(colA[:, :], PS[:, 0, 0:120], ACT.Copy).then_inc(s_colc, 1)

        def rows_of_modulation(i):
            act.wait_ge(s_adam, 2 * i + 2)
            if i >= 2:
                act.wait_ge(s_modT, i - 1)
            act.activation(modr[:, i % 2], PS[0:2, i if i < 4 else i + 2], ACT.Copy).then_inc(s_modr, 1)
        act.wait_ge(s_xst, 1)
        rows_of_modulation(0)
        act.wait_ge(s_cols, 2)
        act.activation(colB[:, :], PS[:, 4, 0:99], ACT.Copy).then_inc(s_colc, 1)
        for t in range(9):
            if t in (3, 6):
                rows_of_modulation(t // 3)
            rows_t = P if t < 8 else DEC
            act.wait_ge(s_x[t // 4], 16)
            act.activation(hf[0:rows_t, 0:2].rearrange("p a b -> p (a b)"), R[0:rows_t, t], ACT.Square, accum_out=xst[0:rows_t, 0, t:t + 1]).then_inc(s_xss, 1)
            act.drain()
        rows_of_modulation(3)
        act.wait_ge(s_mod, 1)
        for n in range(NG):
            g, k, w = x_group(n)
            if n in (16, 20):
                rows_of_modulation(n // 4)
            act.wait_ge(s_xT, n + 1)
            if n >= NHF:
                act.wait_ge(s_hl, n - NHF + 1)
            act.activation(hf[:, n % NHF, 0:w], PS[:, n % 4, 0:w], ACT.Identity, scale=G[:, k, g // 2:g // 2 + 1],
                           bias=mod[:, k, g // 2:g // 2 + 1]).then_inc(s_hf, 1)

        def split_hi(s, l, fill):
            act.wait_ge(s_raw[s], fill)
            act.wait_ge(s_chunk, 2 * l + 2)
            act.activation(WH[:, s], Wraw[:, s], ACT.Copy).then_inc(s_whi, 1)

        split_hi(0, 0, 16)
        base = 0
        for iters, _, kind in SEGMENTS:
            with act.Fori(0, iters) as it:
                for c in range(4):
                    n = 4 * it + 4 * base + c
                    if c % 2 == 0:
                        split_hi(1 - c // 2, 2 * (it + base) + c // 2 + 1, 16 * (it + base + c // 2 + 1))
                    act.wait_ge(s_chunk, n + 1 + 4)
                    b3 = PS[:, 3 * (c % 2):3 * (c % 2) + 3, 0:TB]
                    st = stage[:, c % 2, 0:TOK]
                    if kind == "conv":
                        act.wait_ge(s_pad, n + 2)
                        act.wait_ge(s_edge, n + 1)
                        act.activation(Xr[:, c % 2, 3:3 + 2 * TB].rearrange("p (b n) -> p b n", b=2), b3[:, 0:2], ACT.Copy)
                        act.activation(Xr[:, c % 2, 3 + 2 * TB:3 + SEQ], PS[:, 3 * (c % 2) + 2, 0:SEQ - 2 * TB], ACT.Copy)
                        act.activation(Xr[:, c % 2, 6 + SEQ:XW], PS[:, 3 * (c % 2) + 2, SEQ - 2 * TB:TB], ACT.Copy).then_inc(s_evac, 1)
                        act.wait_ge(s_conv, n + 3)
                        act.wait_ge(s_store[c % 2], 16 * (2 * (it + base) + c // 2 + 1))
                        act.activation(stage[:, c % 2, 0:SEQ], cv[:, 0:SEQ], ACT.Silu)
                        act.activation(stage[:, c % 2, SEQ:TOK], cv[:, SEQ + 3:SEQ + 3 + DEC], ACT.Silu).then_inc(s_stage, 1)
                    else:
                        act.wait_ge(s_store[c % 2], 16 * (2 * (it + base) + c // 2 + 1))
                        f = {"silu": ACT.Silu, "copy": ACT.Copy, "sigmoid": ACT.Sigmoid}[kind]
                        act.activation(st.rearrange("p (b n) -> p b n", b=3), b3, f).then_inc(s_stage, 1)
                        act.drain().then_inc(s_evac, 1)
            base += iters
        act.wait_ge(s_chunk, 4 * base + 5)
        act.wait_ge(s_store[0], 16 * (2 * base + 1))
        act.activation(stage[0:MISC, 0, 0:TOK].rearrange("p (b n) -> p b n", b=3), PS[0:MISC, 0:3, 0:TB], ACT.Copy).then_inc(s_stage, 1)
        for i in range(2):
            act.wait_ge(s_edT, i + 1)
            act.activation(edT[0:72, i], PS[0:72, 6 + i, 0:P], ACT.Copy).then_inc(s_edc, 1)

    @block.scalar
    def _(act):
        act_pass01(act)
        meet(act, 1)
        act_latents(act)
        meet(act, 2)
        act_attention(act)
        meet(act, 3)
        act_delta(act)
        meet(act, 4)
        act_out(act)
        act_y(act)

    def pe_chunk(pe, s, c, psum, lo=0, m=P):
        for k in range(KD):
            for w, h, first in ((WL, HH, True), (WH, HL, False), (WH, HH, False)):
                for b in range(NB):
                    last = pe.matmul(PS[0:m, psum + b, 0:TB], w[:, s, k, c * P:c * P + m], h[:, k, b * TB:(b + 1) * TB],
                                     start=(k == 0 and first), stop=(k == KD - 1 and h is HH and not first))
        last.then_inc(s_chunk, 1)

    def pe_pass01(pe):
        pe.sem_inc(s_chunk, 4)
        pe.wait_ge(s_cst, 16)
        pe.wait_ge(s_rows, 16 * 4)
        pe.transpose(PS[:, 0, 0:120], rows[0:120, 0], ident[0:120, 0:120]).then_inc(s_cols, 1)
        pe.wait_ge(s_colc, 1)

        def modulation(l):
            pe.wait_ge(s_ada[ada_slot(l)], 16 * ada_fill(l))
            bank = l // 2 if l < 8 else l // 2 + 2
            for k in range(KD):
                last = pe.matmul(PS[0:2, bank, 256 * (l % 2):256 * (l % 2) + 256], colA[:, A_C + k:A_C + 16:8], Wraw[:, ada_slot(l), k],
                                 start=(k == 0), stop=(k == KD - 1))
            last.then_inc(s_adam, 1)

        def modulation_columns(i):
            pe.wait_ge(s_modr, i + 1)
            for j in range(4):
                last = pe.transpose(PS[:, 5, 8 * i + 2 * j:8 * i + 2 * j + 2], modr[:, i % 2, j * P:(j + 1) * P], ident[0:2, 0:2])
            last.then_inc(s_modT, 1)

        for l in range(8):
            modulation(l)
            if l == 1:
                pe.wait_ge(s_vecs, 16 * 5)
                pe.transpose(PS[:, 4, 0:99], rows[0:99, 1], ident[0:99, 0:99]).then_inc(s_cols, 1)
            if l and l % 2 == 0:
                modulation_columns(l // 2 - 1)
        modulation_columns(3)
        for n in range(NG):
            g, k, w = x_group(n)
            if k == 0:
                pe.wait_ge(s_xn, min(4 * g + 4, 9))
            if n >= 4:
                pe.wait_ge(s_hf, n - 3)
            for t in range(4 if g < 2 else 1):
                r = P if g < 2 else DEC
                last = pe.transpose(PS[:, n % 4, t * P:t * P + r], R[0:r, 4 * g + t, k * P:(k + 1) * P], ident[0:r, 0:r])
            last.then_inc(s_xT, 1)
            if n in (5, 9, 13, 17):
                modulation(8 + (n - 5) // 4)
        for i in (4, 5):
            modulation_columns(i)
        pe.wait_ge(s_hl, NG)
        pe.wait_ge(s_mod, 2)
        with pe.Fori(0, 18) as it:
            for c in range(4):
                if c % 2 == 0:
                    pe.wait_ge(s_wlo, 2 * it + c // 2 + 3)
                pe.wait_ge(s_evac, 4 * it + c + 1)
                pe_chunk(pe, c // 2, c % 2, 3 * (c % 2))
        pe.wait_ge(s_wlo, 39)
        pe.wait_ge(s_evac, 73)
        pe_chunk(pe, 0, 0, 0, m=MISC)
        pe.wait_ge(s_edge, NCV + 2)
        for i in range(2):
            pe.transpose(PS[0:72, 6 + i, 0:P], edge[:, 72 * i:72 * i + 72], ident).then_inc(s_edT, 1)

    @block.tensor
    def _(pe):
        pe_pass01(pe)
        meet(pe, 1)
        pe_latents(pe)
        meet(pe, 2)
        pe_attention(pe)
        meet(pe, 3)
        pe_delta(pe)
        meet(pe, 4)
        pe_branches(pe)
        pe_y(pe)

    def dve_pass01(dve):
        dve.memset(xst[:, :, :], 1.0).then_inc(s_xst, 1)
        dve.sem_inc(s_wlo, 2)
        dve.sem_inc(s_conv, 2)
        dve.wait_ge(s_colc, 2)
        dve.wait_ge(s_xss, 9)
        ss, r, tmp = xst[:, 0], xst[:, 1], xst[:, 2]
        dve.tensor_scalar(ss, ss, 1.0 / D, EPS, ALU.mult, ALU.add)
        dve.drain()
        rsqrt(dve, r, tmp, ss)
        for t in range(9):
            n = P if t < 8 else DEC
            dve.tensor_scalar(R[0:n, t], R[0:n, t], r[0:n, t:t + 1], None, ALU.mult).then_inc(s_xn, 1)
        dve.wait_ge(s_modT, 4)
        dve.tensor_tensor(mod[:, 0:16], PS[:, 5, 0:32].rearrange("p (j s) -> p j s", s=2),
                          colB[:, B_ADA:B_ADA + 16].unsqueeze(2).to_broadcast([P, 16, 2]), ALU.add)
        dve.drain()
        dve.scalar_tensor_tensor(G[:, :, :], mod[:, 8:16, :], 1.0,
                                 colA[:, A_GAIN:A_GAIN + 8].unsqueeze(2).to_broadcast([P, 8, 2]), ALU.add, ALU.mult).then_inc(s_mod, 1)
        for n in range(NG):
            g, k, w = x_group(n)
            cols = slice(512 * g, 512 * g + w)
            dve.wait_ge(s_hf, n + 1)
            dve.tensor_copy(HH[:, k, cols], hf[:, n % NHF, 0:w])
            dve.drain()
            dve.tensor_tensor(HL[:, k, cols], hf[:, n % NHF, 0:w], HH[:, k, cols].bitcast(F32), ALU.subtract).then_inc(s_hl, 1)

        def split_lo(s, l):
            dve.wait_ge(s_whi, l + 1)
            dve.tensor_tensor(WL[:, s], Wraw[:, s], WH[:, s].bitcast(F32), ALU.subtract).then_inc(s_wlo, 1)

        split_lo(0, 0)
        dve.wait_ge(s_modT, 6)
        dve.tensor_tensor(mod[:, 16:24], PS[:, 5, 32:48].rearrange("p (j s) -> p j s", s=2),
                          colB[:, B_ADA + 16:B_ADA + 24].unsqueeze(2).to_broadcast([P, 8, 2]), ALU.add).then_inc(s_mod, 1)
        base = 0
        for iters, _, kind in SEGMENTS:
            with dve.Fori(0, iters) as it:
                for c in range(4):
                    n = 4 * it + 4 * base + c
                    if c % 2 == 0:
                        split_lo(1 - c // 2, 2 * (it + base) + c // 2 + 1)
                    if kind == "conv":
                        x = Xr[:, c % 2]
                        wt = wcv[:, c % 2]
                        dve.wait_ge(s_evac, n + 3)
                        dve.wait_ge(s_stage, n + 1)
                        dve.tensor_scalar(cv, x[:, 0:XW - 3], wt[:, 0:1], None, ALU.mult)
                        dve.drain()
                        for i in range(1, CONV):
                            last = dve.scalar_tensor_tensor(cv, x[:, i:i + XW - 3], wt[:, i:i + 1], cv, ALU.mult, ALU.add)
                            if i < CONV - 1:
                                dve.drain()
                        last.then_inc(s_conv, 1)
            base += iters

    @block.vector
    def _(dve):
        dve_pass01(dve)
        meet(dve, 1)
        dve_latents(dve)
        meet(dve, 2)
        dve_attention(dve)
        meet(dve, 3)
        dve_delta(dve)
        meet(dve, 4)
        dve_branches(dve)
        dve_y(dve)


INPUTS = ["x_prompt", "x_sample", "c_prompt", "c_sample", "cache_ckv", "cache_krope", "state_delta", "state_conv",
          "norm_gain", "w_ada", "b_ada", "w_in", "w_conv", "a_log", "dt_bias", "dn_out_norm", "q_nope_norm",
          "q_rope_norm", "k_nope_norm", "k_rope_norm", "kv_norm", "w_uk", "w_uv", "w_o_dn", "w_o_mla", "w_out"]
OUTPUTS = [("y_prompt", (1, SEQ, D)), ("y_sample", (1, DEC, D)),
           ("new_ckv_prompt", (1, 1, SEQ, KV)), ("new_krope_prompt", (1, 1, SEQ, ROPE)),
           ("new_delta_prompt", (1, 1, H, HD, HD)), ("new_conv_prompt", (1, 1, CONV - 1, CONV_CH)),
           ("new_ckv_sample", (1, 1, DEC, KV)), ("new_krope_sample", (1, 1, DEC, ROPE)),
           ("new_delta_sample", (1, 1, H, HD, HD)), ("new_conv_sample", (1, 1, CONV - 1, CONV_CH))]


def kernel(**inputs):
    from concourse import bacc
    from concourse.bass_utils import run_bass_kernel_spmd

    nc = bacc.Bacc("TRN2", target_bir_lowering=False, num_devices=1)
    arrays = {name: np.ascontiguousarray(inputs[name]) for name in INPUTS}
    arrays["shape_constants"] = shape_constants()
    arrays["rotary_tables"] = rotary_tables()
    a = {n: nc.dram_tensor(f"in_{n}", v.shape, F32, kind="ExternalInput").ap() for n, v in arrays.items()}
    o = {n: nc.dram_tensor(f"out_{n}", shape, F32, kind="ExternalOutput").ap() for n, shape in OUTPUTS}
    kind = "Internal"
    scr = {n: nc.dram_tensor(f"scratch_{n}", shape, F32, kind=kind).ap()
           for n, shape in (("proj", (NCHUNK, P, TPAD)), ("u", (2 * H, P, TPAD)), ("gcum", (NT + 1, H, P)))}
    with ExitStack() as ctx:
        build(nc, a, o, scr, ctx)
    r = run_bass_kernel_spmd(nc, [{f"in_{n}": v for n, v in arrays.items()}], core_ids=[0])
    return tuple(r.results[0][f"out_{n}"] for n, _ in OUTPUTS)
```
